# Optimizing a Trainium2 kernel written in Bass

```python
import jax, jax.numpy as jnp
from jax import lax
import numpy as np

D_MODEL = 1024
BATCH = 1
SEQ = 512
DEPTH = 1
DEC_BATCH = 8
DEC_SEQ = 1
PAST_LEN = 2048
PAGE_SIZE = 128

N_HEADS = 8
HEAD_DIM = 128
N_KV_HEADS = 2
Q_GROUP = N_HEADS // N_KV_HEADS
ATTN_WIDTH = N_HEADS * HEAD_DIM
IDX_HEADS = 16
IDX_DIM = 64
TOPK_MAX = 256
Q_BLOCK = 128
D_INNER = 2 * D_MODEL
SSM_HEAD_DIM = 64
SSM_HEADS = D_INNER // SSM_HEAD_DIM
SSM_GROUPS = 8
HEADS_PER_GROUP = SSM_HEADS // SSM_GROUPS
D_STATE = 128
CONV_W = 4
CONV_DIM = D_INNER + 2 * SSM_GROUPS * D_STATE
CHUNK = 128
D_FF = -(-(-(-8 * D_MODEL // 3)) // 256) * 256
EPS = 1e-6

SPLIT_SIZES = (ATTN_WIDTH, N_KV_HEADS * HEAD_DIM, N_KV_HEADS * HEAD_DIM,
               IDX_HEADS * IDX_DIM, IDX_DIM, IDX_HEADS,
               D_INNER, CONV_DIM, SSM_HEADS, D_MODEL, D_MODEL)
D_IN_PROJ = (ATTN_WIDTH + 2 * N_KV_HEADS * HEAD_DIM + IDX_HEADS * IDX_DIM + IDX_DIM + IDX_HEADS
             + D_INNER + CONV_DIM + SSM_HEADS + 2 * D_MODEL)

kernel_name = "hybrid_dsa_ssd_gated_decoder_step"

F32 = jnp.float32

def rmsnorm(x, w):
    xf = x.astype(F32)
    y = xf * lax.rsqrt(jnp.mean(xf * xf, axis=-1, keepdims=True) + EPS)
    return (y * w.astype(F32)).astype(x.dtype)

def layernorm(x, w, b):
    xf = x.astype(F32)
    mu = jnp.mean(xf, axis=-1, keepdims=True)
    var = jnp.mean(jnp.square(xf - mu), axis=-1, keepdims=True)
    y = (xf - mu) * lax.rsqrt(var + EPS)
    return (y * w.astype(F32) + b.astype(F32)).astype(x.dtype)

def topk_count(n_keys):
    return min(TOPK_MAX, n_keys // 4)

def in_projection(x, norm1_w, w_in, idx_ln_w, idx_ln_b):
    b, t = x.shape[:2]
    u = rmsnorm(x, norm1_w) @ w_in
    offsets = [int(o) for o in np.cumsum(SPLIT_SIZES)[:-1]]
    q, k, v, iq, ik, iw, z, xbc, dt, ga, gm = jnp.split(u, offsets, axis=-1)
    q = q.reshape(b, t, N_HEADS, HEAD_DIM)
    k = k.reshape(b, t, N_KV_HEADS, HEAD_DIM)
    v = v.reshape(b, t, N_KV_HEADS, HEAD_DIM)
    iq = iq.reshape(b, t, IDX_HEADS, IDX_DIM)
    ik = layernorm(ik, idx_ln_w, idx_ln_b)
    iw = iw * (IDX_HEADS ** -0.5)
    return q, k, v, iq, ik, iw, z, xbc, dt, ga, gm

def index_scores(iq, iw, ik):
    s = jax.nn.relu(jnp.einsum('bthd,bsd->bths', iq.astype(F32), ik.astype(F32))) * (IDX_DIM ** -0.5)
    return jnp.einsum('bths,bth->bts', s, iw.astype(F32))

def select_keys(scores, q_pos, n_sel):
    key_pos = jnp.arange(scores.shape[-1])
    admissible = key_pos[None, None, :] <= q_pos[None, :, None]
    _, idx = lax.top_k(jnp.where(admissible, scores, -jnp.inf), n_sel)
    valid = idx <= q_pos[None, :, None]
    return idx, valid

def attend_selected(q, k_sel, v_sel, valid):
    b, t = q.shape[:2]
    qg = q.reshape(b, t, N_KV_HEADS, Q_GROUP, HEAD_DIM).astype(F32)
    logits = jnp.einsum('btkgd,btjkd->btkgj', qg, k_sel.astype(F32)) * (HEAD_DIM ** -0.5)
    logits = jnp.where(valid[:, :, None, None, :], logits, -jnp.inf)
    p = jax.nn.softmax(logits, axis=-1)
    o = jnp.einsum('btkgj,btjkd->btkgd', p, v_sel.astype(F32))
    return o.reshape(b, t, ATTN_WIDTH).astype(q.dtype)

def prompt_sparse_attention(q, k, v, iq, iw, ik):
    b, s = q.shape[:2]
    n_blk = s // Q_BLOCK
    n_sel = topk_count(s)
    bidx = jnp.arange(b)[:, None, None]

    def to_blocks(a):
        return a.reshape(b, n_blk, Q_BLOCK, *a.shape[2:]).swapaxes(0, 1)

    def block(args):
        blk, qb, iqb, iwb = args
        q_pos = blk * Q_BLOCK + jnp.arange(Q_BLOCK)
        idx, valid = select_keys(index_scores(iqb, iwb, ik), q_pos, n_sel)
        return attend_selected(qb, k[bidx, idx], v[bidx, idx], valid)

    out = lax.map(block, (jnp.arange(n_blk), to_blocks(q), to_blocks(iq), to_blocks(iw)))
    return out.swapaxes(0, 1).reshape(b, s, ATTN_WIDTH)

def sample_sparse_attention(q, k_new, v_new, iq, iw, ik_new, cache_k, cache_v, cache_idx_k, page_table):
    db, ds = q.shape[:2]
    past = page_table.shape[1] * PAGE_SIZE
    ik_past = cache_idx_k[page_table].reshape(db, past, IDX_DIM).astype(ik_new.dtype)
    ik_all = jnp.concatenate([ik_past, ik_new], axis=1)
    q_pos = past + jnp.arange(ds)
    idx, valid = select_keys(index_scores(iq, iw, ik_all), q_pos, topk_count(past + ds))
    bidx = jnp.arange(db)[:, None, None]
    in_past = (idx < past)[..., None, None]
    pidx = jnp.minimum(idx, past - 1)
    phys = page_table[bidx, pidx // PAGE_SIZE]
    off = pidx % PAGE_SIZE
    nidx = jnp.clip(idx - past, 0, ds - 1)
    k_sel = jnp.where(in_past, cache_k[phys, off].astype(k_new.dtype), k_new[bidx, nidx])
    v_sel = jnp.where(in_past, cache_v[phys, off].astype(v_new.dtype), v_new[bidx, nidx])
    return attend_selected(q, k_sel, v_sel, valid)

def causal_conv(xpad, conv_w, conv_b):
    t = xpad.shape[1] - (CONV_W - 1)
    out = conv_b
    for i in range(CONV_W):
        out = out + xpad[:, i:i + t] * conv_w[i]
    return jax.nn.silu(out)

def ssd_chunked(xs, Bm, Cm, dt, A):
    b, t = xs.shape[:2]
    nc = t // CHUNK
    c = lambda a: a.reshape(b, nc, CHUNK, *a.shape[2:])
    x_c, B_c, C_c, dt_c = c(xs), c(Bm), c(Cm), c(dt)
    xdt = x_c * dt_c[..., None]
    a_cum = jnp.cumsum(dt_c * A, axis=2)
    seg = a_cum[:, :, :, None] - a_cum[:, :, None, :]
    tri = jnp.arange(CHUNK)[:, None] >= jnp.arange(CHUNK)[None, :]
    L = jnp.exp(jnp.where(tri[:, :, None, None], seg, -jnp.inf))
    CB = jnp.einsum('bclgn,bcsgn->bclsg', C_c, B_c)
    y_diag = jnp.einsum('bclsg,bclsgr,bcsgrp->bclgrp', CB, L, xdt)

    def chunk_step(h, inp):
        Bk, Ck, xk, ak = inp
        y_off = jnp.einsum('blgn,bgrpn,blgr->blgrp', Ck, h, jnp.exp(ak))
        h_new = (h * jnp.exp(ak[:, -1])[..., None, None]
                 + jnp.einsum('blgn,blgr,blgrp->bgrpn', Bk, jnp.exp(ak[:, -1:] - ak), xk))
        return h_new, y_off

    h0 = jnp.zeros((b, SSM_GROUPS, HEADS_PER_GROUP, SSM_HEAD_DIM, D_STATE), F32)
    sw = lambda a: a.swapaxes(0, 1)
    h_fin, y_off = lax.scan(chunk_step, h0, (sw(B_c), sw(C_c), sw(xdt), sw(a_cum)))
    y = (y_diag + sw(y_off)).reshape(b, t, SSM_GROUPS, HEADS_PER_GROUP, SSM_HEAD_DIM)
    return y, h_fin

def ssd_recurrent(xs, Bm, Cm, dt, A, h0):
    def step(h, inp):
        xt, Bt, Ct, dtt = inp
        h = h * jnp.exp(dtt * A)[..., None, None] + jnp.einsum('bgrp,bgn,bgr->bgrpn', xt, Bt, dtt)
        return h, jnp.einsum('bgrpn,bgn->bgrp', h, Ct)

    sw = lambda a: a.swapaxes(0, 1)
    h, ys = lax.scan(step, h0, (sw(xs), sw(Bm), sw(Cm), sw(dt)))
    return sw(ys), h

def ssd_branch(z, xbc_pad, dt_raw, h0, conv_w, conv_b, dt_bias, a_log, d_skip, ssm_norm_w):
    b, t = z.shape[:2]
    xbc = causal_conv(xbc_pad, conv_w, conv_b).astype(F32)
    xs, Bm, Cm = jnp.split(xbc, [D_INNER, D_INNER + SSM_GROUPS * D_STATE], axis=-1)
    xs = xs.reshape(b, t, SSM_GROUPS, HEADS_PER_GROUP, SSM_HEAD_DIM)
    Bm = Bm.reshape(b, t, SSM_GROUPS, D_STATE)
    Cm = Cm.reshape(b, t, SSM_GROUPS, D_STATE)
    dt = jax.nn.softplus(dt_raw.astype(F32) + dt_bias.astype(F32)).reshape(b, t, SSM_GROUPS, HEADS_PER_GROUP)
    A = -jnp.exp(a_log.astype(F32)).reshape(SSM_GROUPS, HEADS_PER_GROUP)
    if h0 is None:
        y, h = ssd_chunked(xs, Bm, Cm, dt, A)
    else:
        h_in = h0.astype(F32).reshape(b, SSM_GROUPS, HEADS_PER_GROUP, SSM_HEAD_DIM, D_STATE)
        y, h = ssd_recurrent(xs, Bm, Cm, dt, A, h_in)
    y = y + d_skip.astype(F32).reshape(SSM_GROUPS, HEADS_PER_GROUP)[..., None] * xs
    y = y.reshape(b, t, D_INNER) * jax.nn.silu(z.astype(F32))
    yg = y.reshape(b, t, SSM_GROUPS, D_INNER // SSM_GROUPS)
    yg = yg * lax.rsqrt(jnp.mean(yg * yg, axis=-1, keepdims=True) + EPS)
    y = yg.reshape(b, t, D_INNER) * ssm_norm_w.astype(F32)
    return y.astype(z.dtype), h.reshape(b, SSM_HEADS, SSM_HEAD_DIM, D_STATE).astype(z.dtype)

def merge_and_ffn(x, attn_o, ssm_o, ga, gm, w_attn_br, w_ssm_br, w_out, norm2_w, w_ffn_gate, w_ffn_up, w_ffn_down):
    mix = jax.nn.sigmoid(ga) * (attn_o @ w_attn_br) + jax.nn.sigmoid(gm) * (ssm_o @ w_ssm_br)
    x = x + mix @ w_out
    h = rmsnorm(x, norm2_w)
    return x + (jax.nn.silu(h @ w_ffn_gate) * (h @ w_ffn_up)) @ w_ffn_down

def setup_inputs(seed: int = 0) -> dict:
    key = jax.random.key(seed)
    ks = jax.random.split(key, 32)
    n_pages = PAST_LEN // PAGE_SIZE
    n_used = DEC_BATCH * n_pages
    n_phys = n_used + -(-n_used // 4)
    nrm = lambda k, shape, scale=1.0: jax.random.normal(k, shape, F32) * scale
    page_table = jax.random.permutation(ks[0], n_phys)[:n_used].reshape(DEC_BATCH, n_pages).astype(jnp.int32)
    dt0 = jnp.exp(jax.random.uniform(ks[1], (DEPTH, SSM_HEADS), F32, np.log(1e-3), np.log(1e-1)))
    return {
        "x_prompt": nrm(ks[2], (BATCH, SEQ, D_MODEL)),
        "x_sample": nrm(ks[3], (DEC_BATCH, DEC_SEQ, D_MODEL)),
        "cache_k": nrm(ks[4], (DEPTH, n_phys, PAGE_SIZE, N_KV_HEADS, HEAD_DIM)),
        "cache_v": nrm(ks[5], (DEPTH, n_phys, PAGE_SIZE, N_KV_HEADS, HEAD_DIM)),
        "cache_idx_k": nrm(ks[6], (DEPTH, n_phys, PAGE_SIZE, IDX_DIM)),
        "state_ssm": nrm(ks[7], (DEPTH, DEC_BATCH, SSM_HEADS, SSM_HEAD_DIM, D_STATE), 0.5),
        "state_conv": nrm(ks[8], (DEPTH, DEC_BATCH, CONV_W - 1, CONV_DIM)),
        "page_table": page_table,
        "norm1_w": 1.0 + nrm(ks[9], (DEPTH, D_MODEL), 0.05),
        "w_in": nrm(ks[10], (DEPTH, D_MODEL, D_IN_PROJ), D_MODEL ** -0.5),
        "idx_ln_w": 1.0 + nrm(ks[11], (DEPTH, IDX_DIM), 0.05),
        "idx_ln_b": nrm(ks[12], (DEPTH, IDX_DIM), 0.02),
        "conv_w": nrm(ks[13], (DEPTH, CONV_W, CONV_DIM), CONV_W ** -0.5),
        "conv_b": nrm(ks[14], (DEPTH, CONV_DIM), 0.02),
        "dt_bias": dt0 + jnp.log(-jnp.expm1(-dt0)),
        "a_log": jnp.log(jax.random.uniform(ks[15], (DEPTH, SSM_HEADS), F32, 1.0, 16.0)),
        "d_skip": 1.0 + nrm(ks[16], (DEPTH, SSM_HEADS), 0.1),
        "ssm_norm_w": 1.0 + nrm(ks[17], (DEPTH, D_INNER), 0.05),
        "w_attn_br": nrm(ks[18], (DEPTH, ATTN_WIDTH, D_MODEL), ATTN_WIDTH ** -0.5),
        "w_ssm_br": nrm(ks[19], (DEPTH, D_INNER, D_MODEL), D_INNER ** -0.5),
        "w_out": nrm(ks[20], (DEPTH, D_MODEL, D_MODEL), D_MODEL ** -0.5),
        "norm2_w": 1.0 + nrm(ks[21], (DEPTH, D_MODEL), 0.05),
        "w_ffn_gate": nrm(ks[22], (DEPTH, D_MODEL, D_FF), D_MODEL ** -0.5),
        "w_ffn_up": nrm(ks[23], (DEPTH, D_MODEL, D_FF), D_MODEL ** -0.5),
        "w_ffn_down": nrm(ks[24], (DEPTH, D_FF, D_MODEL), D_FF ** -0.5),
        "normf_w": 1.0 + nrm(ks[25], (D_MODEL,), 0.05),
    }

def reference(x_prompt, x_sample, cache_k, cache_v, cache_idx_k, state_ssm, state_conv, page_table,
              norm1_w, w_in, idx_ln_w, idx_ln_b, conv_w, conv_b, dt_bias, a_log, d_skip, ssm_norm_w,
              w_attn_br, w_ssm_br, w_out, norm2_w, w_ffn_gate, w_ffn_up, w_ffn_down, normf_w):
    xp, xs = x_prompt, x_sample
    kp_l, vp_l, ikp_l, hp_l, cp_l = [], [], [], [], []
    ks_l, vs_l, iks_l, hs_l, cs_l = [], [], [], [], []
    for l in range(DEPTH):
        ssm_w = (conv_w[l], conv_b[l], dt_bias[l], a_log[l], d_skip[l], ssm_norm_w[l])
        tail_w = (w_attn_br[l], w_ssm_br[l], w_out[l], norm2_w[l], w_ffn_gate[l], w_ffn_up[l], w_ffn_down[l])
        q, k, v, iq, ik, iw, z, xbc, dt, ga, gm = in_projection(xp, norm1_w[l], w_in[l], idx_ln_w[l], idx_ln_b[l])
        a_o = prompt_sparse_attention(q, k, v, iq, iw, ik)
        xbc_pad = jnp.pad(xbc, ((0, 0), (CONV_W - 1, 0), (0, 0)))
        m_o, h_fin = ssd_branch(z, xbc_pad, dt, None, *ssm_w)
        xp = merge_and_ffn(xp, a_o, m_o, ga, gm, *tail_w)
        kp_l.append(k); vp_l.append(v); ikp_l.append(ik); hp_l.append(h_fin)
        cp_l.append(xbc[:, -(CONV_W - 1):])
        q, k, v, iq, ik, iw, z, xbc, dt, ga, gm = in_projection(xs, norm1_w[l], w_in[l], idx_ln_w[l], idx_ln_b[l])
        a_o = sample_sparse_attention(q, k, v, iq, iw, ik, cache_k[l], cache_v[l], cache_idx_k[l], page_table)
        xbc_pad = jnp.concatenate([state_conv[l].astype(xbc.dtype), xbc], axis=1)
        m_o, h_new = ssd_branch(z, xbc_pad, dt, state_ssm[l], *ssm_w)
        xs = merge_and_ffn(xs, a_o, m_o, ga, gm, *tail_w)
        ks_l.append(k); vs_l.append(v); iks_l.append(ik); hs_l.append(h_new)
        cs_l.append(xbc_pad[:, -(CONV_W - 1):])
    y_prompt = rmsnorm(xp, normf_w)
    y_sample = rmsnorm(xs, normf_w)
    return (y_prompt, y_sample,
            jnp.stack(kp_l), jnp.stack(vp_l), jnp.stack(ikp_l), jnp.stack(hp_l), jnp.stack(cp_l),
            jnp.stack(ks_l), jnp.stack(vs_l), jnp.stack(iks_l), jnp.stack(hs_l), jnp.stack(cs_l))


_drawn_inputs = setup_inputs


def setup_inputs(seed=0):
    import zlib

    import numpy as np

    out = dict(_drawn_inputs(seed))
    spreads = {}
    factors = {'idx_ln_b': 3.094}
    for name, (base, spread) in spreads.items():
        noise = np.random.default_rng([zlib.crc32(name.encode()), seed]).standard_normal(out[name].shape)
        drawn = base * np.exp(spread * noise) if base else spread * noise
        out[name] = __import__('jax').numpy.asarray(drawn.astype(out[name].dtype))
    for name, factor in factors.items():
        out[name] = (out[name] * factor).astype(out[name].dtype)
    return out
```

```python
from contextlib import ExitStack

import concourse.bass as bass
from concourse import mybir
from concourse.alu_op_type import AluOpType as ALU

ACT = mybir.ActivationFunctionType
AX = mybir.AxisListType
F32 = mybir.dt.float32
I32 = mybir.dt.int32
U32 = mybir.dt.uint32

P = 128
D = 1024
SEQ = 512
NB = 8
T = SEQ + NB
TH = T // 2
KT = D // P
NH = 8
GRP = 4
IH = 16
ID = 64
PAST = 2048
PAGE = 128
NPG = PAST // PAGE
NG = 8
NS = 128
DI = 2048
CONV = 4096
DFF = 2816
FT = DFF // P
TOPK = 256
TOPK_P = 128
EPS = 1e-6
LOW = -3.0e38
MASK = -1.0e30
OPEN = 1
C_IQ, C_IK, C_IW = 1536, 2560, 2624
C_Z, C_X, C_B, C_C = 2640, 4688, 6736, 7760
C_DT, C_GA, C_GM = 8784, 8816, 9840
SLOT = KT * 2 * P
NSLOT = 6
SCALE = P ** -0.5

K_ID, K_ONE, K_BLK, K_TRI, K_CB, K_P16, K_PG, K_HALF, K_PAR, K_J = 0, 128, 256, 384, 512, 640, 641, 897, 1025, 1027
NK = 1043
GSEL = 768


class Chain:

    def __init__(self, engine, sem, base=0):
        self.engine, self.sem, self.base, self.n = engine, sem, base, 0

    def __call__(self, ins):
        self.n += 1
        ins.then_inc(self.sem, 1)
        self.engine.wait_ge(self.sem, self.base + self.n)


def build(nc, x_prompt, x_sample, cache_k, cache_v, cache_idx_k, state_ssm, state_conv, page_table,
          norm1_w, w_in, idx_ln_w, idx_ln_b, conv_w, conv_b, dt_bias, a_log, d_skip, ssm_norm_w,
          w_attn_br, w_ssm_br, w_out, norm2_w, w_ffn_gate, w_ffn_up, w_ffn_down, normf_w,
          consts, gsel_d,
          y_prompt, y_sample, k_prompt, v_prompt, ik_prompt, ssm_prompt, conv_prompt,
          k_sample, v_sample, ik_sample, ssm_sample, conv_sample):
    with ExitStack() as ctx:
        def sb(name, shape, dt=F32):
            return ctx.enter_context(nc.sbuf_tensor(name, shape, dt))

        sems = {}

        def S(name):
            if name not in sems:
                sems[name] = ctx.enter_context(nc.semaphore(name))
            return sems[name]

        xT = sb("xT", [P, KT, T])
        xn = sb("xn", [P, KT, T])
        uT = sb("uT", [P, 8, T])
        work = sb("work", [P, 16384])
        ssm_o = sb("ssm_o", [P, 16, T])
        ring = sb("ring", [P, NSLOT, KT, 2 * P])
        cst = sb("cst", [P, NK])
        gs = sb("gs", [32, GSEL])
        vec = sb("vec", [P, 96])
        cwg = sb("cwg", [P, NG, 24])
        eps = sb("eps", [P, 1])
        ps = ctx.enter_context(nc.psum_tensor("ps", [P, 8, 512], F32))
        ident, ones = cst[:, K_ID:K_ID + P], cst[:, K_ONE:K_ONE + P]
        blk64, tri, cbias = cst[:, K_BLK:K_BLK + P], cst[:, K_TRI:K_TRI + P], cst[:, K_CB:K_CB + P]

        def W(off, *shape):
            n = 1
            for s in shape:
                n *= s
            v = work[:, off:off + n]
            if len(shape) == 2:
                v = v.rearrange("p (a b) -> p a b", b=shape[1])
            if len(shape) == 3:
                v = v.rearrange("p (a b c) -> p a b c", b=shape[1], c=shape[2])
            return v, off + n

        ssm_flat = ssm_o[:].rearrange("p a b -> p (a b)")

        def O(off, *shape):
            n = 1
            for s in shape:
                n *= s
            v = ssm_flat[:, off:off + n]
            if len(shape) == 2:
                v = v.rearrange("p (a b) -> p a b", b=shape[1])
            if len(shape) == 3:
                v = v.rearrange("p (a b c) -> p a b c", b=shape[1], c=shape[2])
            return v, off + n

        kviq, at = W(0, 12, T)
        keep = 16384 - 4096
        smp, k1 = W(keep, PAST + 1)
        sel_idx, k1 = W(k1, TOPK)
        small, k1 = W(k1, T)
        dtT = small[0:32, :]
        acT, k1 = W(k1, T)
        tok, k1 = W(k1, 5, 48)
        actok, k1 = W(k1, 4, 32)
        qkvs, k1 = W(k1, 12, NB)
        dsk, k1 = W(k1, 16)
        ik_s, k1 = W(k1, NB)
        hvec, k1 = W(k1, 8)
        ilv, k1 = W(k1, 8)
        vload, k1 = W(k1, P)
        assert k1 <= 16384, k1
        ik2, at = W(at, T)
        ikt1, at = W(at, T)
        ikt2, at = W(at, T)
        ikt3, at = W(at, T)
        iqs, at = W(at, 8, NB)
        iqsw, at = W(at, 8, NB)
        IQ, at = W(at, NB, 32)
        wdiag, at = W(at, NB, IH)
        wbc, at = W(at, NB, IH)
        tapload, at = W(at, P)
        dskload, at = W(at, 16)
        taps, at = W(at, P)
        pgf, at = W(at, 24)
        drelu, at = W(at, 16)
        iqp, at = W(at, 8, NB)
        gat, at = W(at, 2, 512)
        gatT, at = W(at, 512)
        drs, at = W(at, P)
        dsc, at = W(at, NB * 2 * 8)
        assert at <= keep, at
        gatT = [gatT, O(7488, 512)[0]]
        xtok, o1 = O(0, 4, D)
        xstok, o1 = O(o1, D)
        sq2, o1 = O(o1, 2, T)
        rbc, o1 = O(o1, T)
        spz, o1 = O(o1, T)
        spw, o1 = O(o1, T)
        spa, spe = sq2[:, 0, :], sq2[:, 1, :]
        kvtok, o2 = O(0, 5, 512)
        iktok, o2 = O(o2, 5, ID)
        X0 = [None, 0, 256, 640]
        EXT = [P, 256, 384, 512]
        sc, o2 = O(o2, 1152)
        wk, o2 = O(o2, 1152)
        rl, _ = O(o2, 2, 1152)
        AT = [0, P, 384, 768]
        lg, _ = O(o2, 1280)
        pT, _ = O(o2 + 1280, 10, P)
        qslot = ikt1
        PB = [(4, 0), (4, 128), (4, 256), (5, 0), (5, 128), (5, 256), (6, 0), (6, 128), (6, 256), (6, 384)]
        amx = sb("amx", [P, 4])
        anm = sb("anm", [P, 4])
        asum = sb("asum", [P, 4])
        idxT = sb("idxT", [P, 24], I32)
        gidx = sb("gidx", [P, 16], U32)
        m8 = sb("m8", [P, 3, 8])
        scratch = nc.dram_tensor("decode_scores", (NB, PAST), F32, kind="Internal").ap()
        iqslot = [ikt3, ikt1]

        ring_flat = ring[:].rearrange("p s k c -> p (s k c)")[:, 3 * SLOT:]

        def R(off, *shape):
            n = 1
            for d in shape:
                n *= d
            v = ring_flat[:, off:off + n]
            if len(shape) == 2:
                v = v.rearrange("p (a b) -> p a b", b=shape[1])
            if len(shape) == 3:
                v = v.rearrange("p (a b c) -> p a b c", b=shape[1], c=shape[2])
            return v, off + n

        raw, sa = W(0, 4, T + 3)
        xc, sa = W(sa, 4, T)
        st, sa = W(sa, 2, NB, NS)
        Y, sa = W(sa, 2, T)
        th, sa = W(sa, 2, T)
        thz, sa = W(sa, 2, T)
        sqg, sa = W(sa, 2, T)
        rbg, sa = W(sa, T)
        hT, sa = W(sa, 256)
        t2, ra = R(0, NB, NS)
        M2, ra = R(ra, 2, 512)
        Cx2, ra = R(ra, 2, 512)
        CBm, ra = R(ra, 4, P)
        Bt, ra = R(ra, 4, P)
        xw, ra = R(ra, 4, 256)
        sout, ra = R(ra, 2, P)
        assert ra <= 3 * SLOT, ra
        xdt = sb("xdt", [P, 4, 256])
        scl, ra = R(ra, 512)
        scl = scl[0:24, :]
        smallg, sa = W(sa, 512)
        ctok, sa = W(sa, 512)
        assert sa <= keep and ra <= 3 * SLOT, (sa, ra)
        so = 0

        def G(*shape):
            nonlocal so
            n = 1
            for d in shape:
                n *= d
            v = smallg[:, so:so + n]
            so += n
            if len(shape) == 2:
                v = v.rearrange("p (a b) -> p a b", b=shape[1])
            if len(shape) == 3:
                v = v.rearrange("p (a b c) -> p a b c", b=shape[1], c=shape[2])
            return v

        cw = G(24)
        dtg, atg = G(4, 4), G(4, 4)
        sct = G(4, 24)
        sc0, sc1, sc2, sc3 = G(4, NB), G(4, NB), G(4, NB), G(4, NB)
        dts, dAs, xdts, ys = G(2, NB), G(2, NB), G(2, NB), G(2, NB)
        alast, ealast = G(4, 4), G(4, 4)
        wexp = G(4, 4)
        dm8 = G(8)
        dix = sb("dix", [NB, 8], U32)
        pgb32 = sb("pgb32", [P, P], I32)

        mix, da = W(0, KT, T)
        hid, _ = W(0, FT, T)
        KV, da = W(da, 2, 16, 256)
        stage, _ = W(da, 2, T)
        KTd, da = W(da, 2, 512)
        da += 2 * T - 1024
        hit, da = W(da, 16, 16)
        pgb, da = W(da, NB, NPG)
        dpg, da = W(da, NB, NPG)
        pos, da = W(da, 16)
        posc, da = W(da, 16)
        gone, da = W(da, 16)
        lk, da = W(da, 2, NB, NH)
        lrow, da = W(da, TOPK + 1)
        assert da <= keep + PAST + 1, da
        gate, _ = W(keep + PAST + 1 + TOPK, 2, T)
        xdt_flat = xdt[:].rearrange("p c q -> p (c q)")
        qk_new = xdt_flat[:, 0:64].rearrange("p (b h) -> p b h", h=NH)
        pTd = xdt_flat[:, 64:192].rearrange("p (o b h) -> p o b h", o=2, h=NH)
        pv_new = xdt_flat[:, 192:256].rearrange("p (b h) -> p b h", h=NH)
        dmin, dmax, dsum = xdt_flat[0:64, 256:257], xdt_flat[0:64, 257:258], xdt_flat[0:64, 258:259]
        ytok, ystok = xtok, xstok
        SBR_SLOTS = [(0, 1, 2), (3, 4, 5)]
        ATT_SLOTS = [(0, 1), (2, 3)]
        DOWN_SLOTS = [(4, 5, 2), (3, 0, 1)]

        N_IQ, N_QKV, N_SSM, N_SBR = 2, 10, 22, 70
        N_ATT, N_OUT, N_FFN, N_DOWN, N_END = 86, 102, 110, 154, 162
        F_SSM = [2, 2, 0, 2, 2, 2]
        F_SBR = [10, 2, 8, 2, 2, 2]
        F_ATT = [12, 4, 10, 4, 4, 4]
        F_OUT = [14, 6, 12, 6, 4, 4]
        F_FFN = [14, 6, 12, 6, 6, 6]
        F_DOWN = [20, 12, 17, 11, 6, 6]
        VECS_TURNED, IK_MEAN, PAGES_TURNED, IK_VAR, PAGES_SPREAD, TOK_TURNED = 1, 2, 3, 4, 5, 6
        WBC_DONE, IK_TURNED, POS_TURNED, LK_TURNED, DP_TURNED, DVALUES_DONE = 7, 8, 9, 10, 11, 12
        EPS_SET, IQ_ZERO, PAGES_F, DT_ABS, IK_SQ_IN, PAGEST = 1, 2, 3, 4, 5, 6
        GIDX_READY, IK_READY, IDX_ZERO, WK_READY, MASK_READY, RAW_ZERO = 7, 8, 9, 10, 11, 12
        QK_NEW_READY, ROWS_READY, LK_READY, DMAX_READY, DP_READY, DO_READY = 13, 14, 15, 16, 17, 18
        POS_READ, LROW_READY, DEXP_DONE, PTD_READY = 1, 2, 3, 4
        w_in_slot = [S(f"weights_in_slot{i}") for i in range(NSLOT)]

        def w_block(w, c0, n=2 * P, k0=0, kt=KT):
            return w[0, k0:k0 + kt * P].rearrange("(k p) c -> p k c", p=P)[:, :, bass.ds(c0, n)]

        def load(sp, slot, src, freed=None, col=0):
            if freed is not None:
                sp.wait_ge(S("dense_done"), freed)
            kt, n = src.shape[1], src.shape[2]
            sp.dma_start(ring[:, slot, 0:kt, col:col + n], src).then_inc(w_in_slot[slot], 16)

        def dense(pe, n, pair, lhs, rhs, m=P, k0=0, k1=None):
            if k0 == 0 and (not isinstance(n, int) or n >= 2):
                pe.wait_ge(S("dense_read"), n - 1)
            for k in range(k0, k1 or len(lhs)):
                for h in range(2):
                    mm = pe.matmul(ps[0:m, 2 * pair + h, 0:TH], lhs[k], rhs[k][:, h * TH:(h + 1) * TH],
                                   start=(k == 0), stop=(k == len(lhs) - 1))
            if k == len(lhs) - 1:
                mm.then_inc(S("dense_done"), 1)

        def tile_out(pair, m=P):
            return ps[0:m, 2 * pair:2 * pair + 2, 0:TH]

        def two(ap):
            return ap.rearrange("p (h t) -> p h t", h=2)

        xns = [xn[:, k, :] for k in range(KT)]

        def block_of(slot, j, kt=KT):
            return [ring[:, slot, k, j * P:(j + 1) * P] for k in range(kt)]

        def rms_pe(pe, i, sq):
            for k in range(KT):
                pe.wait_ge(S("norm_squared"), KT * i + k + 1)
                for h in range(2):
                    mm = pe.matmul(ps[:, 6 + h, 0:TH], ones, sq[:, k % 2, h * TH:(h + 1) * TH],
                                   start=(k == 0), stop=(k == KT - 1))
                mm.then_inc(S("norm_summed"), 1)

        def rms_act(act, i, x_of, sq, root, ready=None):
            for k in range(KT):
                if ready is not None:
                    act.wait_ge(S("res_added"), ready + k + 1)
                if k >= 2:
                    act.wait_ge(S("norm_summed"), KT * i + k - 1)
                act.activation(sq[:, k % 2, :], x_of(k), ACT.Square).then_inc(S("norm_squared"), 1)
            act.wait_ge(S("norm_summed"), KT * i + KT)
            act.activation(two(root), ps[:, 6:8, 0:TH], ACT.Sqrt, scale=1.0 / D,
                           bias=eps[:, 0:1]).then_inc(S("norm_root"), 1)

        def rms_dve(v, i, x_of, out_of, w_col, root):
            v.wait_ge(S("norm_root"), i + 1)
            v.reciprocal(root, root).then_inc(S("norm_recip"), 1)
            v.wait_ge(S("norm_recip"), i + 1)
            for k in range(KT):
                v.scalar_tensor_tensor(out_of(k), x_of(k), vec[:, w_col + k:w_col + k + 1], root,
                                       ALU.mult, ALU.mult).then_inc(S("norm_ready"), 1)

        block = ctx.enter_context(nc.Block())

        @block.sync
        def _(sp):
            sp.sem_inc(S("sout_out"), OPEN)
            sp.dma_start(cst[:], consts).then_inc(S("consts_in"), 16)
            sp.dma_start(xtok[:], x_prompt[0].rearrange("(b p) d -> p b d", p=P)).then_inc(S("x_in"), 16)
            sp.dma_start(xstok[0:NB, :], x_sample[:, 0, :]).then_inc(S("x_in"), 16)
            r = 0
            for v, n in ((norm1_w[0], 8), (norm2_w[0], 8), (normf_w, 8), (ssm_norm_w[0], 16), (conv_b[0], 32)):
                sp.dma_start(vload[r:r + n, :], v.rearrange("(n p) -> n p", p=P)).then_inc(S("vecs_in"), 16)
                r += n
            sp.dma_start(tapload, conv_w[0].rearrange("i (n p) -> (i n) p", p=P)).then_inc(S("vecs_in"), 16)
            with nc.allow_non_contiguous_dma(reason="a few small vectors"):
                for i, v in enumerate((dt_bias, a_log)):
                    sp.dma_start(hvec[0:32, i:i + 1], v[0].rearrange("(p o) -> p o", o=1)).then_inc(S("vecs_in"), 16)
                for i, v in enumerate((idx_ln_w, idx_ln_b)):
                    for h in range(2):
                        sp.dma_start(ilv[64 * h:64 * h + 64, i:i + 1],
                                     v[0].rearrange("(p o) -> p o", o=1)).then_inc(S("vecs_in"), 16)
                sp.dma_start(dskload[0:2, 0:16], d_skip[0].rearrange("(j k) -> k j", k=2)).then_inc(S("vecs_in"), 16)
            for o, c, n in ((0, C_IK, 64), (64, C_IK, 64), (128, C_DT, 32), (160, C_IW, 16)):
                sp.dma_start(ring[:, 2, :, o:o + n], w_block(w_in, c, n)).then_inc(S("small_in"), 16)
            sp.dma_start(idxT[0:NB, 0:NPG], page_table).then_inc(S("pages_in"), 16)
            for s in range(2):
                load(sp, s, w_block(w_in, C_IQ + s * 256))
            for s in range(3):
                load(sp, 3 + s, w_block(w_in, s * 256))
            for s in range(2):
                load(sp, s, w_block(w_in, C_IQ + (2 + s) * 256), N_IQ + 2 * s + 2)
            for s in range(3):
                load(sp, 3 + s, w_block(w_in, (3 + s) * 256), N_QKV + 2 * s + 2)
            sp.wait_ge(S("iqs_copied"), 1)
            sp.dma_start(iqsw[0:64].rearrange("p j b -> p (j b)"), iqs[64:P].rearrange("p j b -> p (j b)")).then_inc(S("iqs_swapped"), 16)
            sp.dma_start(iqsw[64:P].rearrange("p j b -> p (j b)"), iqs[0:64].rearrange("p j b -> p (j b)")).then_inc(S("iqs_swapped"), 16)
            sp.wait_ge(S("dsc_ready"), OPEN + 16)
            sp.dma_start(scratch.rearrange("b (o p k) -> p (b o) k", o=2, k=8),
                         dsc.rearrange("p (a k) -> p a k", k=8)).then_inc(S("dsc_out"), 16)
            sp.wait_ge(S("dsc_out"), 16)
            sp.dma_start(smp[0:NB, 0:PAST], scratch).then_inc(S("smp_in"), 16)
            sp.wait_ge(S("iktok_copied"), 2)
            sp.dma_start(ik_prompt[0, 0].rearrange("(b p) d -> p b d", p=P), iktok[:, 0:4, :]).then_inc(S("stored"), 16)
            sp.dma_start(ik_sample[0, :, 0], iktok[0:NB, 4, :]).then_inc(S("stored"), 16)
            sp.wait_ge(S("kvtok_copied"), 5)
            for o, c in ((k_prompt, 0), (v_prompt, 256)):
                sp.dma_start(o[0, 0].rearrange("(b p) g d -> p b (g d)", p=P),
                             kvtok[:, 0:4, c:c + 256]).then_inc(S("stored"), 16)
            for o, c in ((k_sample, 0), (v_sample, 256)):
                sp.dma_start(o[0, :, 0].rearrange("b g d -> b (g d)"), kvtok[0:NB, 4, c:c + 256]).then_inc(S("stored"), 16)
            sp.dma_start(conv_sample[0, :, 0:2, :], state_conv[0, :, 1:3, :]).then_inc(S("stored"), 16)

            def group_weights(g):
                first = isinstance(g, int) and g == 0
                load(sp, 0, w_block(w_in, C_X + g * 256), N_QKV if first else N_SSM + 6 * g - 4)
                yield
                for o, c in ((0, C_B), (128, C_C)):
                    if o == 0:
                        sp.wait_ge(S("dense_done"), N_QKV if first else N_SSM + 6 * g - 2)
                    sp.dma_start(ring[:, 1, :, o:o + P], w_block(w_in, c + g * P, P)).then_inc(S("bc_in"), 16)
                yield
                load(sp, 2, w_block(w_in, C_Z + g * 256), N_QKV if first else N_SSM + 6 * g)
                yield

            def load_state(g):
                for j in range(2):
                    sp.dma_start(st[:, j], state_ssm[0].rearrange("b (j h) p n -> (h p) j b n", h=2)[
                        :, bass.ds(2 * g + j, 1)].rearrange("p o b n -> p (o b) n")).then_inc(S("state_in"), 16)

            def load_conv(g):
                src = state_conv[0].rearrange("b i c -> (b i) c")
                for o, c, n in ((0, 256 * g, 256), (256, DI + P * g, P), (384, DI + NG * P + P * g, P)):
                    sp.dma_start(scl[:, o:o + n], src[:, bass.ds(c, n)]).then_inc(S("scl_in"), 16)

            def store_state(g):
                sp.wait_ge(S("state_new"), 2 * g + 2)
                for j in range(2):
                    sp.dma_start(ssm_sample[0].rearrange("b (j h) p n -> (h p) j b n", h=2)[
                        :, bass.ds(2 * g + j, 1)].rearrange("p o b n -> p (o b) n"), st[:, j]).then_inc(S("state_out"), 16)

            def store_conv(g):
                sp.wait_ge(S("ctok_ready"), g + 1)
                for o, c, n in ((0, 256 * g, 256), (256, DI + P * g, P), (384, DI + NG * P + P * g, P)):
                    sp.dma_start(conv_prompt[0, 0][:, bass.ds(c, n)], ctok[0:3, o:o + n]).then_inc(S("ctok_out"), 16)
                    sp.dma_start(conv_sample[0, :, 2, :][:, bass.ds(c, n)], ctok[3:11, o:o + n]).then_inc(S("ctok_out"), 16)

            def store_prompt_state(g):
                sp.wait_ge(S("sout_ready"), g + 1)
                sp.dma_start(ssm_prompt[0, 0].rearrange("h p n -> (h p) n").rearrange("(j q) n -> q j n", q=P)[
                    :, bass.ds(2 * g, 2)], sout).then_inc(S("sout_out"), 16)

            def load_selectors(g):
                sp.dma_start(gs[:], gsel_d[bass.ds(g, 1)].rearrange("o p c -> (o p) c")
                             if not isinstance(g, int) else gsel_d[g]).then_inc(S("gs_in"), 16)

            for _ in group_weights(0):
                pass
            load_selectors(0)
            sp.wait_ge(S("o_done"), OPEN + NH)
            load_conv(0)
            load_state(0)
            for _ in group_weights(1):
                pass

            def group_io(g, more, last=False):
                store_conv(g)
                sp.wait_ge(S("aux_done"), g + 1)
                if not last:
                    load_conv(g + 1)
                ws = group_weights(g + 2) if more else iter(())
                next(ws, None)
                store_state(g)
                next(ws, None)
                if not last:
                    sp.wait_ge(S("state_out"), 32 * g + 32)
                    sp.wait_ge(S("C_used"), 2 * g + 2)
                    load_state(g + 1)
                next(ws, None)
                if not last:
                    sp.wait_ge(S("abc_done"), 4 * g + 4)
                    load_selectors(g + 1)

            group_io(0, True)
            with sp.Fori(1, NG - 2) as g:
                store_prompt_state(g - 1)
                group_io(g, True)
            store_prompt_state(NG - 3)
            group_io(NG - 2, False)
            store_prompt_state(NG - 2)
            def load_sbr(it):
                slots, n = SBR_SLOTS[it % 2], N_SBR + 4 * (it - 2)
                first = it < 2
                load(sp, slots[0], w_block(w_in, C_GM + it * 256), N_SBR - 4 if first else n + 2)
                load(sp, slots[1], w_block(w_ssm_br, it * 256), N_SBR - 2 if first else n + 4)
                load(sp, slots[2], w_block(w_ssm_br, it * 256, k0=D), N_SBR if first else n + 4)

            load_sbr(0)
            sp.dma_start(pgb32[:], page_table.rearrange("b n -> (b n)").partition_broadcast(P)).then_inc(S("pgb_in"), 16)
            group_io(NG - 1, False, last=True)
            store_prompt_state(NG - 1)
            sp.wait_ge(S("sout_out"), 16 * NG + OPEN)
            sp.wait_ge(S("y_done"), 4 * NG)
            sp.wait_ge(S("h_done"), 4 * NG)
            sp.wait_ge(S("ys_ready"), 2 * NG)
            for it in range(1, 4):
                load_sbr(it)
            for it in range(4):
                ga_slot, at_slot = ATT_SLOTS[it % 2]
                freed = ((N_SBR + 10, N_SBR + 12), (N_SBR + 12, N_SBR + 14), (N_ATT + 2, N_ATT + 4),
                         (N_ATT + 6, N_ATT + 8))[it]
                load(sp, ga_slot, w_block(w_in, C_GA + it * 256), freed[0])
                load(sp, at_slot, w_block(w_attn_br, it * 256), freed[1])
                if it == 1:
                    load(sp, 4, w_block(w_out, 0), N_ATT)
                    load(sp, 5, w_block(w_out, 256), N_ATT)
            for it in range(2):
                load(sp, 2 * it, w_block(w_ffn_gate, it * 256), N_ATT + 10 + 4 * it)
                load(sp, 2 * it + 1, w_block(w_ffn_up, it * 256), N_ATT + 12 + 4 * it)
            load(sp, 4, w_block(w_out, 512), N_OUT + 2)
            load(sp, 5, w_block(w_out, 768), N_OUT + 4)
            load(sp, 4, w_block(w_ffn_down, 0), N_OUT + 6)
            load(sp, 5, w_block(w_ffn_down, 0, k0=D), N_OUT + 8)
            with sp.Fori(0, 4) as k:
                for o in range(2):
                    load(sp, 2 * o, w_block(w_ffn_gate, 512 * k + 256 * (o + 2)), 8 * k + N_FFN + 4 * o + 2)
                    load(sp, 2 * o + 1, w_block(w_ffn_up, 512 * k + 256 * (o + 2)), 8 * k + N_FFN + 4 * o + 4)
            load(sp, 0, w_block(w_ffn_gate, 2560), N_FFN + 34)
            load(sp, 1, w_block(w_ffn_up, 2560), N_FFN + 36)
            for it in range(4):
                for i, slot in enumerate(DOWN_SLOTS[it % 2]):
                    if it == 0 and i < 2:
                        continue
                    freed = N_DOWN + 2 * (it - 1) if it > 1 else {2: N_FFN + 38, 3: N_FFN + 40, 0: N_FFN + 42, 1: N_FFN + 44}[slot]
                    load(sp, slot, w_block(w_ffn_down, 256 * it, k0=D * i, kt=(8, 8, 6)[i]), freed)
            for b in range(4):
                sp.wait_ge(S("y_ready"), 2 * b + 2)
                sp.dma_start(y_prompt[0, b * P:(b + 1) * P, :], ytok[:, b, :]).then_inc(S("stored"), 16)
            sp.wait_ge(S("y_ready"), 10)
            sp.dma_start(y_sample[:, 0, :], ystok[0:NB, :]).then_inc(S("stored"), 16)
            sp.wait_ge(S("smp_in"), 16)
            sp.wait_ge(S("stored"), 12 * 16)
            sp.wait_ge(S("ctok_out"), 96 * NG)
            sp.wait_ge(S("state_out"), 32 * NG)
            sp.wait_ge(S("sout_out"), 16 * NG + OPEN)

        @block.tensor
        def _(pe):
            def index_scores(pe):
                pe.wait_ge(S("vector_mark"), IK_READY)
                pe.wait_ge(S("dense_read"), 16)
                pe.wait_ge(S("tok_copied"), 3)
                with pe.Fori(0, 4) as k:
                    for j in range(2):
                        pe.wait_ge(S("iq_in_slot"), 2 * k + j + 1)
                        for h in range(2):
                            pe.wait_ge(S("relu_done"), OPEN + 12 * k + 6 * j)
                            for b in (1, 2, 3):
                                mm = pe.matmul(ps[:, 1 + 3 * h + b, 0:EXT[b]],
                                               iqslot[j][64 * h:64 * h + 64, b * P:(b + 1) * P],
                                               ik2[64 * h:64 * h + 64, 0:EXT[b]], start=True, stop=True)
                                mm.then_inc(S("idx_done"), 1)

            def decode_scores(pe):
                pe.wait_ge(S("IQ_ready"), 4)
                pe.wait_ge(S("relu_done"), OPEN + 48)
                pe.wait_ge(S("wdiag_ready"), 2)
                pe.matmul(ps[:, 0, 0:P], ones[32:48, :], wdiag[32:48].rearrange("p b h -> p (b h)"),
                          start=True, stop=True)
                for j in range(8):
                    mm = pe.matmul(ps[0:NB, 0, P + 2 * j:P + 2 * j + 2], iqp[:, j, :],
                                   cst[:, K_PAR:K_PAR + 2], start=True, stop=True)
                mm.then_inc(S("tensor_mark"), 1)

                def turn(k, o):
                    pe.wait_ge(S("gathered%d" % o), 16 * k + 16)
                    for c in range(4):
                        mm = pe.transpose(ps[:, 4 + o, c * P:(c + 1) * P], gat[:, o, c * P:(c + 1) * P], ident)
                    mm.then_inc(S("gat_turned"), 1)

                with pe.Fori(0, NB) as k:
                    for o in range(2):
                        pe.wait_ge(S("gatT_ready"), OPEN + 2 * k)
                        turn(k, o)
                    for o in range(2):
                        pe.wait_ge(S("gatT_ready"), OPEN + 2 * k + o + 1)
                        pe.wait_ge(S("drs_done"), OPEN + 2 * k)
                        for c in range(4):
                            mm = pe.matmul(ps[:, 6 + o, 32 * c:32 * c + 32], gatT[o][:, c * P:(c + 1) * P],
                                           IQ[:, k, :], start=True, stop=True)
                        mm.then_inc(S("dec_done"), 1)

            for name in ("dec_done", "idx_done", "p_turned", "o_done", "logits_done"):
                pe.sem_inc(S(name), OPEN)
            pe.wait_ge(S("consts_in"), 16)
            pe.wait_ge(S("x_in"), 32)
            for k in range(KT):
                if k >= 2:
                    pe.wait_ge(S("xT_ready"), 2 * k - 2)
                for b in range(4):
                    pe.transpose(ps[:, k % 2, b * P:(b + 1) * P], xtok[:, b, k * P:(k + 1) * P], ident)
                pe.transpose(ps[:, 2 + k % 2, 0:NB], xstok[0:NB, k * P:(k + 1) * P],
                             ident[0:NB, 0:NB]).then_inc(S("x_turned"), 1)
            pe.wait_ge(S("vecs_in"), 16 * 13)
            pe.transpose(ps[:, 4, 0:72], vload[0:72, :], ident[0:72, 0:72])
            pe.transpose(ps[:, 4, 128:256], tapload, ident)
            pe.matmul(ps[:, 4, 256:272], cst[0:2, K_HALF:K_HALF + P], dskload[0:2, :], start=True,
                      stop=True).then_inc(S("tensor_mark"), 1)
            rms_pe(pe, 0, sq2)
            pe.wait_ge(S("norm_ready"), KT)
            pe.wait_ge(S("xT_ready"), 2 * KT)
            pe.wait_ge(S("small_in"), 64)
            dense(pe, 0, 0, [ring[:, 2, k, 0:P] for k in range(KT)], xns)
            dense(pe, 1, 1, [ring[:, 2, k, P:P + 48] for k in range(KT)], xns, m=48)
            pe.wait_ge(S("dense_read"), 1)
            for h in range(2):
                mm = pe.matmul(ps[:, 4 + h, 0:TH], blk64, ik2[:, h * TH:(h + 1) * TH], start=True, stop=True)
            mm.then_inc(S("tensor_mark"), 1)
            pe.wait_ge(S("vector_mark"), PAGES_F)
            pe.transpose(ps[0:NPG, 6, 0:NB], pgf[0:NB, 0:NPG], ident[0:NB, 0:NB]).then_inc(S("tensor_mark"), 1)
            with pe.Fori(0, 2) as k:
                for s in range(2):
                    pe.wait_ge(w_in_slot[s], 16 * k + 16)
                    for j in range(2):
                        dense(pe, 4 * k + N_IQ + 2 * s + j, j, block_of(s, j), xns)
            pe.wait_ge(S("ik_sq"), 1)
            for h in range(2):
                mm = pe.matmul(ps[:, 4 + h, 0:TH], blk64, ikt2[:, h * TH:(h + 1) * TH], start=True, stop=True)
            mm.then_inc(S("tensor_mark"), 1)
            pe.wait_ge(S("vector_mark"), PAGEST)
            for o in range(2):
                mm = pe.matmul(ps[:, 6, 16 + o * NB:16 + (o + 1) * NB], cst[0:NPG, K_PG + o * P:K_PG + (o + 1) * P],
                               pgf[0:NPG, NPG:NPG + NB], start=True, stop=True)
            mm.then_inc(S("tensor_mark"), 1)
            pe.wait_ge(S("a_summed"), 4)
            for b in range(5):
                n = P if b < 4 else NB
                pe.transpose(ps[0:n, 7, 48 * b:48 * b + 48], small[0:48, b * P:b * P + n], ident[0:48, 0:48])
            for c in range(4):
                mm = pe.transpose(ps[:, 7, 256 + 32 * c:288 + 32 * c], acT[0:32, c * P:(c + 1) * P], ident[0:32, 0:32])
            mm.then_inc(S("tensor_mark"), 1)
            for k in range(2):
                for s in range(3):
                    pe.wait_ge(w_in_slot[3 + s], 16 * k + 16)
                    for j in range(2):
                        dense(pe, 6 * k + N_QKV + 2 * s + j, j, block_of(3 + s, j), xns)
                if k == 0:
                    index_scores(pe)
                    decode_scores(pe)
            pe.wait_ge(S("gatT_ready"), OPEN + 2 * NB)
            pe.wait_ge(S("drs_done"), OPEN + 2 * NB)
            for b in range(4):
                pe.transpose(ps[:, 4, b * ID:(b + 1) * ID], ik2[0:64, b * P:(b + 1) * P], ident[0:64, 0:64])
            pe.transpose(ps[0:NB, 4, 256:256 + ID], ik2[0:64, SEQ:T], ident[0:64, 0:64]).then_inc(S("tensor_mark"), 1)
            pe.wait_ge(S("dense_read"), N_SSM)
            for b in range(5):
                n, bank = (P, 5 + b % 2) if b < 4 else (NB, 5)
                if b >= 2:
                    pe.wait_ge(S("kvtok_copied"), b - 1)
                for i in range(4):
                    mm = pe.transpose(ps[0:n, bank, i * P:(i + 1) * P], kviq[:, i, b * P:b * P + n], ident)
                mm.then_inc(S("kv_turned"), 1)

            def logits(i, kv):
                pe.wait_ge(S("q_in_slot"), i + 1)
                for b in range(4):
                    if b == 0:
                        pe.wait_ge(S("logits_read"), OPEN + 4 * i)
                    mm = pe.matmul(ps[:, b, 0:EXT[b]], qslot[:, b * P:(b + 1) * P], kviq[:, kv, 0:EXT[b]],
                                   start=True, stop=True)
                    mm.then_inc(S("logits_done"), 1)

            def values(i, kv):
                for b in range(4):
                    pe.wait_ge(S("p_ready"), 4 * i + b + 1)
                    for c in range(b + 1):
                        n = AT[b] // P + c
                        bank, col = PB[n]
                        mm = pe.transpose(ps[:, bank, col:col + P], lg[:, AT[b] + c * P:AT[b] + (c + 1) * P], ident)
                    mm.then_inc(S("p_turned"), 1)
                pe.wait_ge(S("o_read"), OPEN + i)
                for b in range(4):
                    pe.wait_ge(S("pT_ready"), 3 * i + (1, 1, 2, 3)[b])
                    for c in range(b + 1):
                        mm = pe.matmul(ps[:, 7, b * P:(b + 1) * P], kvtok[:, c, 256 + kv * P:256 + (kv + 1) * P],
                                       pT[:, AT[b] // P + c, :], start=(c == 0), stop=(c == b))
                mm.then_inc(S("o_done"), 1)

            pe.wait_ge(S("kvtok_copied"), 5)
            pe.wait_ge(S("iktok_copied"), 2)
            pe.wait_ge(S("dense_read"), N_SSM)
            logits(0, 0)
            with pe.Fori(0, 3) as r:
                logits(r + 1, 0)
                values(r, 0)
            logits(4, 1)
            values(3, 0)
            with pe.Fori(4, 7) as r:
                logits(r + 1, 1)
                values(r, 1)
            values(7, 1)

            def group_tile(g, i, k0=0, k1=KT):
                s, j = i // 2, i % 2
                if k0:
                    pass
                elif i == 2:
                    pe.wait_ge(S("bc_in"), 32 * g + 32)
                elif j == 0:
                    pe.wait_ge(w_in_slot[s], 16 * (g + F_SSM[s]) + 16)
                dense(pe, 6 * g + N_SSM + i, j, block_of(s, j), xns, k0=k0, k1=k1)

            def step_aux(g, prev):
                pe.wait_ge(S("dense_read"), 6 * g + N_SSM + 4)
                if prev:
                    pe.wait_ge(S("h_done"), 4 * g)
                for i in range(4):
                    mm = pe.transpose(ps[0:11, 5, i * P:(i + 1) * P], raw[:, i, SEQ:SEQ + 11], ident)
                mm.then_inc(S("ctok_done"), 1)
                pe.wait_ge(S("scl_in"), 48 * g + 48)
                pe.wait_ge(S("gs_in"), 16 * g + 16)
                for j in range(2):
                    sel = gs[:, 512 + j * P:512 + (j + 1) * P]
                    pe.matmul(ps[:, 4, 96 + NB * j:96 + NB * (j + 1)], sel, dtT[0:32, SEQ:T], start=True, stop=True)
                    pe.matmul(ps[:, 4, 112 + NB * j:112 + NB * (j + 1)], sel, acT[0:32, SEQ:T], start=True, stop=True)
                for i in range(4):
                    mm = pe.transpose(ps[:, 4, i * 24:(i + 1) * 24], scl[:, i * P:(i + 1) * P], ident[0:24, 0:24])
                for r in range(4):
                    mm = pe.matmul(ps[:, 4, 384 + 4 * r:388 + 4 * r], gs[:, r * P:(r + 1) * P], acT[0:32, P - 1:SEQ:P],
                                   start=True, stop=True)
                if prev:
                    for j in range(2):
                        mm = pe.transpose(ps[:, 4, P + j * P:P + (j + 1) * P], hT[:, j * P:(j + 1) * P], ident)
                mm.then_inc(S("aux_done"), 1)

            def step_norm(g):
                for j in range(2):
                    pe.wait_ge(S("sqg_ready"), 2 * g + j + 1)
                    for h in range(2):
                        mm = pe.matmul(ps[:, 6 + h, 0:TH], ones, sqg[:, j, h * TH:(h + 1) * TH],
                                       start=(j == 0), stop=(j == 1))
                mm.then_inc(S("sumg_done"), 1)

            def step_turn(g, prev):
                pe.wait_ge(S("ctok_ready"), g + 1)
                if prev:
                    pe.wait_ge(S("rootg"), g)
                pe.wait_ge(S("silu_done"), 4 * g + 3)
                for c in range(4):
                    for j in range(2):
                        pe.transpose(ps[:, 6 + c // 2, (c % 2) * 256 + j * P:(c % 2) * 256 + (j + 1) * P],
                                     xc[:, j, c * P:(c + 1) * P], ident)
                for c in range(4):
                    mm = pe.transpose(ps[:, 5, c * P:(c + 1) * P], xc[:, 2, c * P:(c + 1) * P], ident)
                mm.then_inc(S("turned"), 1)

            def step_decode(g):
                pe.wait_ge(S("xdt_ready"), 2 * g + 2)
                pe.wait_ge(S("Bt_ready"), g + 1)
                pe.wait_ge(S("aux_read"), g + 1)
                pe.wait_ge(S("silu_done"), 4 * g + 4)
                for t, bank in ((2, 6), (3, 4)):
                    for b in range(NB):
                        mm = pe.matmul(ps[:, bank + b // 4, (b % 4) * P:(b % 4 + 1) * P],
                                       xc[:, t, SEQ + b:SEQ + b + 1].broadcast_to((P, P)), ident,
                                       start=True, stop=True)
                    mm.then_inc(S("bcast_done"), 1)

            def step_cb(g):
                pe.wait_ge(S("C_used"), 2 * g + 2)
                for c in range(4):
                    mm = pe.matmul(ps[:, 5, c * P:(c + 1) * P], xc[:, 2, c * P:(c + 1) * P],
                                   xc[:, 3, c * P:(c + 1) * P], start=True, stop=True)
                mm.then_inc(S("cb_done"), 1)

            def step_a(g, c):
                if c:
                    pe.wait_ge(S("abc_read"), 4 * g + c)
                for r in range(4):
                    mm = pe.matmul(ps[:, 4, r * P:(r + 1) * P], gs[:, r * P:(r + 1) * P],
                                   acT[0:32, c * P:(c + 1) * P], start=True, stop=True)
                mm.then_inc(S("abc_done"), 1)

            def step_y(g, c):
                pe.wait_ge(S("M_ready"), 7 * g + 2 * c + 1)
                if c:
                    pe.wait_ge(S("h_done"), 4 * g + c)
                else:
                    pe.wait_ge(S("B_used"), 2 * g + 2)
                for r in range(4):
                    o = ps[64 * (r % 2):64 * (r % 2) + 64, 6 + r // 2, c * P:(c + 1) * P]
                    pe.matmul(o, xdt[:, c, 64 * r:64 * r + 64], M2[:, c % 2, r * P:(r + 1) * P],
                              start=True, stop=(c == 0))
                    if c:
                        pe.matmul(o, hT[:, 64 * r:64 * r + 64], Cx2[:, c % 2, r * P:(r + 1) * P],
                                  start=False, stop=True)
                pe.wait_ge(S("xw_ready"), g + 1)
                pe.matmul(ps[:, 5, 256 * (c % 2):256 * (c % 2) + 256], Bt[:, c, :], xw[:, c, :],
                          start=True, stop=True).then_inc(S("y_done"), 1)

            def group(g, prev, more):
                D = (lambda *a: group_tile(g + 1, *a)) if more else (lambda *a: None)
                D(0, 0, 4)
                step_aux(g, prev)
                D(0, 4, 8)
                D(1, 0, 4)
                if prev:
                    step_norm(g - 1)
                D(1, 4, 8)
                step_turn(g, prev)
                D(2)
                step_decode(g)
                D(3)
                step_cb(g)
                step_a(g, 0)
                D(4, 0, 4)
                step_a(g, 1)
                D(4, 4, 8)
                step_y(g, 0)
                D(5, 0, 2)
                step_a(g, 2)
                D(5, 2, 4)
                step_y(g, 1)
                D(5, 4, 5)
                step_a(g, 3)
                D(5, 5, 8)
                step_y(g, 2)
                step_y(g, 3)

            pe.wait_ge(S("o_read"), OPEN + NH)
            pe.wait_ge(S("vector_mark"), RAW_ZERO)
            for i in range(6):
                group_tile(0, i)
            group(0, False, True)
            with pe.Fori(1, NG - 1) as g:
                group(g, True, True)
            group(NG - 1, True, False)
            step_norm(NG - 1)
            pe.wait_ge(S("h_done"), 4 * NG)
            pe.wait_ge(S("abc_read"), 4 * NG)
            for j in range(2):
                mm = pe.transpose(ps[:, 4, P + j * P:P + (j + 1) * P], hT[:, j * P:(j + 1) * P], ident)
            mm.then_inc(S("aux_done"), 1)

            def sbr(it):
                slots, f = SBR_SLOTS[it % 2], it // 2 + 1
                pe.wait_ge(w_in_slot[slots[0]], 16 * (F_SBR[slots[0]] + f))
                for j in range(2):
                    dense(pe, N_SBR + 4 * it + j, j, block_of(slots[0], j), xns)
                for s in slots[1:]:
                    pe.wait_ge(w_in_slot[s], 16 * (F_SBR[s] + f))
                pe.wait_ge(S("ssm_ready"), 2 * NG)
                for j in range(2):
                    dense(pe, N_SBR + 4 * it + 2 + j, j, block_of(slots[1], j) + block_of(slots[2], j),
                          [ssm_o[:, k, :] for k in range(16)])

            sbr(0)
            pe.wait_ge(S("dtop_kept"), 4 * NG + OPEN)
            pe.wait_ge(S("sout_ready"), NG)
            for o in range(2):
                mm = pe.transpose(ps[:, 4, NB * o:NB * o + NB], sel_idx[0:NB, o * P:(o + 1) * P], ident[0:NB, 0:NB])
            mm.then_inc(S("tensor_mark"), 1)
            sbr(1)
            pe.wait_ge(S("rootg"), NG)
            pe.wait_ge(S("decode_read"), POS_READ)
            pe.wait_ge(S("vector_mark"), QK_NEW_READY)
            pe.matmul(ps[0:64, 7, TOPK:TOPK + 1], qk_new.rearrange("p b h -> p (b h)"), ones[:, 0:1],
                      start=True, stop=True)

            def turn_keys(b):
                if b >= 2:
                    pe.wait_ge(S("KT_ready"), b - 1)
                for o in range(2):
                    for kv in range(2):
                        mm = pe.transpose(ps[:, 4 + b % 2, (2 * o + kv) * P:(2 * o + kv + 1) * P],
                                          KV[:, 0, NB * o + b, kv * P:(kv + 1) * P], ident)
                mm.then_inc(S("keys_turned"), 1)

            pe.wait_ge(S("keys_in"), 16 * 16)
            turn_keys(0)
            for b in range(NB):
                if b + 1 < NB:
                    turn_keys(b + 1)
                pe.wait_ge(S("KT_ready"), b + 1)
                for o in range(2):
                    for kv in range(2):
                        mm = pe.matmul(ps[:, 6, 64 * o + 8 * b + 4 * kv:64 * o + 8 * b + 4 * kv + 4],
                                       KTd[:, b % 2, (2 * o + kv) * P:(2 * o + kv + 1) * P],
                                       qkvs[:, 4 * kv:4 * kv + 4, b], start=True, stop=True)
                mm.then_inc(S("dlogits_done"), 1)
            sbr(2)
            pe.wait_ge(S("vector_mark"), LK_READY)
            for o in range(2):
                mm = pe.transpose(ps[0:64, 7, o * P:(o + 1) * P], lk[:, o].rearrange("p b h -> p (b h)"), ident)
            mm.then_inc(S("tensor_mark"), 1)
            sbr(3)
            pe.wait_ge(S("vector_mark"), DP_READY)
            for o in range(2):
                pe.transpose(ps[:, 4, 64 * o:64 * o + 64], lrow[0:64, o * P:(o + 1) * P], ident[0:64, 0:64])
            pe.matmul(ps[:, 4, 128:192], lrow[0:64, TOPK:TOPK + 1].broadcast_to((64, P)), ident[0:64, 0:64],
                      start=True, stop=True).then_inc(S("tensor_mark"), 1)
            for it in range(4):
                ga_slot, at_slot = ATT_SLOTS[it % 2]
                pe.wait_ge(w_in_slot[ga_slot], 16 * (F_ATT[ga_slot] + it // 2 + 1))
                for j in range(2):
                    dense(pe, N_ATT + 4 * it + j, j, block_of(ga_slot, j), xns)
                if it == 0:
                    pe.wait_ge(S("decode_read"), PTD_READY)
                    pe.wait_ge(S("values_in"), 16 * 16)
                    for b in range(NB):
                        for kv in range(2):
                            for o in range(2):
                                mm = pe.matmul(ps[:, 5, 8 * b + 4 * kv:8 * b + 4 * kv + 4],
                                               KV[:, 1, NB * o + b, kv * P:(kv + 1) * P],
                                               pTd[:, o, b, 4 * kv:4 * kv + 4], start=(o == 0), stop=(o == 1))
                    mm.then_inc(S("tensor_mark"), 1)
                    pe.wait_ge(S("vector_mark"), DO_READY)
                pe.wait_ge(w_in_slot[at_slot], 16 * (F_ATT[at_slot] + it // 2 + 1))
                for j in range(2):
                    dense(pe, N_ATT + 4 * it + 2 + j, j, block_of(at_slot, j), [uT[:, k, :] for k in range(KT)])
            for u in range(4):
                pe.wait_ge(w_in_slot[4 + u % 2], 16 * (F_OUT[4 + u % 2] + u // 2 + 1))
                for j in range(2):
                    if u == 0:
                        pe.wait_ge(S("mixed"), 16)
                    dense(pe, N_OUT + 2 * u + j, j, block_of(4 + u % 2, j), [mix[:, k, :] for k in range(KT)])
            rms_pe(pe, 1, sq2)
            pe.wait_ge(S("norm_ready"), 2 * KT)
            def ffn(k, o):
                for s in range(2):
                    pe.wait_ge(w_in_slot[2 * o + s], 16 * (k + F_FFN[2 * o + s] + 1))
                    for j in range(2):
                        dense(pe, 8 * k + N_FFN + 4 * o + 2 * s + j, j, block_of(2 * o + s, j), xns)

            with pe.Fori(0, 5) as k:
                ffn(k, 0)
                ffn(k, 1)
            ffn(5, 0)
            pe.wait_ge(S("hid_ready"), 2 * OPEN + FT)
            with pe.Fori(0, 2) as k:
                for o in range(2):
                    slots = DOWN_SLOTS[o]
                    for s in slots:
                        pe.wait_ge(w_in_slot[s], 16 * (k + F_DOWN[s] + 1))
                    for j in range(2):
                        blocks = block_of(slots[0], j) + block_of(slots[1], j) + block_of(slots[2], j, 6)
                        dense(pe, 4 * k + N_DOWN + 2 * o + j, j, blocks, [hid[:, i, :] for i in range(FT)])
            rms_pe(pe, 2, sq2)
            pe.wait_ge(S("dense_read"), N_END)
            for b in range(5):
                n = P if b < 4 else NB
                if b >= 2:
                    pe.wait_ge(S("y_ready"), 2 * b - 2)
                for k in range(KT):
                    if b == 0:
                        pe.wait_ge(S("norm_ready"), 2 * KT + k + 1)
                    mm = pe.transpose(ps[0:n, 2 * (b % 2) + k // 4, (k % 4) * P:(k % 4 + 1) * P],
                                      xn[:, k, b * P:b * P + n], ident)
                mm.then_inc(S("y_turned"), 1)

        @block.scalar
        def _(act):
            for name in ("relu_done", "gatT_ready", "o_read"):
                act.sem_inc(S(name), OPEN)
            for k in range(KT):
                act.wait_ge(S("x_turned"), k + 1)
                act.activation(xT[:, k, 0:SEQ], ps[:, k % 2, :], ACT.Copy).then_inc(S("xT_ready"), 1)
                act.activation(xT[:, k, SEQ:T], ps[:, 2 + k % 2, 0:NB], ACT.Copy).then_inc(S("xT_ready"), 1)
            act.wait_ge(S("tensor_mark"), VECS_TURNED)
            act.activation(vec[:, 0:72], ps[:, 4, 0:72], ACT.Copy).then_inc(S("vec_ready"), 1)
            act.activation(taps, ps[:, 4, 128:256], ACT.Copy, scale=0.5).then_inc(S("taps_ready"), 1)
            act.activation(dsk, ps[:, 4, 256:272], ACT.Copy).then_inc(S("dsk_ready"), 1)
            act.wait_ge(S("vector_mark"), EPS_SET)
            act.wait_ge(S("xT_ready"), 2 * KT)
            rms_act(act, 0, lambda k: xT[:, k, :], sq2, rbc)
            act.wait_ge(S("dense_done"), 1)
            act.activation(two(ik2), tile_out(0), ACT.Copy).then_inc(S("dense_read"), 1)
            act.wait_ge(S("dense_done"), 2)
            act.activation(two(small[0:48, :]), tile_out(1, 48), ACT.Copy).then_inc(S("dense_read"), 1)
            act.wait_ge(S("vector_mark"), DT_ABS)
            act.activation(spe[0:32, :], spa[0:32, :], ACT.Exp, scale=-1.0).then_inc(S("dt_exp"), 1)
            act.activation(hvec[0:32, 2:3], hvec[0:32, 1:2], ACT.Exp).then_inc(S("a_exp"), 1)
            act.wait_ge(S("vector_mark"), IK_SQ_IN)
            act.activation(ikt2, ikt1, ACT.Square).then_inc(S("ik_sq"), 1)
            with act.Fori(0, 4) as k:
                for j in range(2):
                    act.wait_ge(S("dense_done"), 2 * k + N_IQ + 1 + j)
                    act.activation(two(kviq[:, 2 * k + 4 + j, :]), tile_out(j), ACT.Copy).then_inc(S("dense_read"), 1)
            act.wait_ge(S("dense_read"), N_QKV)
            act.activation(iqs, kviq[:, 4:12, SEQ:T], ACT.Copy).then_inc(S("iqs_copied"), 1)
            act.wait_ge(S("tensor_mark"), IK_VAR)
            act.activation(two(ikt2), ps[:, 4:6, 0:TH], ACT.Sqrt, bias=eps[:, 0:1]).then_inc(S("ik_root"), 1)
            act.wait_ge(S("tensor_mark"), TOK_TURNED)
            tk = ps[:, 7, 0:240].rearrange("p (b h) -> p b h", h=48)
            act.activation(tok[:, 0:4, 0:32], tk[:, 0:4, 0:32], ACT.Copy).then_inc(S("tok_copied"), 1)
            act.activation(tok[:, 0:4, 32:48], tk[:, 0:4, 32:48], ACT.Copy, scale=1.0 / 32).then_inc(S("tok_copied"), 1)
            act.activation(tok[0:NB, 4, 32:48], tk[0:NB, 4, 32:48], ACT.Copy, scale=1.0 / 32).then_inc(S("tok_copied"), 1)
            act.activation(actok, ps[:, 7, 256:384].rearrange("p (b h) -> p b h", h=32), ACT.Copy).then_inc(S("actok_ready"), 1)
            for j in range(6):
                act.wait_ge(S("dense_done"), N_QKV + 1 + j)
                act.activation(two(uT[:, j, :]), tile_out(j % 2), ACT.Copy).then_inc(S("dense_read"), 1)
            with act.Fori(0, 4) as k:
                for j in range(2):
                    for h in range(2):
                        for b in (1, 2, 3):
                            act.wait_ge(S("idx_done"), OPEN + 12 * k + 6 * j + 3 * h + b)
                            if b == 1:
                                act.wait_ge(S("idx_added"), OPEN + 12 * k + 6 * j)
                            act.activation(rl[:, h, X0[b]:X0[b] + EXT[b]], ps[:, 1 + 3 * h + b, 0:EXT[b]],
                                           ACT.Relu).then_inc(S("relu_done"), 1)
            act.wait_ge(S("tensor_mark"), WBC_DONE)
            act.activation(wbc.rearrange("p b h -> p (b h)"), ps[:, 0, 0:P], ACT.Copy).then_inc(S("wbc_ready"), 1)
            act.activation(drelu[0:NB, :], ps[0:NB, 0, P:P + 16], ACT.Relu).then_inc(S("wbc_ready"), 1)
            with act.Fori(0, NB) as k:
                for o in range(2):
                    act.wait_ge(S("gat_turned"), 2 * k + o + 1)
                    act.wait_ge(S("dec_done"), OPEN + 2 * k)
                    act.activation(gatT[o], ps[:, 4 + o, :], ACT.Copy).then_inc(S("gatT_ready"), 1)
            for j in range(6):
                act.wait_ge(S("dense_done"), N_QKV + 7 + j)
                dst = uT[:, 6 + j, :] if j < 2 else kviq[:, j - 2, :]
                act.activation(two(dst), tile_out(j % 2), ACT.Copy).then_inc(S("dense_read"), 1)
            act.wait_ge(S("dense_read"), N_SSM)
            act.activation(qkvs[:, 0:8, :], uT[:, :, SEQ:T], ACT.Copy).then_inc(S("qkvs_ready"), 1)
            act.activation(qkvs[:, 8:12, :], kviq[:, 0:4, SEQ:T], ACT.Copy).then_inc(S("qkvs_ready"), 1)
            act.wait_ge(S("tensor_mark"), IK_TURNED)
            act.activation(iktok[:, 0:4, :], ps[:, 4, 0:256].rearrange("p (b d) -> p b d", b=4), ACT.Copy).then_inc(S("iktok_copied"), 1)
            act.activation(iktok[0:NB, 4, :], ps[0:NB, 4, 256:320], ACT.Copy).then_inc(S("iktok_copied"), 1)
            for b in range(5):
                n, bank = (P, 5 + b % 2) if b < 4 else (NB, 5)
                act.wait_ge(S("kv_turned"), b + 1)
                act.activation(kvtok[0:n, b, :], ps[0:n, bank, :], ACT.Copy).then_inc(S("kvtok_copied"), 1)
            with act.Fori(0, NH) as i:
                for b in range(4):
                    act.wait_ge(S("neg_max"), 4 * i + b + 1)
                    l = lg[:, AT[b]:AT[b] + EXT[b]]
                    act.activation(l, l, ACT.Exp, scale=SCALE, bias=anm[:, b:b + 1],
                                   accum_out=asum[:, b:b + 1]).then_inc(S("exp_done"), 1)
                for b, (t0, n) in enumerate(((0, 3), (3, 3), (6, 4))):
                    act.wait_ge(S("p_turned"), OPEN + 4 * i + b + 2)
                    if b == 0:
                        act.wait_ge(S("o_done"), OPEN + i)
                    act.activation(pT[:, t0:t0 + n, :], ps[:, 4 + b, 0:n * P].rearrange("p (a t) -> p a t", t=P),
                                   ACT.Copy).then_inc(S("pT_ready"), 1)
                act.wait_ge(S("o_done"), OPEN + i + 1)
                act.activation(uT[:, bass.ds(i, 1), 0:SEQ].rearrange("p o t -> p (o t)"), ps[:, 7, :],
                               ACT.Copy).then_inc(S("o_read"), 1)


            def tile_in(g, i):
                act.wait_ge(S("dense_done"), 6 * g + N_SSM + i + 1)
                if i < 4:
                    if not isinstance(g, int) or g > 0:
                        act.wait_ge(S("conv_done"), 4 * g - 3 + i)
                        act.wait_ge(S("ctok_done"), g)
                        act.wait_ge(S("dconv_done"), g)
                    act.activation(two(raw[:, i, 3:T + 3]), tile_out(i % 2), ACT.Copy).then_inc(S("dense_read"), 1)
                else:
                    j = i - 4
                    z = ssm_o[:, bass.ds(2 * g + j, 1), :].rearrange("p o (h t) -> p (o h) t", h=2)
                    act.activation(two(thz[:, j, :]), tile_out(j), ACT.Tanh, scale=0.5).then_inc(S("thz_ready"), 1)
                    act.activation(z, tile_out(j), ACT.Copy, scale=0.5).then_inc(S("dense_read"), 1)

            def chunk(g, c):
                act.wait_ge(S("abc_done"), 4 * g + c + 1)
                if c > 1:
                    act.wait_ge(S("y_done"), 4 * g + c - 1)
                elif not isinstance(g, int) or g > 0:
                    act.wait_ge(S("y_done"), 4 * g)
                abc = ps[:, 4, :]
                for r in range(4):
                    act.activation(M2[:, c % 2, r * P:(r + 1) * P], abc[:, r * P:(r + 1) * P], ACT.Relu, scale=-1.0,
                                   bias=atg[:, c, r:r + 1]).then_inc(S("E_relu"), 1)
                act.activation(Cx2[:, c % 2, :], abc, ACT.Exp).then_inc(S("abc_read"), 1)
                act.wait_ge(S("E_relu"), 16 * g + 4 * c + 4)
                act.activation(M2[:, c % 2, :], M2[:, c % 2, :], ACT.Exp, scale=-1.0).then_inc(S("E_ready"), 1)

            def squares(g):
                for j in range(2):
                    act.wait_ge(S("Y_ready"), 2 * g + j + 1)
                    act.activation(sqg[:, j, :], Y[:, j, :], ACT.Square).then_inc(S("sqg_ready"), 1)

            def root(g):
                act.wait_ge(S("sumg_done"), g + 1)
                act.activation(two(rbg), ps[:, 6:8, 0:TH], ACT.Sqrt, scale=1.0 / 256, bias=eps[:, 0:1]).then_inc(S("rootg"), 1)

            def group(g, prev, more):
                for i in range(4):
                    act.wait_ge(S("cw_ready"), 3 * g + 3)
                    act.activation(xc[:, i, 0:SEQ], raw[:, i, 0:SEQ], ACT.Identity, scale=cw[:, 5 * i:5 * i + 1],
                                   bias=cw[:, 5 * i + 4:5 * i + 5]).then_inc(S("tap0"), 1)
                act.wait_ge(S("ctok_done"), g + 1)
                if prev:
                    act.wait_ge(S("ctok_out"), 96 * g)
                act.activation(ctok[0:11, :], ps[0:11, 5, :], ACT.Copy).then_inc(S("ctok_ready"), 1)
                act.wait_ge(S("aux_done"), g + 1)
                act.activation(sct, ps[:, 4, 0:96].rearrange("p (i c) -> p i c", c=24), ACT.Copy).then_inc(S("sct_ready"), 1)
                act.activation(alast.rearrange("p r c -> p (r c)"), ps[:, 4, 384:400], ACT.Copy).then_inc(S("alast"), 1)
                act.activation(ealast.rearrange("p r c -> p (r c)"), ps[:, 4, 384:400], ACT.Exp).then_inc(S("alast"), 1)
                act.activation(dts, ps[:, 4, 96:112].rearrange("p (i c) -> p i c", c=NB), ACT.Copy).then_inc(S("dts_ready"), 1)
                if prev:
                    act.wait_ge(S("sout_out"), 16 * g - 16 + OPEN)
                    act.activation(sout, ps[:, 4, P:3 * P].rearrange("p (j n) -> p j n", n=P), ACT.Copy).then_inc(S("sout_ready"), 1)
                act.activation(dAs, ps[:, 4, 112:128].rearrange("p (i c) -> p i c", c=NB), ACT.Exp).then_inc(S("aux_read"), 1)
                for i in range(4):
                    act.wait_ge(S("conv_done"), 4 * g + i + 1)
                    if i == 0:
                        act.wait_ge(S("dconv_done"), g + 1)
                    if i > 1:
                        act.wait_ge(S("silu_done"), 4 * g + i - 1)
                    act.activation(th[:, i % 2, :], xc[:, i, :], ACT.Tanh).then_inc(S("th_ready"), 1)
                act.wait_ge(S("wdiff"), g + 1)
                act.activation(wexp, wexp, ACT.Exp).then_inc(S("wexp_ready"), 1)
                if prev:
                    root(g - 1)
                if more:
                    tile_in(g + 1, 0)
                    tile_in(g + 1, 1)
                act.wait_ge(S("turned"), g + 1)
                act.activation(Bt, ps[:, 5, :].rearrange("p (c n) -> p c n", n=P), ACT.Copy).then_inc(S("Bt_ready"), 1)
                if more:
                    tile_in(g + 1, 2)
                if more:
                    tile_in(g + 1, 3)
                chunk(g, 0)
                chunk(g, 1)
                if more:
                    tile_in(g + 1, 4)
                chunk(g, 2)
                chunk(g, 3)
                if more:
                    tile_in(g + 1, 5)
                squares(g)

            act.wait_ge(S("o_read"), OPEN + NH)
            for i in range(6):
                tile_in(0, i)
            group(0, False, True)
            with act.Fori(1, NG - 1) as g:
                group(g, True, True)
            group(NG - 1, True, False)
            root(NG - 1)
            act.wait_ge(S("aux_done"), NG + 1)
            act.wait_ge(S("sout_out"), 16 * NG - 16 + OPEN)
            act.activation(sout, ps[:, 4, P:3 * P].rearrange("p (j n) -> p j n", n=P), ACT.Copy).then_inc(S("sout_ready"), 1)

            def gate_tile(n, j, free):
                act.wait_ge(S("dense_done"), n + 1)
                if free:
                    act.wait_ge(S("mixed"), free)
                act.activation(two(gate[:, j, :]), tile_out(j), ACT.Tanh, scale=0.5).then_inc(S("dense_read"), 1)

            def sbr(it):
                for j in range(2):
                    gate_tile(N_SBR + 4 * it + j, j, 2 * it + j - 1 if it else 0)
                for j in range(2):
                    act.wait_ge(S("dense_done"), N_SBR + 4 * it + 3 + j)
                    if it == 0:
                        act.wait_ge(S("ssm_ready"), 2 * NG)
                    act.activation(two(mix[:, 2 * it + j, :]), tile_out(j), ACT.Copy, scale=0.5).then_inc(S("dense_read"), 1)

            act.wait_ge(S("dtop_kept"), 4 * NG + OPEN)
            sbr(0)
            act.wait_ge(S("tensor_mark"), POS_TURNED)
            act.activation(pos, ps[:, 4, 0:16], ACT.Copy).then_inc(S("decode_read"), 1)
            sbr(1)
            for b in range(NB):
                act.wait_ge(S("keys_turned"), b + 1)
                if b >= 2:
                    act.wait_ge(S("dlogits_done"), b - 1)
                act.activation(KTd[:, b % 2, :], ps[:, 4 + b % 2, :], ACT.Copy).then_inc(S("KT_ready"), 1)
            sbr(2)
            act.wait_ge(S("tensor_mark"), LK_TURNED)
            act.activation(lrow[0:64, :], ps[0:64, 7, 0:TOPK + 1], ACT.Copy).then_inc(S("decode_read"), 1)
            act.wait_ge(S("vector_mark"), DMAX_READY)
            act.activation(lrow[0:64, :], lrow[0:64, :], ACT.Exp, scale=SCALE, bias=dmax,
                           accum_out=dsum).then_inc(S("decode_read"), 1)
            sbr(3)
            act.wait_ge(S("tensor_mark"), DP_TURNED)
            act.activation(pTd.rearrange("p o b h -> p (o b h)"), ps[:, 4, 0:128], ACT.Copy).then_inc(S("decode_read"), 1)
            for it in range(4):
                for j in range(2):
                    gate_tile(N_ATT + 4 * it + j, j, 8 + 2 * it + j - 1)
                for j in range(2):
                    act.wait_ge(S("dense_done"), N_ATT + 4 * it + 3 + j)
                    if it:
                        act.wait_ge(S("mixed"), 8 + 2 * it + j - 1)
                    act.activation(two(stage[:, j, :]), tile_out(j), ACT.Copy, scale=0.5).then_inc(S("dense_read"), 1)
            def residual(n0, before):
                for n in range(8):
                    act.wait_ge(S("dense_done"), n0 + n + 1)
                    if n >= 2:
                        act.wait_ge(S("res_added"), before + n - 1)
                    else:
                        act.wait_ge(S("mixed"), 16)
                        if before:
                            act.wait_ge(S("hid_ready"), 2 * OPEN + FT)
                    act.activation(two(stage[:, n % 2, :]), tile_out(n % 2), ACT.Copy).then_inc(S("dense_read"), 1)

            residual(N_OUT, 0)
            rms_act(act, 1, lambda k: xT[:, k, :], sq2, rbc, ready=0)

            def ffn(k, o):
                for j in range(2):
                    act.wait_ge(S("dense_done"), 8 * k + N_FFN + 4 * o + j + 1)
                    act.wait_ge(S("hid_ready"), 2 * OPEN + 4 * k + 2 * o + j - 1)
                    act.activation(two(gate[:, j, :]), tile_out(j), ACT.Tanh, scale=0.5).then_inc(S("gate_read"), 1)
                    act.activation(hid[:, bass.ds(4 * k + 2 * o + j, 1), :].rearrange("p o (h t) -> p (o h) t", h=2),
                                   tile_out(j), ACT.Copy, scale=0.5).then_inc(S("dense_read"), 1)
                for j in range(2):
                    act.wait_ge(S("dense_done"), 8 * k + N_FFN + 4 * o + j + 3)
                    act.activation(two(stage[:, j, :]), tile_out(j), ACT.Copy).then_inc(S("dense_read"), 1)

            with act.Fori(0, 5) as k:
                ffn(k, 0)
                ffn(k, 1)
            ffn(5, 0)
            residual(N_DOWN, KT)
            rms_act(act, 2, lambda k: xT[:, k, :], sq2, rbc, ready=KT)
            for b in range(5):
                n = P if b < 4 else NB
                dst = ytok[:, b, :] if b < 4 else ystok[0:NB, :]
                act.wait_ge(S("y_turned"), b + 1)
                for h in range(2):
                    act.activation(dst[:, h * 512:(h + 1) * 512], ps[0:n, 2 * (b % 2) + h, :], ACT.Copy).then_inc(S("y_ready"), 1)

        @block.vector
        def _(v):
            for name in ("drs_done", "idx_added", "dsc_ready", "top_cut", "logits_read", "dtop_cut", "dtop_kept"):
                v.sem_inc(S(name), OPEN)
            v.sem_inc(S("hid_ready"), 2 * OPEN)
            v.memset(eps[:], EPS).then_inc(S("vector_mark"), 1)
            v.memset(IQ, 0.0).then_inc(S("vector_mark"), 1)
            v.wait_ge(S("pages_in"), 16)
            v.tensor_copy(pgf[0:NB, 0:NPG], idxT[0:NB, 0:NPG]).then_inc(S("vector_mark"), 1)
            v.wait_ge(S("vec_ready"), 1)
            rms_dve(v, 0, lambda k: xT[:, k, :], lambda k: xn[:, k, :], 0, rbc)
            v.wait_ge(S("dense_read"), 2)
            chain = Chain(v, S("dt_steps"))
            chain(v.tensor_scalar(dtT, small[0:32, :], hvec[0:32, 0:1], None, ALU.add))
            v.scalar_tensor_tensor(spa[0:32, :], dtT, -1.0, dtT, ALU.mult, ALU.max).then_inc(S("vector_mark"), 1)
            v.wait_ge(S("dt_exp"), 1)
            chain(v.tensor_scalar(spz[0:32, :], spe[0:32, :], 2.0, None, ALU.add))
            chain(v.reciprocal(spz[0:32, :], spz[0:32, :]))
            chain(v.tensor_tensor(spz[0:32, :], spz[0:32, :], spe[0:32, :], ALU.mult))
            chain(v.tensor_tensor(spw[0:32, :], spz[0:32, :], spz[0:32, :], ALU.mult))
            chain(v.tensor_scalar(spe[0:32, :], spw[0:32, :], 1.0 / 17, None, ALU.mult))
            for i in (15, 13, 11, 9, 7, 5, 3):
                chain(v.scalar_tensor_tensor(spe[0:32, :], spe[0:32, :], 1.0 / i, spw[0:32, :], ALU.add, ALU.mult))
            chain(v.scalar_tensor_tensor(spe[0:32, :], spe[0:32, :], 1.0, spz[0:32, :], ALU.add, ALU.mult))
            chain(v.tensor_scalar(dtT, dtT, 0.0, None, ALU.max))
            chain(v.scalar_tensor_tensor(dtT, spe[0:32, :], 2.0, dtT, ALU.mult, ALU.add))
            v.wait_ge(S("tensor_mark"), IK_MEAN)
            v.tensor_tensor(two(ikt1), two(ik2), ps[:, 4:6, 0:TH], ALU.subtract).then_inc(S("vector_mark"), 1)
            v.wait_ge(S("tensor_mark"), PAGES_TURNED)
            v.tensor_copy(pgf[0:NPG, NPG:NPG + NB], ps[0:NPG, 6, 0:NB]).then_inc(S("vector_mark"), 1)
            v.wait_ge(S("a_exp"), 1)
            chain(v.tensor_scalar(acT[0:32, :], dtT, hvec[0:32, 2:3], -1.0, ALU.mult, ALU.mult))
            for c in range(4):
                v.tensor_tensor_scan(acT[0:32, c * P:(c + 1) * P], ones[0:32, :], acT[0:32, c * P:(c + 1) * P],
                                     0.0, ALU.mult, ALU.add).then_inc(S("a_summed"), 1)
            v.wait_ge(S("tensor_mark"), PAGES_SPREAD)
            v.scalar_tensor_tensor(gidx[:], ps[:, 6, 16:32], 16.0, cst[:, K_P16:K_P16 + 1].broadcast_to((P, 16)),
                                   ALU.mult, ALU.add).then_inc(S("vector_mark"), 1)
            v.wait_ge(S("ik_root"), 1)
            chain(v.reciprocal(ikt2, ikt2))
            chain(v.scalar_tensor_tensor(ikt1, ikt1, ilv[:, 0:1], ikt2, ALU.mult, ALU.mult))
            v.tensor_scalar(ik2, ikt1, ilv[:, 1:2], None, ALU.add).then_inc(S("vector_mark"), 1)
            v.wait_ge(S("iqs_swapped"), 32)
            v.wait_ge(S("vector_mark"), IQ_ZERO)
            for r, h, src in ((0, 0, iqs), (0, 1, iqsw), (1, 0, iqsw), (1, 1, iqs)):
                lo, hi = 64 * r, 64 * r + 64
                v.tensor_copy(IQ[lo:hi, :, 16 * r:16 * r + 16].rearrange("p b (j s) -> p b j s", s=2)[:, :, :, h],
                              src[lo:hi].rearrange("p j b -> p b j")).then_inc(S("IQ_ready"), 1)
            v.scalar_tensor_tensor(wdiag[32:48], small[32:48, SEQ:T].unsqueeze(2).broadcast_to((16, NB, IH)), 1.0 / 32,
                                   ident[32:48, 32:48].unsqueeze(1).broadcast_to((16, NB, IH)),
                                   ALU.mult, ALU.mult).then_inc(S("wdiag_ready"), 1)
            v.wait_ge(S("vector_mark"), IK_READY)
            v.tensor_tensor(iqp, iqs, ik2[:, SEQ:T].unsqueeze(1).broadcast_to((P, 8, NB)),
                            ALU.mult).then_inc(S("wdiag_ready"), 1)
            v.memset(sc, 0.0).then_inc(S("vector_mark"), 1)
            v.wait_ge(S("tok_copied"), 3)
            v.wait_ge(S("vector_mark"), IDX_ZERO)
            with v.Fori(0, 4) as k:
                for j in range(2):
                    for h in range(2):
                        for b in (1, 2, 3):
                            v.wait_ge(S("relu_done"), OPEN + 12 * k + 6 * j + 3 * h + b)
                            v.wait_ge(S("idx_added"), OPEN + 12 * k + 6 * j + 3 * h)
                            acc = sc[:, X0[b]:X0[b] + EXT[b]]
                            v.scalar_tensor_tensor(acc, rl[:, h, X0[b]:X0[b] + EXT[b]],
                                                   tok[:, b, bass.ds(4 * k + 32 + 2 * j + h, 1)], acc,
                                                   ALU.mult, ALU.add).then_inc(S("idx_added"), 1)
            v.wait_ge(S("idx_added"), OPEN + 48)
            for b in (1, 2, 3):
                d = sc[:, X0[b] + b * P:X0[b] + (b + 1) * P]
                v.scalar_tensor_tensor(d, cbias, -LOW / -MASK, d, ALU.mult, ALU.add).then_inc(S("sc_ready"), 1)
            v.wait_ge(S("sc_ready"), 3)
            v.tensor_copy(wk, sc).then_inc(S("vector_mark"), 1)
            v.wait_ge(S("wbc_ready"), 2)
            chain(v.tensor_tensor(drelu[0:NB, :], drelu[0:NB, :], tok[0:NB, 4, 32:48], ALU.mult))
            chain(v.tensor_reduce(smp[0:NB, PAST:PAST + 1], drelu[0:NB, :], AX.X, ALU.add))
            with v.Fori(0, NB) as k:
                for o in range(2):
                    v.wait_ge(S("dec_done"), OPEN + 2 * k + o + 1)
                    v.wait_ge(S("dsc_ready"), OPEN + 2 * k + o)
                    v.scalar_tensor_tensor(drs.rearrange("p (a h) -> p a h", h=IH),
                                           ps[:, 6 + o, 0:P].rearrange("p (a h) -> p a h", h=IH), 0.0,
                                           wbc[:, bass.ds(k, 1), :].broadcast_to((P, 8, IH)),
                                           ALU.max, ALU.mult).then_inc(S("drs_done"), 1)
                    v.wait_ge(S("drs_done"), OPEN + 2 * k + o + 1)
                    v.tensor_reduce(dsc[:, bass.ds(16 * k + 8 * o, 8)], drs.rearrange("p (a h) -> p a h", h=IH),
                                    AX.X, ALU.add).then_inc(S("dsc_ready"), 1)
            v.wait_ge(S("vector_mark"), WK_READY)
            with v.Fori(0, TOPK_P // 8) as k:
                for b in (1, 2, 3):
                    v.wait_ge(S("top_cut"), OPEN + 3 * k)
                    v.sem_inc(S("pad"), 1)
                    v.max(m8[:, b - 1, :], wk[:, X0[b]:X0[b] + EXT[b]]).then_inc(S("top_max"), 1)
                for b in (1, 2, 3):
                    v.wait_ge(S("top_max"), 3 * k + b)
                    v.sem_inc(S("pad"), 1)
                    w_ = wk[:, X0[b]:X0[b] + EXT[b]]
                    v.match_replace(w_, m8[:, b - 1, :], w_, -3.3e38).then_inc(S("top_cut"), 1)
            v.wait_ge(S("top_cut"), OPEN + 3 * TOPK_P // 8)
            chain(v.tensor_tensor(sc, sc, wk, ALU.not_equal))
            v.tensor_scalar(sc, sc, -MASK, MASK, ALU.mult, ALU.add).then_inc(S("vector_mark"), 1)
            v.wait_ge(S("vector_mark"), MASK_READY)
            with v.Fori(0, NH) as i:
                for b in range(4):
                    if b == 0:
                        v.wait_ge(S("p_turned"), OPEN + 4 * i)
                    v.wait_ge(S("logits_done"), OPEN + 4 * i + b + 1)
                    v.sem_inc(S("pad"), 1)
                    mask = cbias if b == 0 else sc[:, X0[b]:X0[b] + EXT[b]]
                    v.tensor_tensor_reduce(lg[:, AT[b]:AT[b] + EXT[b]], ps[:, b, 0:EXT[b]], mask, 1.0, LOW,
                                           ALU.add, ALU.max, amx[:, b:b + 1]).then_inc(S("logits_read"), 1)
                    v.wait_ge(S("logits_read"), OPEN + 4 * i + b + 1)
                    v.tensor_scalar(anm[:, b:b + 1], amx[:, b:b + 1], -SCALE, None, ALU.mult).then_inc(S("neg_max"), 1)
                for b in range(4):
                    v.wait_ge(S("exp_done"), 4 * i + b + 1)
                    v.reciprocal(asum[:, b:b + 1], asum[:, b:b + 1]).then_inc(S("sum_recip"), 1)
                    v.wait_ge(S("sum_recip"), 4 * i + b + 1)
                    l = lg[:, AT[b]:AT[b] + EXT[b]]
                    v.tensor_scalar(l, l, asum[:, b:b + 1], None, ALU.mult).then_inc(S("p_ready"), 1)


            v.wait_ge(S("o_done"), OPEN + NH)
            v.memset(raw[:, :, 0:3], 0.0).then_inc(S("vector_mark"), 1)
            v.wait_ge(S("vector_mark"), RAW_ZERO)
            v.wait_ge(S("cwg_ready"), 12)

            def top(g, *pieces):
                best, row = dm8[0:NB, :], smp[0:NB, :]
                for piece in pieces:
                    r = piece // 3
                    if piece % 3 == 0:
                        v.wait_ge(S("dtop_cut"), 4 * g + r + OPEN)
                        v.sem_inc(S("pad"), 1)
                        v.max(best, row).then_inc(S("dtop_max"), 1)
                    elif piece % 3 == 1:
                        v.wait_ge(S("dtop_max"), 4 * g + r + 1)
                        v.wait_ge(S("dtop_kept"), 4 * g + r + OPEN)
                        v.sem_inc(S("pad"), 1)
                        v.max_index(dix[:], best, row).then_inc(S("dtop_index"), 1)
                    else:
                        v.match_replace(row, best, row, -3.3e38).then_inc(S("dtop_cut"), 1)
                        v.wait_ge(S("dtop_index"), 4 * g + r + 1)
                        v.tensor_copy(sel_idx[0:NB, bass.ds(32 * g + 8 * r, 8)], dix[:]).then_inc(S("dtop_kept"), 1)

            def z_gate(g):
                for j in range(2):
                    v.wait_ge(S("thz_ready"), 2 * g + j + 1)
                    v.wait_ge(S("dense_read"), 6 * g + N_SSM + 5 + j)
                    z = ssm_o[:, bass.ds(2 * g + j, 1), :].rearrange("p o t -> p (o t)")
                    v.scalar_tensor_tensor(z, thz[:, j, :], 1.0, z, ALU.add, ALU.mult).then_inc(S("z_ready"), 1)

            def norm(g):
                v.wait_ge(S("rootg"), g + 1)
                v.reciprocal(rbg, rbg).then_inc(S("recipg"), 1)
                v.wait_ge(S("recipg"), g + 1)
                for j in range(2):
                    v.scalar_tensor_tensor(ssm_o[:, bass.ds(2 * g + j, 1), :].rearrange("p o t -> p (o t)"), Y[:, j, :],
                                           cwg[:, bass.ds(g, 1), 22 + j:23 + j].rearrange("p o t -> p (o t)"), rbg,
                                           ALU.mult, ALU.mult).then_inc(S("ssm_ready"), 1)

            def group(g, prev, more):
                if prev:
                    v.wait_ge(S("abc_read"), 4 * g)
                    v.wait_ge(S("Y_ready"), 2 * g)
                v.tensor_copy(cw, cwg[:, bass.ds(g, 1), :].rearrange("p o t -> p (o t)")).then_inc(S("cw_ready"), 1)
                v.tensor_copy(dtg, tok[:, 0:4, bass.ds(4 * g, 4)]).then_inc(S("cw_ready"), 1)
                v.tensor_copy(atg, actok[:, :, bass.ds(4 * g, 4)]).then_inc(S("cw_ready"), 1)
                v.wait_ge(S("cw_ready"), 3 * g + 3)
                for pair in range(2):
                    for t in range(1, 4):
                        for i in (2 * pair, 2 * pair + 1):
                            v.wait_ge(S("tap%d" % (t - 1)), 4 * g + i + 1)
                            v.scalar_tensor_tensor(xc[:, i, 0:SEQ], raw[:, i, t:t + SEQ], cw[:, 5 * i + t:5 * i + t + 1],
                                                   xc[:, i, 0:SEQ], ALU.mult,
                                                   ALU.add).then_inc(S("tap%d" % t if t < 3 else "conv_done"), 1)
                v.wait_ge(S("alast"), 2 * g + 2)
                v.tensor_tensor(wexp, alast.rearrange("p r c -> p c r"), atg, ALU.subtract).then_inc(S("wdiff"), 1)
                for i in range(4):
                    v.wait_ge(S("th_ready"), 4 * g + i + 1)
                    v.scalar_tensor_tensor(xc[:, i, :], th[:, i % 2, :], 1.0, xc[:, i, :], ALU.add,
                                           ALU.mult).then_inc(S("silu_done"), 1)
                if prev:
                    norm(g - 1)
                v.wait_ge(S("turned"), g + 1)
                for c in range(2):
                    v.tensor_tensor(xdt[:, 2 * c:2 * c + 2, :].rearrange("p c (r q) -> p c r q", q=64),
                                    ps[:, 6 + c, :].rearrange("p (c r q) -> p c r q", r=4, q=64),
                                    dtg[:, 2 * c:2 * c + 2, :].unsqueeze(3).broadcast_to((P, 2, 4, 64)),
                                    ALU.mult).then_inc(S("xdt_ready"), 1)
                v.wait_ge(S("wexp_ready"), g + 1)
                v.wait_ge(S("xdt_ready"), 2 * g + 2)
                v.tensor_tensor(xw.rearrange("p c (r q) -> p (c r) q", q=64), xdt.rearrange("p c (r q) -> p (c r) q", q=64),
                                wexp.rearrange("p c r -> p (c r)").unsqueeze(2).broadcast_to((P, 16, 64)),
                                ALU.mult).then_inc(S("xw_ready"), 1)
                top(g, 0, 1, 2, 3)
                v.wait_ge(S("silu_done"), 4 * g + 4)
                v.wait_ge(S("dts_ready"), g + 1)
                v.tensor_tensor(xdts, xc[:, 0:2, SEQ:T], dts, ALU.mult).then_inc(S("xdts_ready"), 1)
                v.wait_ge(S("xdts_ready"), g + 1)
                v.wait_ge(S("bcast_done"), 2 * g + 1)
                for j in range(2):
                    if j:
                        v.wait_ge(S("state_new"), 2 * g + 1)
                    v.tensor_tensor(t2, ps[:, 6:8, :].rearrange("p k (b n) -> p (k b) n", n=NS),
                                    xdts[:, j, :].unsqueeze(2).broadcast_to((P, NB, NS)),
                                    ALU.mult).then_inc(S("B_used"), 1)
                    v.wait_ge(S("B_used"), 2 * g + j + 1)
                    v.wait_ge(S("st_decayed"), 2 * g + j + 1)
                    v.tensor_tensor(st[:, j], st[:, j], t2, ALU.add).then_inc(S("state_new"), 1)
                v.wait_ge(S("bcast_done"), 2 * g + 2)
                for j in range(2):
                    v.wait_ge(S("state_new"), 2 * g + 2)
                    if j:
                        v.wait_ge(S("ys_ready"), 2 * g + 1)
                    v.tensor_tensor(t2, ps[:, 4:6, :].rearrange("p k (b n) -> p (k b) n", n=NS), st[:, j],
                                    ALU.mult).then_inc(S("C_used"), 1)
                    v.wait_ge(S("C_used"), 2 * g + j + 1)
                    v.tensor_reduce(ys[:, j, :], t2, AX.X, ALU.add).then_inc(S("ys_ready"), 1)
                v.wait_ge(S("cb_done"), g + 1)
                v.tensor_tensor(CBm, ps[:, 5, :].rearrange("p (c l) -> p c l", l=P),
                                tri.unsqueeze(1).broadcast_to((P, 4, P)), ALU.mult).then_inc(S("CBm_ready"), 1)
                top(g, 4, 5, 6, 7, 8)
                for c in range(4):
                    if c == 3 and more:
                        z_gate(g + 1)
                    v.wait_ge(S("y_done"), 4 * g + c + 1)
                    inc = ps[:, 5, 256 * (c % 2):256 * (c % 2) + 256]
                    if c == 0:
                        v.tensor_copy(hT, inc).then_inc(S("h_done"), 1)
                    else:
                        v.tensor_tensor(hT.rearrange("p (r q) -> p r q", q=64), hT.rearrange("p (r q) -> p r q", q=64),
                                        ealast[:, :, c:c + 1].broadcast_to((P, 4, 64)), ALU.mult).then_inc(S("h_decayed"), 1)
                        v.wait_ge(S("h_decayed"), 3 * g + c)
                        v.tensor_tensor(hT, hT, inc, ALU.add).then_inc(S("h_done"), 1)
                    if c == 0:
                        top(g, 9, 10)
                    if c == 1:
                        top(g, 11)
                for j in range(2):
                    v.scalar_tensor_tensor(Y[:, j, 0:SEQ], xc[:, j, 0:SEQ], cw[:, 20 + j:21 + j], ps[:, 6 + j, :],
                                           ALU.mult, ALU.add).then_inc(S("Y_sum"), 1)
                    v.wait_ge(S("ys_ready"), 2 * g + j + 1)
                    v.scalar_tensor_tensor(Y[:, j, SEQ:T], xc[:, j, SEQ:T], cw[:, 20 + j:21 + j], ys[:, j, :],
                                           ALU.mult, ALU.add).then_inc(S("Y_sum"), 1)
                for j in range(2):
                    v.wait_ge(S("Y_sum"), 4 * g + 2 * j + 2)
                    v.wait_ge(S("z_ready"), 2 * g + j + 1)
                    v.tensor_tensor(Y[:, j, :], Y[:, j, :], ssm_o[:, bass.ds(2 * g + j, 1), :].rearrange("p o t -> p (o t)"),
                                    ALU.mult).then_inc(S("Y_ready"), 1)

            z_gate(0)
            group(0, False, True)
            with v.Fori(1, NG - 1) as g:
                group(g, True, True)
            group(NG - 1, True, False)
            norm(NG - 1)

            def gated(it):
                for j in range(2):
                    v.wait_ge(S("dense_read"), N_SBR + 4 * it + 3 + j)
                    m = mix[:, 2 * it + j, :]
                    v.scalar_tensor_tensor(m, gate[:, j, :], 1.0, m, ALU.add, ALU.mult).then_inc(S("mixed"), 1)

            
            v.wait_ge(S("pgb_in"), 16)
            v.wait_ge(S("dtop_kept"), 4 * NG + OPEN)
            chain(v.tensor_scalar(pgb.rearrange("p b j -> p (b j)"), pgb32[:], float(PAGE), None, ALU.mult))
            v.tensor_copy(dpg[:, :, 0:1], pgb[:, :, 0:1]).then_inc(S("dpg_ready"), 1)
            v.scalar_tensor_tensor(dpg[:, :, 1:NPG], pgb[:, :, 1:NPG], -float(PAGE), pgb[:, :, 0:NPG - 1], ALU.add,
                                   ALU.subtract).then_inc(S("dpg_ready"), 1)
            v.wait_ge(S("aux_done"), NG + 1)
            v.tensor_tensor(qk_new.rearrange("p b (g h) -> p g h b", g=2),
                            qkvs[:, 0:8, :].rearrange("p (g h) b -> p g h b", g=2),
                            qkvs[:, 8:10, :].unsqueeze(2).broadcast_to((P, 2, 4, NB)), ALU.mult).then_inc(S("vector_mark"), 1)
            gated(0)
            v.wait_ge(S("decode_read"), POS_READ)
            v.wait_ge(S("dpg_ready"), 2)
            chain(v.tensor_scalar(posc, pos, float(PAST - 1), None, ALU.min))
            v.tensor_scalar(gone, pos, PAST - 0.5, MASK, ALU.is_gt, ALU.mult).then_inc(S("gone_ready"), 1)
            chain(v.tensor_tensor(hit, posc.unsqueeze(2).broadcast_to((P, 16, 16)),
                                  cst[:, K_J:K_J + NPG].unsqueeze(1).broadcast_to((P, 16, 16)), ALU.is_ge))
            hit4 = hit.rearrange("p (o b) j -> p o b j", o=2)
            chain(v.tensor_tensor(hit4, hit4, dpg.unsqueeze(1).broadcast_to((P, 2, NB, NPG)), ALU.mult))
            chain(v.tensor_reduce(pos, hit, AX.X, ALU.add))
            v.tensor_tensor(gidx[:], pos, posc, ALU.add).then_inc(S("vector_mark"), 1)
            gated(1)
            v.wait_ge(S("dlogits_done"), NB)
            v.wait_ge(S("gone_ready"), 1)
            v.tensor_tensor(lk.rearrange("p o b h -> p (o b) h"), ps[:, 6, 0:128].rearrange("p (a h) -> p a h", h=NH),
                            gone.unsqueeze(2).broadcast_to((P, 16, NH)), ALU.add).then_inc(S("vector_mark"), 1)
            gated(2)
            v.wait_ge(S("decode_read"), LROW_READY)
            chain(v.tensor_reduce(dmin, lrow[0:64, 0:TOPK], AX.X, ALU.min))
            chain(v.tensor_scalar(dmin, dmin, MASK / 2, MASK, ALU.is_gt, ALU.mult))
            chain(v.tensor_tensor(lrow[0:64, TOPK:TOPK + 1], lrow[0:64, TOPK:TOPK + 1], dmin, ALU.add))
            chain(v.tensor_reduce(dmax, lrow[0:64, :], AX.X, ALU.max))
            v.tensor_scalar(dmax, dmax, -SCALE, None, ALU.mult).then_inc(S("vector_mark"), 1)
            v.wait_ge(S("decode_read"), DEXP_DONE)
            chain(v.reciprocal(dsum, dsum))
            v.tensor_scalar(lrow[0:64, :], lrow[0:64, :], dsum, None, ALU.mult).then_inc(S("vector_mark"), 1)
            gated(3)
            v.wait_ge(S("tensor_mark"), DP_TURNED)
            v.wait_ge(S("decode_read"), PTD_READY)
            chain(v.tensor_tensor(pv_new.rearrange("p b (g h) -> p g h b", g=2),
                                  ps[:, 4, 128:192].rearrange("p (b g h) -> p g h b", g=2, h=4),
                                  qkvs[:, 10:12, :].unsqueeze(2).broadcast_to((P, 2, 4, NB)), ALU.mult))
            v.wait_ge(S("tensor_mark"), DVALUES_DONE)
            v.tensor_tensor(uT[:, :, SEQ:T].rearrange("p h b -> p b h"), ps[:, 5, 0:64].rearrange("p (b h) -> p b h", h=NH),
                            pv_new, ALU.add).then_inc(S("vector_mark"), 1)
            for it in range(4):
                for j in range(2):
                    v.wait_ge(S("dense_read"), N_ATT + 4 * it + 3 + j)
                    v.scalar_tensor_tensor(stage[:, j, :], gate[:, j, :], 1.0, stage[:, j, :], ALU.add,
                                           ALU.mult).then_inc(S("att_gated"), 1)
                    v.wait_ge(S("att_gated"), 2 * it + j + 1)
                    m = mix[:, 2 * it + j, :]
                    v.tensor_tensor(m, m, stage[:, j, :], ALU.add).then_inc(S("mixed"), 1)

            def residual(n0):
                for n in range(8):
                    v.wait_ge(S("dense_read"), n0 + n + 1)
                    v.tensor_tensor(xT[:, n, :], xT[:, n, :], stage[:, n % 2, :], ALU.add).then_inc(S("res_added"), 1)

            residual(N_OUT)
            rms_dve(v, 1, lambda k: xT[:, k, :], lambda k: xn[:, k, :], 8, rbc)

            def ffn(k, o):
                hs = [hid[:, bass.ds(4 * k + 2 * o + j, 1), :].rearrange("p o t -> p (o t)") for j in range(2)]
                for j in range(2):
                    v.wait_ge(S("dense_read"), 8 * k + N_FFN + 4 * o + j + 1)
                    v.wait_ge(S("gate_read"), 4 * k + 2 * o + j + 1)
                    v.scalar_tensor_tensor(hs[j], gate[:, j, :], 1.0, hs[j], ALU.add, ALU.mult).then_inc(S("silu_h"), 1)
                for j in range(2):
                    v.wait_ge(S("silu_h"), 4 * k + 2 * o + j + 1)
                    v.wait_ge(S("dense_read"), 8 * k + N_FFN + 4 * o + j + 3)
                    v.tensor_tensor(hs[j], hs[j], stage[:, j, :], ALU.mult).then_inc(S("hid_ready"), 1)

            with v.Fori(0, 5) as k:
                ffn(k, 0)
                ffn(k, 1)
            ffn(5, 0)
            residual(N_DOWN)
            rms_dve(v, 2, lambda k: xT[:, k, :], lambda k: xn[:, k, :], 16, rbc)

        @block.gpsimd
        def _(g):
            g.wait_ge(S("vec_ready"), 1)
            g.wait_ge(S("taps_ready"), 1)
            g.wait_ge(S("dsk_ready"), 1)
            tp = taps.rearrange("p (t n) -> p n t", t=4)
            cb = vec[:, 40:72]
            for i, sl in enumerate((slice(0, 16, 2), slice(1, 16, 2), slice(16, 24), slice(24, 32))):
                g.tensor_copy(cwg[:, :, 5 * i:5 * i + 4], tp[:, sl, :]).then_inc(S("cwg_ready"), 1)
                g.tensor_scalar(cwg[:, :, 5 * i + 4], cb[:, sl], 0.5, None, ALU.mult).then_inc(S("cwg_ready"), 1)
            for j in range(2):
                g.tensor_copy(cwg[:, :, 20 + j], dsk[:, j:16:2]).then_inc(S("cwg_ready"), 1)
                g.tensor_copy(cwg[:, :, 22 + j], vec[:, 24 + j:40:2]).then_inc(S("cwg_ready"), 1)

            g.wait_ge(S("vector_mark"), GIDX_READY)
            rows = cache_idx_k[0].rearrange("n (s k) d -> (n s) (k d)", k=8)

            def gather(b, o):
                g.indirect_dma_start(gat[:, o, :], None, rows,
                                     bass.IndirectOffsetOnAxis(gidx[:, o * NB + b:o * NB + b + 1], 0)
                                     ).then_inc(S("gathered%d" % o), 16)

            gather(0, 0)
            gather(0, 1)
            g.wait_ge(S("dense_read"), N_QKV)
            g.wait_ge(S("vector_mark"), IK_READY)
            with g.Fori(0, 4) as k:
                for j in range(2):
                    g.wait_ge(S("idx_done"), OPEN + 12 * k)
                    g.tensor_copy(iqslot[j], kviq[:, bass.ds(2 * k + 4 + j, 1), :].rearrange("p o t -> p (o t)")).then_inc(S("iq_in_slot"), 1)
            for b in range(1, NB):
                for o in range(2):
                    g.wait_ge(S("gat_turned"), 2 * b - 1 + o)
                    gather(b, o)

            with g.Fori(0, NH) as i:
                g.wait_ge(S("logits_done"), OPEN + 4 * i)
                g.wait_ge(S("dense_read"), N_SSM)
                g.tensor_copy(qslot, uT[:, bass.ds(i, 1), :].rearrange("p o t -> p (o t)")).then_inc(S("q_in_slot"), 1)

            def group(i):
                w4 = cw[:, 0:20].rearrange("p (i t) -> p i t", t=5)
                old = sct.rearrange("p i (b t) -> p i b t", t=3)
                g.wait_ge(S("sct_ready"), i + 1)
                g.wait_ge(S("cw_ready"), 3 * i + 3)
                g.wait_ge(S("dense_read"), 6 * i + N_SSM + 4)
                for t, o in enumerate((sc0, sc1, sc2)):
                    g.tensor_tensor(o, old[:, :, :, t], w4[:, :, t:t + 1].broadcast_to((P, 4, NB)),
                                    ALU.mult).then_inc(S("dconv_steps"), 1)
                g.tensor_tensor(sc3, raw[:, :, SEQ + 3:T + 3], w4[:, :, 3:4].broadcast_to((P, 4, NB)),
                                ALU.mult).then_inc(S("dconv_steps"), 1)
                g.wait_ge(S("dconv_steps"), 7 * i + 4)
                g.tensor_tensor(sc0, sc0, sc1, ALU.add).then_inc(S("dconv_steps"), 1)
                g.tensor_tensor(sc2, sc2, sc3, ALU.add).then_inc(S("dconv_steps"), 1)
                g.wait_ge(S("dconv_steps"), 7 * i + 6)
                g.tensor_tensor(sc0, sc0, sc2, ALU.add).then_inc(S("dconv_steps"), 1)
                g.wait_ge(S("dconv_steps"), 7 * i + 7)
                g.tensor_tensor(xc[:, :, SEQ:T], sc0, w4[:, :, 4:5].broadcast_to((P, 4, NB)), ALU.add).then_inc(S("dconv_done"), 1)
                g.wait_ge(S("aux_read"), i + 1)
                g.wait_ge(S("state_in"), 32 * i + 32)
                for j in range(2):
                    g.tensor_tensor(st[:, j], st[:, j], dAs[:, j, :].unsqueeze(2).broadcast_to((P, NB, NS)),
                                    ALU.mult).then_inc(S("st_decayed"), 1)
                for c in range(4):
                    g.wait_ge(S("CBm_ready"), i + 1)
                    g.wait_ge(S("E_ready"), 4 * i + c + 1)
                    m = M2[:, c % 2, :].rearrange("p (r l) -> p r l", l=P)
                    g.tensor_tensor(m, m, CBm[:, c:c + 1, :].broadcast_to((P, 4, P)), ALU.mult).then_inc(S("M_ready"), 1)
                    if c:
                        x = Cx2[:, c % 2, :].rearrange("p (r l) -> p r l", l=P)
                        g.tensor_tensor(x, x, xc[:, 3:4, c * P:(c + 1) * P].broadcast_to((P, 4, P)),
                                        ALU.mult).then_inc(S("M_ready"), 1)

            with g.Fori(0, NG) as i:
                group(i)
            g.wait_ge(S("vector_mark"), ROWS_READY)
            g.wait_ge(S("ssm_ready"), 2 * NG)
            g.wait_ge(S("state_out"), 32 * NG)
            rows_k = cache_k[0].rearrange("n s g d -> (n s) (g d)")
            rows_v = cache_v[0].rearrange("n s g d -> (n s) (g d)")
            for kind, rows in enumerate((rows_k, rows_v)):
                for b in range(NB):
                    for o in range(2):
                        c = NB * o + b
                        g.indirect_dma_start(KV[:, kind, c, :], None, rows,
                                             bass.IndirectOffsetOnAxis(gidx[:, c:c + 1], 0)
                                             ).then_inc(S("values_in" if kind else "keys_in"), 16)


_INS = ["x_prompt", "x_sample", "cache_k", "cache_v", "cache_idx_k", "state_ssm", "state_conv", "page_table",
        "norm1_w", "w_in", "idx_ln_w", "idx_ln_b", "conv_w", "conv_b", "dt_bias", "a_log", "d_skip",
        "ssm_norm_w", "w_attn_br", "w_ssm_br", "w_out", "norm2_w", "w_ffn_gate", "w_ffn_up", "w_ffn_down",
        "normf_w"]
_OUTS = [(1, 512, 1024), (8, 1, 1024), (1, 1, 512, 2, 128), (1, 1, 512, 2, 128), (1, 1, 512, 64),
         (1, 1, 32, 64, 128), (1, 1, 3, 4096), (1, 8, 1, 2, 128), (1, 8, 1, 2, 128), (1, 8, 1, 64),
         (1, 8, 32, 64, 128), (1, 8, 3, 4096)]


def _constants():
    import numpy as np

    p, q = np.arange(P)[:, None], np.arange(P)[None, :]
    c = np.zeros((P, NK), np.float32)
    c[:, K_ID:K_ID + P] = p == q
    c[:, K_ONE:K_ONE + P] = 1.0
    c[:, K_BLK:K_BLK + P] = (p // ID == q // ID) / float(ID)
    c[:, K_TRI:K_TRI + P] = p <= q
    c[:, K_CB:K_CB + P] = np.where(q <= p, 0.0, MASK)
    c[:, K_P16] = np.arange(P) % 16
    for o in range(2):
        c[0:NPG, K_PG + o * P:K_PG + (o + 1) * P] = np.arange(NPG)[:, None] == o * 8 + q // 16
    c[0:2, K_HALF:K_HALF + P] = p[0:2] == q // ID
    c[:, K_PAR] = np.arange(P) < ID
    c[:, K_PAR + 1] = np.arange(P) >= ID
    c[:, K_J:K_J + NPG] = np.arange(NPG) * PAGE
    g = np.zeros((NG, 32, GSEL), np.float32)
    h = np.arange(32)[:, None]
    for i in range(NG):
        for r in range(4):
            g[i, :, r * P:(r + 1) * P] = h == 4 * i + r
        for j in range(2):
            g[i, :, 512 + j * P:512 + (j + 1) * P] = h == 4 * i + 2 * j + q // ID
    return c, g


def kernel(**inputs):
    import concourse.bacc as _bacc
    import numpy as _np
    from concourse.bass_utils import run_bass_kernel_spmd as _run

    nc = _bacc.Bacc("TRN2", target_bir_lowering=False, num_devices=1)
    arrays, args = {}, []
    for name in _INS:
        a = _np.ascontiguousarray(inputs[name])
        arrays[f"in_{name}"] = a
        args.append(nc.dram_tensor(f"in_{name}", a.shape, mybir.dt.from_np(a.dtype), kind="ExternalInput").ap())
    for name, a in zip(("constants", "head_selectors"), _constants()):
        arrays[f"in_{name}"] = a
        args.append(nc.dram_tensor(f"in_{name}", a.shape, F32, kind="ExternalInput").ap())
    for i, shape in enumerate(_OUTS):
        args.append(nc.dram_tensor(f"out_{i}", shape, F32, kind="ExternalOutput").ap())
    build(nc, *args)
    r = _run(nc, [arrays], core_ids=[0])
    return tuple(r.results[0][f"out_{i}"] for i in range(len(_OUTS)))
```

```python
from contextlib import ExitStack

import concourse.bass as bass
from concourse import mybir
from concourse.alu_op_type import AluOpType as ALU

ACT = mybir.ActivationFunctionType
AX = mybir.AxisListType
F32 = mybir.dt.float32
I32 = mybir.dt.int32
U32 = mybir.dt.uint32

P = 128
D = 1024
SEQ = 512
NB = 8
T = SEQ + NB
TH = T // 2
KT = D // P
NH = 8
IH = 16
ID = 64
PAST = 2048
PAGE = 128
NPG = PAST // PAGE
NG = 8
NS = 128
DI = 2048
DFF = 2816
FT = DFF // P
TOPK = 256
TOPK_P = 128
EPS = 1e-6
LOW = -3.0e38
MASK = -1.0e30
OPEN = 1
HEAD, TILE = 4, 7
C_IQ, C_IK, C_IW = 1536, 2560, 2624
C_Z, C_X, C_B, C_C = 2640, 4688, 6736, 7760
C_DT, C_GA, C_GM = 8784, 8816, 9840
SLOT = KT * 2 * P
NSLOT = 6
SCALE = P ** -0.5

K_ID, K_ONE, K_BLK, K_TRI, K_CB, K_P16, K_PG, K_HALF, K_PAR, K_J = 0, 128, 256, 384, 512, 640, 641, 897, 1025, 1027
NK = 1043
GSEL = 768


class Chain:

    def __init__(self, engine, sem, base=0):
        self.engine, self.sem, self.base, self.n = engine, sem, base, 0

    def __call__(self, ins):
        self.n += 1
        ins.then_inc(self.sem, 1)
        self.engine.wait_ge(self.sem, self.base + self.n)


def build(nc, x_prompt, x_sample, cache_k, cache_v, cache_idx_k, state_ssm, state_conv, page_table,
          norm1_w, w_in, idx_ln_w, idx_ln_b, conv_w, conv_b, dt_bias, a_log, d_skip, ssm_norm_w,
          w_attn_br, w_ssm_br, w_out, norm2_w, w_ffn_gate, w_ffn_up, w_ffn_down, normf_w,
          consts, gsel_d,
          y_prompt, y_sample, k_prompt, v_prompt, ik_prompt, ssm_prompt, conv_prompt,
          k_sample, v_sample, ik_sample, ssm_sample, conv_sample):
    with ExitStack() as ctx:
        def sb(name, shape, dt=F32):
            return ctx.enter_context(nc.sbuf_tensor(name, shape, dt))

        sems = {}

        def S(name):
            if name not in sems:
                sems[name] = ctx.enter_context(nc.semaphore(name))
            return sems[name]

        xT = sb("xT", [P, KT, T])
        xn = sb("xn", [P, KT, T])
        uT = sb("uT", [P, 8, T])
        work = sb("work", [P, 16384])
        ssm_o = sb("ssm_o", [P, 16, T])
        ring = sb("ring", [P, NSLOT, KT, 2 * P])
        cst = sb("cst", [P, NK])
        gs = sb("gs", [32, GSEL])
        vec = sb("vec", [P, 96])
        cwg = sb("cwg", [P, NG, 24])
        eps = sb("eps", [P, 1])
        ps = ctx.enter_context(nc.psum_tensor("ps", [P, 8, 512], F32))
        ident, ones = cst[:, K_ID:K_ID + P], cst[:, K_ONE:K_ONE + P]
        blk64, tri, cbias = cst[:, K_BLK:K_BLK + P], cst[:, K_TRI:K_TRI + P], cst[:, K_CB:K_CB + P]

        def W(off, *shape):
            n = 1
            for s in shape:
                n *= s
            v = work[:, off:off + n]
            if len(shape) == 2:
                v = v.rearrange("p (a b) -> p a b", b=shape[1])
            if len(shape) == 3:
                v = v.rearrange("p (a b c) -> p a b c", b=shape[1], c=shape[2])
            return v, off + n

        ssm_flat = ssm_o[:].rearrange("p a b -> p (a b)")

        def O(off, *shape):
            n = 1
            for s in shape:
                n *= s
            v = ssm_flat[:, off:off + n]
            if len(shape) == 2:
                v = v.rearrange("p (a b) -> p a b", b=shape[1])
            if len(shape) == 3:
                v = v.rearrange("p (a b c) -> p a b c", b=shape[1], c=shape[2])
            return v, off + n

        kviq, at = W(0, 12, T)
        keep = 16384 - 4096
        smp, k1 = W(keep, PAST + 1)
        sel_idx, k1 = W(k1, TOPK)
        small, k1 = W(k1, T)
        dtT = small[0:32, :]
        acT, k1 = W(k1, T)
        tok, k1 = W(k1, 5, 48)
        actok, k1 = W(k1, 4, 32)
        qkvs, k1 = W(k1, 12, NB)
        dsk, k1 = W(k1, 16)
        hvec, k1 = W(k1, 8)
        ilv, k1 = W(k1, 8)
        vload, k1 = W(k1, P)
        assert k1 <= 16384, k1
        ik2, at = W(at, T)
        ikt1, at = W(at, T)
        ikt2, at = W(at, T)
        ikt3, at = W(at, T)
        iqs, at = W(at, 8, NB)
        iqsw, at = W(at, 8, NB)
        IQ, at = W(at, NB, 32)
        wdiag, at = W(at, NB, IH)
        wbc, at = W(at, NB, IH)
        tapload, at = W(at, P)
        dskload, at = W(at, 16)
        taps, at = W(at, P)
        pgf, at = W(at, 24)
        drelu, at = W(at, 16)
        iqp, at = W(at, 8, NB)
        gat, at = W(at, 2, 512)
        gatT, at = W(at, 512)
        drs, at = W(at, P)
        dsc, at = W(at, NB * 2 * 8)
        assert at <= keep, at
        gatT = [gatT, O(7488, 512)[0]]
        xtok, o1 = O(0, 4, D)
        xstok, o1 = O(o1, D)
        sq2, o1 = O(o1, 2, T)
        rbc, o1 = O(o1, T)
        spz, o1 = O(o1, T)
        spw, o1 = O(o1, T)
        sqx = [W(0, KT, P)[0], W(D, KT, P)[0]]
        sqxs = W(2 * D, KT, NB)[0]
        spa, spe = sq2[:, 0, :], sq2[:, 1, :]
        sqsum = spz
        kvtok, o2 = O(0, 5, 512)
        iktok, o2 = O(o2, 5, ID)
        X0 = [None, 0, 256, 640]
        EXT = [P, 256, 384, 512]
        sc, o2 = O(o2, 1152)
        wk, o2 = O(o2, 1152)
        rl, _ = O(o2, 2, 1152)
        AT = [0, P, 384, 768]
        lg, _ = O(o2, 1280)
        pT, _ = O(o2 + 1280, 10, P)
        qslot = ikt1
        PB = [(4, 0), (4, 128), (4, 256), (5, 0), (5, 128), (5, 256), (6, 0), (6, 128), (6, 256), (6, 384)]
        amx = sb("amx", [P, 4])
        anm = sb("anm", [P, 4])
        asum = sb("asum", [P, 4])
        rt = sb("rt", [P, 5])
        idxT = sb("idxT", [P, 24], I32)
        gidx = sb("gidx", [P, 16], U32)
        m8 = sb("m8", [P, 3, 8])
        scratch = nc.dram_tensor("decode_scores", (NB, PAST), F32, kind="Internal").ap()
        iqslot = [ikt3, ikt1]

        ring_flat = ring[:].rearrange("p s k c -> p (s k c)")[:, 3 * SLOT:]

        def R(off, *shape):
            n = 1
            for d in shape:
                n *= d
            v = ring_flat[:, off:off + n]
            if len(shape) == 2:
                v = v.rearrange("p (a b) -> p a b", b=shape[1])
            if len(shape) == 3:
                v = v.rearrange("p (a b c) -> p a b c", b=shape[1], c=shape[2])
            return v, off + n

        raw, sa = W(0, 4, T + 3)
        xc, sa = W(sa, 4, T)
        st, sa = W(sa, 2, NB, NS)
        Y, sa = W(sa, 2, T)
        th, sa = W(sa, 2, T)
        thz, sa = W(sa, 2, T)
        sqg, sa = W(sa, 2, T)
        rbg, sa = W(sa, T)
        hT, sa = W(sa, 256)
        t2, ra = R(0, NB, NS)
        M2, ra = R(ra, 2, 512)
        Cx2, ra = R(ra, 2, 512)
        CBm, ra = R(ra, 4, P)
        Bt, ra = R(ra, 4, P)
        xw, ra = R(ra, 4, 256)
        sout, ra = R(ra, 2, P)
        assert ra <= 3 * SLOT, ra
        xdt = sb("xdt", [P, 4, 256])
        scl, ra = R(ra, 512)
        scl = scl[0:24, :]
        smallg, sa = W(sa, 512)
        ctok, sa = W(sa, 512)
        assert sa <= keep and ra <= 3 * SLOT, (sa, ra)
        so = 0

        def G(*shape):
            nonlocal so
            n = 1
            for d in shape:
                n *= d
            v = smallg[:, so:so + n]
            so += n
            if len(shape) == 2:
                v = v.rearrange("p (a b) -> p a b", b=shape[1])
            if len(shape) == 3:
                v = v.rearrange("p (a b c) -> p a b c", b=shape[1], c=shape[2])
            return v

        cw = G(24)
        dtg, atg = G(4, 4), G(4, 4)
        sct = G(4, 24)
        sc0, sc1, sc2, sc3 = G(4, NB), G(4, NB), G(4, NB), G(4, NB)
        dts, dAs, xdts, ys = G(2, NB), G(2, NB), G(2, NB), G(2, NB)
        alast, ealast = G(4, 4), G(4, 4)
        wexp = G(4, 4)
        dm8 = G(8)
        dix = sb("dix", [NB, 8], U32)
        pgb32 = sb("pgb32", [P, P], I32)

        mix, da = W(0, KT, T)
        hid, _ = W(0, FT, T)
        KV, da = W(da, 2, 16, 256)
        stage, _ = W(da, 2, T)
        KTd, da = W(da, 2, 512)
        da += 2 * T - 1024
        hit, da = W(da, 16, 16)
        pgb, da = W(da, NB, NPG)
        dpg, da = W(da, NB, NPG)
        pos, da = W(da, 16)
        posc, da = W(da, 16)
        gone, da = W(da, 16)
        lk, da = W(da, 2, NB, NH)
        lrow, da = W(da, TOPK + 1)
        assert da <= keep + PAST + 1, da
        gate, _ = W(keep + PAST + 1 + TOPK, 2, T)
        xdt_flat = xdt[:].rearrange("p c q -> p (c q)")
        qk_new = xdt_flat[:, 0:64].rearrange("p (b h) -> p b h", h=NH)
        pTd = xdt_flat[:, 64:192].rearrange("p (o b h) -> p o b h", o=2, h=NH)
        pv_new = xdt_flat[:, 192:256].rearrange("p (b h) -> p b h", h=NH)
        dmin, dmax, dsum = xdt_flat[0:64, 256:257], xdt_flat[0:64, 257:258], xdt_flat[0:64, 258:259]
        ytok, ystok = xtok, xstok
        raw_flat = raw.rearrange("p i t -> p (i t)")
        gates_ahead = [raw_flat[:, 2 * T:3 * T], raw_flat[:, 3 * T:4 * T], thz[:, 0, :], thz[:, 1, :],
                       gate[:, 0, :], gate[:, 1, :]]
        SBR_SLOTS = [(0, 1), (3, 4), (0, 1), (3, 4)]
        GM_SLOTS = [0, 1, 2, 5]
        ATT_SLOTS = [(5, 0), (1, 2), (3, 4), (5, 0)]
        OUT_SLOTS = [1, 2, 3, 4]
        FFN_SLOTS = [(5, 0), (1, 2)]
        DOWN_SLOTS = [(3, 4, 1), (2, 5, 0)]

        N_IQ, N_QKV, N_SSM, N_SBR = 2, 10, 22, 70
        N_ATT, N_OUT, N_FFN, N_DOWN, N_END = 86, 102, 110, 154, 162
        SBR_TILES = [N_SBR + 6, N_SBR + 8, N_SBR + 10, N_SBR + 14]
        F_SSM = [2, 2, 0, 2, 2, 2]
        F_SBR = [10, 2, 8, 2, 2, 2]
        F_ATT = [13, 5, 9, 4, 4, 3]
        F_OUT = [15, 6, 10, 5, 5, 5]
        F_FFN = [15, 7, 11, 6, 6, 5]
        F_DOWN = [21, 12, 16, 6, 6, 11]
        VECS_TURNED, IK_MEAN, PAGES_TURNED, IK_VAR, PAGES_SPREAD, TOK_TURNED = 1, 2, 3, 4, 5, 6
        WBC_DONE, IK_TURNED, POS_TURNED, LK_TURNED, DP_TURNED, DVALUES_DONE = 7, 8, 9, 10, 11, 12
        EPS_SET, IQ_ZERO, PAGES_F, DT_ABS, IK_SQ_IN, PAGEST = 1, 2, 3, 4, 5, 6
        GIDX_READY, IK_READY, IDX_ZERO, WK_READY, MASK_READY, RAW_ZERO = 7, 8, 9, 10, 11, 12
        QK_NEW_READY, ROWS_READY, LK_READY, DMAX_READY, DP_READY, DO_READY = 13, 14, 15, 16, 17, 18
        POS_READ, LROW_READY, DEXP_DONE, PTD_READY = 1, 2, 3, 4
        w_in_slot = [S(f"weights_in_slot{i}") for i in range(NSLOT)]

        def w_block(w, c0, n=2 * P, k0=0, kt=KT):
            return w[0, k0:k0 + kt * P].rearrange("(k p) c -> p k c", p=P)[:, :, bass.ds(c0, n)]

        def load(sp, slot, src, freed=None, col=0):
            if freed is not None:
                sp.wait_ge(S("dense_done"), freed)
            kt, n = src.shape[1], src.shape[2]
            sp.dma_start(ring[:, slot, 0:kt, col:col + n], src).then_inc(w_in_slot[slot], 16)

        def dense(pe, n, pair, lhs, rhs, m=P, k0=0, k1=None, ready=None):
            if k0 == 0 and (not isinstance(n, int) or n >= 2):
                pe.wait_ge(S("dense_read"), n - 1)
            for k in range(k0, k1 or len(lhs)):
                if ready:
                    pe.wait_ge(S(ready[0]), ready[1] + k + 1)
                for h in range(2):
                    mm = pe.matmul(ps[0:m, 2 * pair + h, 0:TH], lhs[k], rhs[k][:, h * TH:(h + 1) * TH],
                                   start=(k == 0), stop=(k == len(lhs) - 1))
            if k == len(lhs) - 1:
                mm.then_inc(S("dense_done"), 1)

        def tile_out(pair, m=P):
            return ps[0:m, 2 * pair:2 * pair + 2, 0:TH]

        def two(ap):
            return ap.rearrange("p (h t) -> p h t", h=2)

        xns = [xn[:, k, :] for k in range(KT)]

        def block_of(slot, j, kt=KT):
            return [ring[:, slot, k, j * P:(j + 1) * P] for k in range(kt)]

        NORM2, NORMF = NG + 1, NG + 2

        def sum_squares(pe, e, *squares):
            for b in range(5):
                n = P if b < 4 else NB
                for i, sq in enumerate(squares):
                    mm = pe.matmul(ps[0:n, 6, b:b + 1], sq[:, b * P:b * P + n], ones[:, 0:1],
                                   start=(i == 0), stop=(i == len(squares) - 1))
            mm.then_inc(S("norm_summed"), 1)

        def spread_norm(pe, e):
            pe.wait_ge(S("norm_recip"), 2 * e + 2)
            for b in range(4):
                pe.matmul(ps[:, 7, b * P:(b + 1) * P], rt[:, b:b + 1].broadcast_to((P, P)), ident, start=True, stop=True)
            pe.matmul(ps[:, 6, 8:8 + NB], rt[0:NB, 4:5].broadcast_to((NB, P)), ident[0:NB, 0:NB],
                      start=True, stop=True).then_inc(S("norm_spread"), 1)

        def root_norm(act, e, n):
            act.wait_ge(S("norm_summed"), e + 1)
            for rows, cols in ((P, slice(0, 4)), (NB, slice(4, 5))):
                act.activation(rt[0:rows, cols], ps[0:rows, 6, cols], ACT.Sqrt, scale=1.0 / n,
                               bias=eps[0:rows, 0:1]).then_inc(S("norm_root"), 1)

        def recip_norm(v, e):
            v.wait_ge(S("norm_root"), 2 * e + 2)
            for rows, cols in ((P, slice(0, 4)), (NB, slice(4, 5))):
                v.reciprocal(rt[0:rows, cols], rt[0:rows, cols]).then_inc(S("norm_recip"), 1)

        def copy_norm(act, e, out):
            act.wait_ge(S("norm_spread"), e + 1)
            act.activation(out[:, 0:SEQ], ps[:, 7, :], ACT.Copy).then_inc(S("norm_copied"), 1)
            act.activation(out[:, SEQ:T], ps[:, 6, 8:8 + NB], ACT.Copy).then_inc(S("norm_copied"), 1)

        def rms_pe(pe, i, e):
            pe.wait_ge(S("squares_added"), 7 * i + 5)
            sum_squares(pe, e, sqsum)
            spread_norm(pe, e)

        def square(act, i, k, ready=None):
            if ready is not None:
                act.wait_ge(S("res_added"), ready + k + 1)
            if k >= 3:
                act.wait_ge(S("squares_added"), 7 * i + k - 4)
            act.activation(sqsum if k == 0 else sq2[:, k % 2, :], xT[:, k, :], ACT.Square).then_inc(S("norm_squared"), 1)

        def add_square(v, i, k):
            v.wait_ge(S("norm_squared"), KT * i + k - 2)
            if k > 1:
                v.wait_ge(S("squares_added"), 7 * i + k - 3)
            v.tensor_tensor(sqsum, sqsum, sq2[:, k % 2, :], ALU.add).then_inc(S("squares_added"), 1)

        def rms_dve(v, i, e, w_col):
            recip_norm(v, e)
            v.wait_ge(S("norm_copied"), 2 * e + 2)
            for k in range(KT):
                v.scalar_tensor_tensor(xn[:, k, :], xT[:, k, :], vec[:, w_col + k:w_col + k + 1], rbc,
                                       ALU.mult, ALU.mult).then_inc(S("norm_ready"), 1)

        block = ctx.enter_context(nc.Block())

        @block.sync
        def _(sp):
            sp.sem_inc(S("sout_out"), OPEN)
            sp.dma_start(cst[:, 0:2 * P], consts[:, 0:2 * P]).then_inc(S("ident_in"), 16)
            for b in range(4):
                sp.dma_start(xtok[:, b, :], x_prompt[0, b * P:(b + 1) * P, :]).then_inc(S("x%d_in" % b), 16)
            sp.dma_start(xstok[0:NB, :], x_sample[:, 0, :]).then_inc(S("xs_in"), 16)
            sp.dma_start(cst[:, 2 * P:NK], consts[:, 2 * P:NK]).then_inc(S("consts_in"), 16)
            r = 0
            for v, n in ((norm1_w[0], 8), (norm2_w[0], 8), (normf_w, 8), (ssm_norm_w[0], 16), (conv_b[0], 32)):
                sp.dma_start(vload[r:r + n, :], v.rearrange("(n p) -> n p", p=P)).then_inc(S("vecs_in"), 16)
                r += n
            sp.dma_start(tapload, conv_w[0].rearrange("i (n p) -> (i n) p", p=P)).then_inc(S("vecs_in"), 16)
            with nc.allow_non_contiguous_dma(reason="a few small vectors"):
                for i, v in enumerate((dt_bias, a_log)):
                    sp.dma_start(hvec[0:32, i:i + 1], v[0].rearrange("(p o) -> p o", o=1)).then_inc(S("vecs_in"), 16)
                for i, v in enumerate((idx_ln_w, idx_ln_b)):
                    for h in range(2):
                        sp.dma_start(ilv[64 * h:64 * h + 64, i:i + 1],
                                     v[0].rearrange("(p o) -> p o", o=1)).then_inc(S("vecs_in"), 16)
                sp.dma_start(dskload[0:2, 0:16], d_skip[0].rearrange("(j k) -> k j", k=2)).then_inc(S("vecs_in"), 16)
            for o, c, n in ((0, C_IK, 64), (64, C_IK, 64), (128, C_DT, 32), (160, C_IW, 16)):
                sp.dma_start(ring[:, 2, :, o:o + n], w_block(w_in, c, n)).then_inc(S("small_in"), 16)
            sp.dma_start(idxT[0:NB, 0:NPG], page_table).then_inc(S("pages_in"), 16)
            for s in range(2):
                load(sp, s, w_block(w_in, C_IQ + s * 256))
            for s in range(3):
                load(sp, 3 + s, w_block(w_in, s * 256))
            for s in range(2):
                load(sp, s, w_block(w_in, C_IQ + (2 + s) * 256), N_IQ + 2 * s + 2)
            for s in range(3):
                load(sp, 3 + s, w_block(w_in, (3 + s) * 256), N_QKV + 2 * s + 2)
            sp.wait_ge(S("iqs_copied"), 1)
            sp.dma_start(iqsw[0:64].rearrange("p j b -> p (j b)"), iqs[64:P].rearrange("p j b -> p (j b)")).then_inc(S("iqs_swapped"), 16)
            sp.dma_start(iqsw[64:P].rearrange("p j b -> p (j b)"), iqs[0:64].rearrange("p j b -> p (j b)")).then_inc(S("iqs_swapped"), 16)
            sp.wait_ge(S("dsc_ready"), OPEN + 16)
            sp.dma_start(scratch.rearrange("b (o p k) -> p (b o) k", o=2, k=8),
                         dsc.rearrange("p (a k) -> p a k", k=8)).then_inc(S("dsc_out"), 16)
            sp.wait_ge(S("dsc_out"), 16)
            sp.dma_start(smp[0:NB, 0:PAST], scratch).then_inc(S("smp_in"), 16)
            sp.wait_ge(S("iktok_copied"), 2)
            sp.dma_start(ik_prompt[0, 0].rearrange("(b p) d -> p b d", p=P), iktok[:, 0:4, :]).then_inc(S("stored"), 16)
            sp.dma_start(ik_sample[0, :, 0], iktok[0:NB, 4, :]).then_inc(S("stored"), 16)
            sp.wait_ge(S("kvtok_copied"), 5)
            for o, c in ((k_prompt, 0), (v_prompt, 256)):
                sp.dma_start(o[0, 0].rearrange("(b p) g d -> p b (g d)", p=P),
                             kvtok[:, 0:4, c:c + 256]).then_inc(S("stored"), 16)
            for o, c in ((k_sample, 0), (v_sample, 256)):
                sp.dma_start(o[0, :, 0].rearrange("b g d -> b (g d)"), kvtok[0:NB, 4, c:c + 256]).then_inc(S("stored"), 16)
            sp.dma_start(conv_sample[0, :, 0:2, :], state_conv[0, :, 1:3, :]).then_inc(S("stored"), 16)

            def group_weights(g):
                first = isinstance(g, int) and g == 0
                load(sp, 0, w_block(w_in, C_X + g * 256), N_QKV if first else N_SSM + 6 * g - 4)
                yield
                for o, c in ((0, C_B), (128, C_C)):
                    if o == 0:
                        sp.wait_ge(S("dense_done"), N_QKV if first else N_SSM + 6 * g - 2)
                    sp.dma_start(ring[:, 1, :, o:o + P], w_block(w_in, c + g * P, P)).then_inc(S("bc_in"), 16)
                yield
                load(sp, 2, w_block(w_in, C_Z + g * 256), N_QKV if first else N_SSM + 6 * g)
                yield

            def load_state(g):
                for j in range(2):
                    sp.dma_start(st[:, j], state_ssm[0].rearrange("b (j h) p n -> (h p) j b n", h=2)[
                        :, bass.ds(2 * g + j, 1)].rearrange("p o b n -> p (o b) n")).then_inc(S("state_in"), 16)

            def load_conv(g):
                src = state_conv[0].rearrange("b i c -> (b i) c")
                for o, c, n in ((0, 256 * g, 256), (256, DI + P * g, P), (384, DI + NG * P + P * g, P)):
                    sp.dma_start(scl[:, o:o + n], src[:, bass.ds(c, n)]).then_inc(S("scl_in"), 16)

            def store_state(g):
                sp.wait_ge(S("state_new"), 2 * g + 2)
                for j in range(2):
                    sp.dma_start(ssm_sample[0].rearrange("b (j h) p n -> (h p) j b n", h=2)[
                        :, bass.ds(2 * g + j, 1)].rearrange("p o b n -> p (o b) n"), st[:, j]).then_inc(S("state_out"), 16)

            def store_conv(g):
                sp.wait_ge(S("ctok_ready"), g + 1)
                for o, c, n in ((0, 256 * g, 256), (256, DI + P * g, P), (384, DI + NG * P + P * g, P)):
                    sp.dma_start(conv_prompt[0, 0][:, bass.ds(c, n)], ctok[0:3, o:o + n]).then_inc(S("ctok_out"), 16)
                    sp.dma_start(conv_sample[0, :, 2, :][:, bass.ds(c, n)], ctok[3:11, o:o + n]).then_inc(S("ctok_out"), 16)

            def store_prompt_state(g):
                sp.wait_ge(S("sout_ready"), g + 1)
                sp.dma_start(ssm_prompt[0, 0].rearrange("h p n -> (h p) n").rearrange("(j q) n -> q j n", q=P)[
                    :, bass.ds(2 * g, 2)], sout).then_inc(S("sout_out"), 16)

            def load_selectors(g):
                sp.dma_start(gs[:], gsel_d[bass.ds(g, 1)].rearrange("o p c -> (o p) c")
                             if not isinstance(g, int) else gsel_d[g]).then_inc(S("gs_in"), 16)

            for _ in group_weights(0):
                pass
            load_selectors(0)
            sp.wait_ge(S("o_done"), OPEN + NH)
            load_conv(0)
            load_state(0)
            for _ in group_weights(1):
                pass

            def group_io(g, more, last=False):
                store_conv(g)
                sp.wait_ge(S("aux_done"), g + 1)
                if not last:
                    load_conv(g + 1)
                ws = group_weights(g + 2) if more else iter(())
                next(ws, None)
                store_state(g)
                next(ws, None)
                if not last:
                    sp.wait_ge(S("state_out"), 32 * g + 32)
                    sp.wait_ge(S("C_used"), 2 * g + 2)
                    load_state(g + 1)
                next(ws, None)
                if not last:
                    sp.wait_ge(S("abc_done"), 4 * g + 4)
                    load_selectors(g + 1)

            group_io(0, True)
            with sp.Fori(1, NG - 2) as g:
                store_prompt_state(g - 1)
                group_io(g, True)
            store_prompt_state(NG - 3)
            group_io(NG - 2, False)
            load(sp, 0, w_block(w_in, C_GM), N_SBR - 4)
            load(sp, 1, w_block(w_in, C_GM + 256), N_SBR - 2)
            load(sp, 2, w_block(w_in, C_GM + 512), N_SBR)
            store_prompt_state(NG - 2)
            def load_sbr(it, freed):
                load(sp, SBR_SLOTS[it][0], w_block(w_ssm_br, it * 256), freed[0])
                load(sp, SBR_SLOTS[it][1], w_block(w_ssm_br, it * 256, k0=D), freed[1])

            sp.dma_start(pgb32[:], page_table.rearrange("b n -> (b n)").partition_broadcast(P)).then_inc(S("pgb_in"), 16)
            group_io(NG - 1, False, last=True)
            load_sbr(0, (N_SBR + 2, N_SBR + 4))
            store_prompt_state(NG - 1)
            sp.wait_ge(S("sout_out"), 16 * NG + OPEN)
            sp.wait_ge(S("y_done"), 4 * NG)
            sp.wait_ge(S("h_done"), 4 * NG)
            sp.wait_ge(S("ys_ready"), 2 * NG)
            load_sbr(1, (None, None))
            load(sp, GM_SLOTS[3], w_block(w_in, C_GM + 768))
            load_sbr(2, (N_SBR + 8, None))
            load_sbr(3, (N_SBR + 10, None))
            freed = ((N_SBR + 14, None), (None, None), (N_SBR + 16, None), (N_ATT + 2, N_ATT + 4))
            for it in range(4):
                load(sp, ATT_SLOTS[it][0], w_block(w_in, C_GA + it * 256), freed[it][0])
                load(sp, ATT_SLOTS[it][1], w_block(w_attn_br, it * 256), freed[it][1])
            for u in range(4):
                load(sp, OUT_SLOTS[u], w_block(w_out, 256 * u), N_ATT + 6 + 2 * u)
            for it in range(2):
                n = N_ATT + 14 if it == 0 else N_OUT + 2
                load(sp, FFN_SLOTS[it][0], w_block(w_ffn_gate, it * 256), n)
                load(sp, FFN_SLOTS[it][1], w_block(w_ffn_up, it * 256), n + 2)
            load(sp, 3, w_block(w_ffn_down, 0), N_OUT + 6)
            load(sp, 4, w_block(w_ffn_down, 0, k0=D), N_OUT + 8)
            with sp.Fori(0, 4) as k:
                for o in range(2):
                    load(sp, FFN_SLOTS[o][0], w_block(w_ffn_gate, 512 * k + 256 * (o + 2)), 8 * k + N_FFN + 4 * o + 2)
                    load(sp, FFN_SLOTS[o][1], w_block(w_ffn_up, 512 * k + 256 * (o + 2)), 8 * k + N_FFN + 4 * o + 4)
            load(sp, FFN_SLOTS[0][0], w_block(w_ffn_gate, 2560), N_FFN + 34)
            load(sp, FFN_SLOTS[0][1], w_block(w_ffn_up, 2560), N_FFN + 36)
            for it in range(4):
                for i, slot in enumerate(DOWN_SLOTS[it % 2]):
                    if it == 0 and i < 2:
                        continue
                    freed = N_DOWN + 2 * (it - 1) if it > 1 else {1: N_FFN + 38, 2: N_FFN + 40, 5: N_FFN + 42, 0: N_FFN + 44}[slot]
                    load(sp, slot, w_block(w_ffn_down, 256 * it, k0=D * i, kt=(8, 8, 6)[i]), freed)
            for b in range(4):
                sp.wait_ge(S("y_ready"), 2 * b + 2)
                sp.dma_start(y_prompt[0, b * P:(b + 1) * P, :], ytok[:, b, :]).then_inc(S("stored"), 16)
            sp.wait_ge(S("y_ready"), 10)
            sp.dma_start(y_sample[:, 0, :], ystok[0:NB, :]).then_inc(S("stored"), 16)
            sp.wait_ge(S("smp_in"), 16)
            sp.wait_ge(S("stored"), 12 * 16)
            sp.wait_ge(S("ctok_out"), 96 * NG)
            sp.wait_ge(S("state_out"), 32 * NG)
            sp.wait_ge(S("sout_out"), 16 * NG + OPEN)

        @block.tensor
        def _(pe):
            def index_scores(pe):
                pe.wait_ge(S("vector_mark"), IK_READY)
                pe.wait_ge(S("dense_read"), 16)
                pe.wait_ge(S("tok_copied"), 3)
                with pe.Fori(0, 4) as k:
                    for j in range(2):
                        pe.wait_ge(S("iq_in_slot"), 2 * k + j + 1)
                        for h in range(2):
                            pe.wait_ge(S("relu_done"), HEAD + 12 * k + 6 * j + 3 * h - 3)
                            for b in (1, 2, 3):
                                mm = pe.matmul(ps[:, 1 + 3 * h + b, 0:EXT[b]],
                                               iqslot[j][64 * h:64 * h + 64, b * P:(b + 1) * P],
                                               ik2[64 * h:64 * h + 64, 0:EXT[b]], start=True, stop=True)
                                mm.then_inc(S("idx_done"), 1)

            def decode_scores(pe):
                pe.wait_ge(S("IQ_ready"), 4)
                pe.wait_ge(S("relu_done"), HEAD + 48)
                pe.wait_ge(S("wdiag_ready"), 2)
                pe.matmul(ps[:, 0, 0:P], ones[32:48, :], wdiag[32:48].rearrange("p b h -> p (b h)"),
                          start=True, stop=True)
                for j in range(8):
                    mm = pe.matmul(ps[0:NB, 0, P + 2 * j:P + 2 * j + 2], iqp[:, j, :],
                                   cst[:, K_PAR:K_PAR + 2], start=True, stop=True)
                mm.then_inc(S("tensor_mark"), 1)

                def turn(k, o):
                    pe.wait_ge(S("gathered%d" % o), 16 * k + 16)
                    for c in range(4):
                        mm = pe.transpose(ps[:, 4 + o, c * P:(c + 1) * P], gat[:, o, c * P:(c + 1) * P], ident)
                    mm.then_inc(S("gat_turned"), 1)

                def sequence(k, tile):
                    for o in range(2):
                        pe.wait_ge(S("gatT_ready"), OPEN + 2 * k)
                        turn(k, o)
                    tile(0, 4)
                    for o in range(2):
                        pe.wait_ge(S("gatT_ready"), OPEN + 2 * k + o + 1)
                        pe.wait_ge(S("drs_done"), OPEN + 2 * k)
                        for c in range(4):
                            mm = pe.matmul(ps[:, 6 + o, 32 * c:32 * c + 32], gatT[o][:, c * P:(c + 1) * P],
                                           IQ[:, k, :], start=True, stop=True)
                        mm.then_inc(S("dec_done"), 1)
                    tile(4, 8)

                pe.wait_ge(S("wbc_ready"), 2)
                for k in range(6):
                    s, j = k // 2, k % 2
                    if j == 0:
                        pe.wait_ge(w_in_slot[3 + s], 32)
                    sequence(k, lambda k0, k1: dense(pe, 6 + N_QKV + k, j, block_of(3 + s, j), xns, k0=k0, k1=k1))
                with pe.Fori(6, NB) as k:
                    sequence(k, lambda k0, k1: None)

            pe.sem_inc(S("idx_done"), TILE)
            for name in ("dec_done", "p_turned", "o_done", "logits_done"):
                pe.sem_inc(S(name), OPEN)
            pe.wait_ge(S("ident_in"), 16)
            for b in range(4):
                pe.wait_ge(S("x%d_in" % b), 16)
                if b >= 2:
                    pe.wait_ge(S("xT_ready"), 2 * b - 2)
                for k in range(KT):
                    mm = pe.transpose(ps[:, 2 * (b % 2) + k // 4, (k % 4) * P:(k % 4 + 1) * P],
                                      xtok[:, b, k * P:(k + 1) * P], ident)
                mm.then_inc(S("x_turned"), 1)
            pe.wait_ge(S("xs_in"), 16)
            for k in range(KT):
                mm = pe.transpose(ps[:, 5, k * NB:(k + 1) * NB], xstok[0:NB, k * P:(k + 1) * P], ident[0:NB, 0:NB])
            mm.then_inc(S("x_turned"), 1)
            pe.wait_ge(S("squares_added"), 5)
            sum_squares(pe, 0, sqsum)
            pe.wait_ge(S("consts_in"), 16)
            pe.wait_ge(S("vecs_in"), 16 * 13)
            pe.transpose(ps[:, 4, 0:72], vload[0:72, :], ident[0:72, 0:72])
            pe.transpose(ps[:, 4, 128:256], tapload, ident)
            pe.matmul(ps[:, 4, 256:272], cst[0:2, K_HALF:K_HALF + P], dskload[0:2, :], start=True,
                      stop=True).then_inc(S("tensor_mark"), 1)
            spread_norm(pe, 0)
            pe.wait_ge(S("xT_ready"), 9)
            pe.wait_ge(S("small_in"), 64)
            dense(pe, 0, 0, [ring[:, 2, k, 0:P] for k in range(KT)], xns, ready=("norm_ready", 0))
            dense(pe, 1, 1, [ring[:, 2, k, P:P + 48] for k in range(KT)], xns, m=48)
            pe.wait_ge(S("dense_read"), 1)
            for h in range(2):
                mm = pe.matmul(ps[:, 4 + h, 0:TH], blk64, ik2[:, h * TH:(h + 1) * TH], start=True, stop=True)
            mm.then_inc(S("tensor_mark"), 1)
            pe.wait_ge(S("vector_mark"), PAGES_F)
            pe.transpose(ps[0:NPG, 6, 0:NB], pgf[0:NB, 0:NPG], ident[0:NB, 0:NB]).then_inc(S("tensor_mark"), 1)
            with pe.Fori(0, 2) as k:
                for s in range(2):
                    pe.wait_ge(w_in_slot[s], 16 * k + 16)
                    for j in range(2):
                        dense(pe, 4 * k + N_IQ + 2 * s + j, j, block_of(s, j), xns)
            pe.wait_ge(S("ik_sq"), 1)
            for h in range(2):
                mm = pe.matmul(ps[:, 4 + h, 0:TH], blk64, ikt2[:, h * TH:(h + 1) * TH], start=True, stop=True)
            mm.then_inc(S("tensor_mark"), 1)
            pe.wait_ge(S("vector_mark"), PAGEST)
            for o in range(2):
                mm = pe.matmul(ps[:, 6, 16 + o * NB:16 + (o + 1) * NB], cst[0:NPG, K_PG + o * P:K_PG + (o + 1) * P],
                               pgf[0:NPG, NPG:NPG + NB], start=True, stop=True)
            mm.then_inc(S("tensor_mark"), 1)
            pe.wait_ge(S("a_summed"), 4)
            for b in range(5):
                n = P if b < 4 else NB
                pe.transpose(ps[0:n, 7, 48 * b:48 * b + 48], small[0:48, b * P:b * P + n], ident[0:48, 0:48])
            for c in range(4):
                mm = pe.transpose(ps[:, 7, 256 + 32 * c:288 + 32 * c], acT[0:32, c * P:(c + 1) * P], ident[0:32, 0:32])
            mm.then_inc(S("tensor_mark"), 1)
            for s in range(3):
                pe.wait_ge(w_in_slot[3 + s], 16)
                for j in range(2):
                    dense(pe, N_QKV + 2 * s + j, j, block_of(3 + s, j), xns)
            index_scores(pe)
            decode_scores(pe)
            pe.wait_ge(S("gatT_ready"), OPEN + 2 * NB)
            pe.wait_ge(S("drs_done"), OPEN + 2 * NB)
            for b in range(4):
                pe.transpose(ps[:, 4, b * ID:(b + 1) * ID], ik2[0:64, b * P:(b + 1) * P], ident[0:64, 0:64])
            pe.transpose(ps[0:NB, 4, 256:256 + ID], ik2[0:64, SEQ:T], ident[0:64, 0:64]).then_inc(S("tensor_mark"), 1)
            pe.wait_ge(S("dense_read"), N_SSM)
            for b in range(5):
                n, bank = (P, 5 + b % 2) if b < 4 else (NB, 5)
                if b >= 2:
                    pe.wait_ge(S("kvtok_copied"), b - 1)
                for i in range(4):
                    mm = pe.transpose(ps[0:n, bank, i * P:(i + 1) * P], kviq[:, i, b * P:b * P + n], ident)
                mm.then_inc(S("kv_turned"), 1)

            def group_tile(g, i, k0=0, k1=KT):
                s, j = i // 2, i % 2
                if k0:
                    pass
                elif i == 2:
                    pe.wait_ge(S("bc_in"), 32 * g + 32)
                elif j == 0:
                    pe.wait_ge(w_in_slot[s], 16 * (g + F_SSM[s]) + 16)
                dense(pe, 6 * g + N_SSM + i, j, block_of(s, j), xns, k0=k0, k1=k1)

            def logits(i, kv):
                pe.wait_ge(S("q_in_slot"), i + 1)
                for b in range(4):
                    if b == 0:
                        pe.wait_ge(S("logits_read"), OPEN + 4 * i)
                    mm = pe.matmul(ps[:, b, 0:EXT[b]], qslot[:, b * P:(b + 1) * P], kviq[:, kv, 0:EXT[b]],
                                   start=True, stop=True)
                    mm.then_inc(S("logits_done"), 1)

            def values(i, kv):
                for b in range(4):
                    pe.wait_ge(S("p_ready"), 4 * i + b + 1)
                    for c in range(b + 1):
                        n = AT[b] // P + c
                        bank, col = PB[n]
                        mm = pe.transpose(ps[:, bank, col:col + P], lg[:, AT[b] + c * P:AT[b] + (c + 1) * P], ident)
                    mm.then_inc(S("p_turned"), 1)
                pe.wait_ge(S("o_read"), OPEN + i)
                for b in range(4):
                    pe.wait_ge(S("pT_ready"), 3 * i + (1, 1, 2, 3)[b])
                    for c in range(b + 1):
                        mm = pe.matmul(ps[:, 7, b * P:(b + 1) * P], kvtok[:, c, 256 + kv * P:256 + (kv + 1) * P],
                                       pT[:, AT[b] // P + c, :], start=(c == 0), stop=(c == b))
                mm.then_inc(S("o_done"), 1)

            pe.wait_ge(S("kvtok_copied"), 5)
            pe.wait_ge(S("iktok_copied"), 2)
            pe.wait_ge(S("dense_read"), N_SSM)
            logits(0, 0)
            with pe.Fori(0, 3) as r:
                logits(r + 1, 0)
                values(r, 0)
            logits(4, 1)
            values(3, 0)
            with pe.Fori(4, 7) as r:
                logits(r + 1, 1)
                values(r, 1)
            pe.wait_ge(S("logits_read"), OPEN + 4 * NH)
            group_tile(0, 0)
            group_tile(0, 1)
            values(7, 1)

            def last_tile(i, k0=0, k1=KT):
                s, j = GM_SLOTS[i // 2], i % 2
                if j == 0 and k0 == 0:
                    pe.wait_ge(w_in_slot[s], 16 * (F_SBR[s] + 1))
                dense(pe, N_SBR + i, j, block_of(s, j), xns, k0=k0, k1=k1)

            def step_aux(g, prev):
                pe.wait_ge(S("dense_read"), 6 * g + N_SSM + 4)
                if prev:
                    pe.wait_ge(S("h_done"), 4 * g)
                for i in range(4):
                    mm = pe.transpose(ps[0:11, 5, i * P:(i + 1) * P], raw[:, i, SEQ:SEQ + 11], ident)
                mm.then_inc(S("ctok_done"), 1)
                pe.wait_ge(S("scl_in"), 48 * g + 48)
                pe.wait_ge(S("gs_in"), 16 * g + 16)
                for j in range(2):
                    sel = gs[:, 512 + j * P:512 + (j + 1) * P]
                    pe.matmul(ps[:, 4, 96 + NB * j:96 + NB * (j + 1)], sel, dtT[0:32, SEQ:T], start=True, stop=True)
                    pe.matmul(ps[:, 4, 112 + NB * j:112 + NB * (j + 1)], sel, acT[0:32, SEQ:T], start=True, stop=True)
                for i in range(4):
                    mm = pe.transpose(ps[:, 4, i * 24:(i + 1) * 24], scl[:, i * P:(i + 1) * P], ident[0:24, 0:24])
                for r in range(4):
                    mm = pe.matmul(ps[:, 4, 384 + 4 * r:388 + 4 * r], gs[:, r * P:(r + 1) * P], acT[0:32, P - 1:SEQ:P],
                                   start=True, stop=True)
                if prev:
                    for j in range(2):
                        mm = pe.transpose(ps[:, 4, P + j * P:P + (j + 1) * P], hT[:, j * P:(j + 1) * P], ident)
                mm.then_inc(S("aux_done"), 1)

            def step_norm(g):
                pe.wait_ge(S("sqg_added"), g + 1)
                sum_squares(pe, g + 1, sqg[:, 0, :])

            def step_turn(g, prev):
                pe.wait_ge(S("ctok_ready"), g + 1)
                pe.wait_ge(S("silu_done"), 4 * g + 3)
                for c in range(4):
                    pe.transpose(ps[:, 5, c * P:(c + 1) * P], xc[:, 2, c * P:(c + 1) * P], ident)
                if prev:
                    pe.wait_ge(S("norm_copied"), 2 * g + 2)
                for c in range(4):
                    for j in range(2):
                        mm = pe.transpose(ps[:, 6 + c // 2, (c % 2) * 256 + j * P:(c % 2) * 256 + (j + 1) * P],
                                          xc[:, j, c * P:(c + 1) * P], ident)
                mm.then_inc(S("turned"), 1)

            def step_decode(g):
                pe.wait_ge(S("xdt_ready"), 2 * g + 2)
                pe.wait_ge(S("Bt_ready"), g + 1)
                pe.wait_ge(S("aux_read"), g + 1)
                pe.wait_ge(S("silu_done"), 4 * g + 4)
                for t, bank in ((2, 6), (3, 4)):
                    for b in range(NB):
                        mm = pe.matmul(ps[:, bank + b // 4, (b % 4) * P:(b % 4 + 1) * P],
                                       xc[:, t, SEQ + b:SEQ + b + 1].broadcast_to((P, P)), ident,
                                       start=True, stop=True)
                    mm.then_inc(S("bcast_done"), 1)

            def step_cb(g):
                pe.wait_ge(S("C_used"), 2 * g + 2)
                for c in range(4):
                    mm = pe.matmul(ps[:, 5, c * P:(c + 1) * P], xc[:, 2, c * P:(c + 1) * P],
                                   xc[:, 3, c * P:(c + 1) * P], start=True, stop=True)
                mm.then_inc(S("cb_done"), 1)

            def step_a(g, c):
                if c:
                    pe.wait_ge(S("abc_read"), 4 * g + c)
                for r in range(4):
                    mm = pe.matmul(ps[:, 4, r * P:(r + 1) * P], gs[:, r * P:(r + 1) * P],
                                   acT[0:32, c * P:(c + 1) * P], start=True, stop=True)
                mm.then_inc(S("abc_done"), 1)

            def step_y(g, c):
                pe.wait_ge(S("M_ready"), 7 * g + 2 * c + 1)
                if c:
                    pe.wait_ge(S("h_done"), 4 * g + c)
                else:
                    pe.wait_ge(S("B_used"), 2 * g + 2)
                for r in range(4):
                    o = ps[64 * (r % 2):64 * (r % 2) + 64, 6 + r // 2, c * P:(c + 1) * P]
                    pe.matmul(o, xdt[:, c, 64 * r:64 * r + 64], M2[:, c % 2, r * P:(r + 1) * P],
                              start=True, stop=(c == 0))
                    if c:
                        pe.matmul(o, hT[:, 64 * r:64 * r + 64], Cx2[:, c % 2, r * P:(r + 1) * P],
                                  start=False, stop=True)
                pe.wait_ge(S("xw_ready"), g + 1)
                pe.matmul(ps[:, 5, 256 * (c % 2):256 * (c % 2) + 256], Bt[:, c, :], xw[:, c, :],
                          start=True, stop=True).then_inc(S("y_done"), 1)

            def group(g, prev, more):
                D = (lambda *a: group_tile(g + 1, *a)) if more else last_tile
                D(0, 0, 4)
                step_aux(g, prev)
                D(0, 4, 8)
                if prev:
                    step_norm(g - 1)
                D(1)
                if prev:
                    spread_norm(pe, g)
                step_turn(g, prev)
                D(2)
                step_decode(g)
                D(3)
                step_cb(g)
                step_a(g, 0)
                D(4, 0, 4)
                step_a(g, 1)
                D(4, 4, 8)
                step_y(g, 0)
                D(5, 0, 2)
                step_a(g, 2)
                D(5, 2, 4)
                step_y(g, 1)
                D(5, 4, 5)
                step_a(g, 3)
                if more:
                    D(5, 5, 8)
                step_y(g, 2)
                step_y(g, 3)
                if not more:
                    D(5, 5, 8)

            pe.wait_ge(S("o_read"), OPEN + NH)
            pe.wait_ge(S("vector_mark"), RAW_ZERO)
            for i in range(2, 6):
                group_tile(0, i)
            group(0, False, True)
            with pe.Fori(1, NG - 1) as g:
                group(g, True, True)
            group(NG - 1, True, False)
            step_norm(NG - 1)
            spread_norm(pe, NG)
            pe.wait_ge(S("h_done"), 4 * NG)
            pe.wait_ge(S("abc_read"), 4 * NG)
            for j in range(2):
                mm = pe.transpose(ps[:, 4, P + j * P:P + (j + 1) * P], hT[:, j * P:(j + 1) * P], ident)
            mm.then_inc(S("aux_done"), 1)

            def sbr(it, j):
                slots = SBR_SLOTS[it]
                for s in slots:
                    pe.wait_ge(w_in_slot[s], 16 * (F_SBR[s] + (2, 1, 3, 2)[it]))
                dense(pe, SBR_TILES[it] + j, j, block_of(slots[0], j) + block_of(slots[1], j),
                      [ssm_o[:, k, :] for k in range(16)], ready=("ssm_ready", 0) if it + j == 0 else None)

            sbr(0, 0)
            sbr(0, 1)
            pe.wait_ge(S("dtop_kept"), 4 * NG + OPEN)
            pe.wait_ge(S("sout_ready"), NG)
            for o in range(2):
                mm = pe.transpose(ps[:, 4, NB * o:NB * o + NB], sel_idx[0:NB, o * P:(o + 1) * P], ident[0:NB, 0:NB])
            mm.then_inc(S("tensor_mark"), 1)
            sbr(1, 0)
            sbr(1, 1)
            sbr(2, 0)
            pe.wait_ge(S("norm_copied"), 2 * NG + 2)
            pe.wait_ge(S("decode_read"), POS_READ)
            pe.wait_ge(S("vector_mark"), QK_NEW_READY)
            pe.matmul(ps[0:64, 7, TOPK:TOPK + 1], qk_new.rearrange("p b h -> p (b h)"), ones[:, 0:1],
                      start=True, stop=True)

            def turn_keys(b):
                if b >= 2:
                    pe.wait_ge(S("KT_ready"), b - 1)
                for o in range(2):
                    for kv in range(2):
                        mm = pe.transpose(ps[:, 4 + b % 2, (2 * o + kv) * P:(2 * o + kv + 1) * P],
                                          KV[:, 0, NB * o + b, kv * P:(kv + 1) * P], ident)
                mm.then_inc(S("keys_turned"), 1)

            pe.wait_ge(S("keys_in"), 16 * 16)
            turn_keys(0)
            for b in range(NB):
                if b + 1 < NB:
                    turn_keys(b + 1)
                pe.wait_ge(S("KT_ready"), b + 1)
                for o in range(2):
                    for kv in range(2):
                        mm = pe.matmul(ps[:, 6, 64 * o + 8 * b + 4 * kv:64 * o + 8 * b + 4 * kv + 4],
                                       KTd[:, b % 2, (2 * o + kv) * P:(2 * o + kv + 1) * P],
                                       qkvs[:, 4 * kv:4 * kv + 4, b], start=True, stop=True)
                mm.then_inc(S("dlogits_done"), 1)
            sbr(2, 1)
            pe.wait_ge(S("vector_mark"), LK_READY)
            for o in range(2):
                mm = pe.transpose(ps[0:64, 7, o * P:(o + 1) * P], lk[:, o].rearrange("p b h -> p (b h)"), ident)
            mm.then_inc(S("tensor_mark"), 1)
            pe.wait_ge(w_in_slot[GM_SLOTS[3]], 16 * (F_SBR[GM_SLOTS[3]] + 1))
            for j in range(2):
                dense(pe, N_SBR + 12 + j, j, block_of(GM_SLOTS[3], j), xns)
            sbr(3, 0)
            sbr(3, 1)
            pe.wait_ge(S("vector_mark"), DP_READY)
            for o in range(2):
                pe.transpose(ps[:, 4, 64 * o:64 * o + 64], lrow[0:64, o * P:(o + 1) * P], ident[0:64, 0:64])
            pe.matmul(ps[:, 4, 128:192], lrow[0:64, TOPK:TOPK + 1].broadcast_to((64, P)), ident[0:64, 0:64],
                      start=True, stop=True).then_inc(S("tensor_mark"), 1)
            for it in range(4):
                ga_slot, at_slot = ATT_SLOTS[it]
                pe.wait_ge(w_in_slot[ga_slot], 16 * (F_ATT[ga_slot] + it // 3 + 1))
                for j in range(2):
                    dense(pe, N_ATT + 4 * it + j, j, block_of(ga_slot, j), xns)
                if it == 0:
                    pe.wait_ge(S("decode_read"), PTD_READY)
                    pe.wait_ge(S("values_in"), 16 * 16)
                    for b in range(NB):
                        for kv in range(2):
                            for o in range(2):
                                mm = pe.matmul(ps[:, 5, 8 * b + 4 * kv:8 * b + 4 * kv + 4],
                                               KV[:, 1, NB * o + b, kv * P:(kv + 1) * P],
                                               pTd[:, o, b, 4 * kv:4 * kv + 4], start=(o == 0), stop=(o == 1))
                    mm.then_inc(S("tensor_mark"), 1)
                    pe.wait_ge(S("vector_mark"), DO_READY)
                pe.wait_ge(w_in_slot[at_slot], 16 * (F_ATT[at_slot] + it // 3 + 1))
                for j in range(2):
                    dense(pe, N_ATT + 4 * it + 2 + j, j, block_of(at_slot, j), [uT[:, k, :] for k in range(KT)])
            for u in range(4):
                pe.wait_ge(w_in_slot[OUT_SLOTS[u]], 16 * (F_OUT[OUT_SLOTS[u]] + 1))
                for j in range(2):
                    dense(pe, N_OUT + 2 * u + j, j, block_of(OUT_SLOTS[u], j), [mix[:, k, :] for k in range(KT)],
                          ready=("mixed", 8) if u + j == 0 else None)
            rms_pe(pe, 1, NORM2)
            def ffn(k, o):
                for s in range(2):
                    slot = FFN_SLOTS[o][s]
                    pe.wait_ge(w_in_slot[slot], 16 * (k + F_FFN[slot] + 1))
                    for j in range(2):
                        first = isinstance(k, int) and k + o + s + j == 0
                        dense(pe, 8 * k + N_FFN + 4 * o + 2 * s + j, j, block_of(slot, j), xns,
                              ready=("norm_ready", KT) if first else None)

            ffn(0, 0)
            ffn(0, 1)
            with pe.Fori(1, 5) as k:
                ffn(k, 0)
                ffn(k, 1)
            ffn(5, 0)
            def down(it, k):
                slots = DOWN_SLOTS[it]
                for s in slots:
                    pe.wait_ge(w_in_slot[s], 16 * (k + F_DOWN[s] + 1))
                for j in range(2):
                    blocks = block_of(slots[0], j) + block_of(slots[1], j) + block_of(slots[2], j, 6)
                    dense(pe, 4 * k + N_DOWN + 2 * it + j, j, blocks, [hid[:, i, :] for i in range(FT)],
                          ready=("hid_ready", 2 * OPEN) if isinstance(k, int) and k + it + j == 0 else None)

            down(0, 0)
            down(1, 0)
            down(0, 1)
            down(1, 1)
            rms_pe(pe, 2, NORMF)
            pe.wait_ge(S("dense_read"), N_END)
            for b in range(5):
                n = P if b < 4 else NB
                if b >= 2:
                    pe.wait_ge(S("y_ready"), 2 * b - 2)
                for k in range(KT):
                    if b == 0:
                        pe.wait_ge(S("norm_ready"), 2 * KT + k + 1)
                    mm = pe.transpose(ps[0:n, 2 * (b % 2) + k // 4, (k % 4) * P:(k % 4 + 1) * P],
                                      xn[:, k, b * P:b * P + n], ident)
                mm.then_inc(S("y_turned"), 1)

        @block.scalar
        def _(act):
            act.sem_inc(S("relu_done"), HEAD)
            for name in ("gatT_ready", "o_read"):
                act.sem_inc(S(name), OPEN)
            for b in range(4):
                act.wait_ge(S("x_turned"), b + 1)
                for h in range(2):
                    act.activation(xT[:, 4 * h:4 * h + 4, b * P:(b + 1) * P],
                                   ps[:, 2 * (b % 2) + h, :].rearrange("p (k t) -> p k t", t=P), ACT.Copy).then_inc(S("xT_ready"), 1)
                act.wait_ge(S("xT_ready"), 2 * b + 2)
                if b >= 2:
                    act.wait_ge(S("squares_added"), b - 1)
                act.activation(sqx[b % 2], xT[:, :, b * P:(b + 1) * P], ACT.Square).then_inc(S("norm_squared"), 1)
            act.wait_ge(S("x_turned"), 5)
            act.activation(xT[:, :, SEQ:T], ps[:, 5, 0:64].rearrange("p (k t) -> p k t", t=NB), ACT.Copy).then_inc(S("xT_ready"), 1)
            act.wait_ge(S("xT_ready"), 9)
            act.activation(sqxs, xT[:, :, SEQ:T], ACT.Square).then_inc(S("norm_squared"), 1)
            act.wait_ge(S("vector_mark"), EPS_SET)
            root_norm(act, 0, D)
            act.wait_ge(S("tensor_mark"), VECS_TURNED)
            act.activation(vec[:, 0:72], ps[:, 4, 0:72], ACT.Copy).then_inc(S("vec_ready"), 1)
            copy_norm(act, 0, rbc)
            act.activation(taps, ps[:, 4, 128:256], ACT.Copy, scale=0.5).then_inc(S("taps_ready"), 1)
            act.activation(dsk, ps[:, 4, 256:272], ACT.Copy).then_inc(S("dsk_ready"), 1)
            act.wait_ge(S("dense_done"), 1)
            act.activation(two(ik2), tile_out(0), ACT.Copy).then_inc(S("dense_read"), 1)
            act.wait_ge(S("dense_done"), 2)
            act.activation(two(small[0:48, :]), tile_out(1, 48), ACT.Copy).then_inc(S("dense_read"), 1)
            act.wait_ge(S("vector_mark"), DT_ABS)
            act.activation(spe[0:32, :], spa[0:32, :], ACT.Exp, scale=-1.0).then_inc(S("dt_exp"), 1)
            act.activation(hvec[0:32, 2:3], hvec[0:32, 1:2], ACT.Exp).then_inc(S("a_exp"), 1)
            act.wait_ge(S("vector_mark"), IK_SQ_IN)
            act.activation(ikt2, ikt1, ACT.Square).then_inc(S("ik_sq"), 1)
            with act.Fori(0, 4) as k:
                for j in range(2):
                    act.wait_ge(S("dense_done"), 2 * k + N_IQ + 1 + j)
                    act.activation(two(kviq[:, 2 * k + 4 + j, :]), tile_out(j), ACT.Copy).then_inc(S("dense_read"), 1)
            act.wait_ge(S("dense_read"), N_QKV)
            act.activation(iqs, kviq[:, 4:12, SEQ:T], ACT.Copy).then_inc(S("iqs_copied"), 1)
            act.wait_ge(S("tensor_mark"), IK_VAR)
            act.activation(two(ikt2), ps[:, 4:6, 0:TH], ACT.Sqrt, bias=eps[:, 0:1]).then_inc(S("ik_root"), 1)
            act.wait_ge(S("tensor_mark"), TOK_TURNED)
            tk = ps[:, 7, 0:240].rearrange("p (b h) -> p b h", h=48)
            act.activation(tok[:, 0:4, 0:32], tk[:, 0:4, 0:32], ACT.Copy).then_inc(S("tok_copied"), 1)
            act.activation(tok[:, 0:4, 32:48], tk[:, 0:4, 32:48], ACT.Copy, scale=1.0 / 32).then_inc(S("tok_copied"), 1)
            act.activation(tok[0:NB, 4, 32:48], tk[0:NB, 4, 32:48], ACT.Copy, scale=1.0 / 32).then_inc(S("tok_copied"), 1)
            act.activation(actok, ps[:, 7, 256:384].rearrange("p (b h) -> p b h", h=32), ACT.Copy).then_inc(S("actok_ready"), 1)
            for j in range(6):
                act.wait_ge(S("dense_done"), N_QKV + 1 + j)
                act.activation(two(uT[:, j, :]), tile_out(j % 2), ACT.Copy).then_inc(S("dense_read"), 1)
            with act.Fori(0, 4) as k:
                for j in range(2):
                    for h in range(2):
                        for b in (1, 2, 3):
                            act.wait_ge(S("idx_done"), TILE + 12 * k + 6 * j + 3 * h + b)
                            if b == 1:
                                act.wait_ge(S("idx_added"), HEAD + 12 * k + 6 * j + 3 * h - 3)
                            act.activation(rl[:, h, X0[b]:X0[b] + EXT[b]], ps[:, 1 + 3 * h + b, 0:EXT[b]],
                                           ACT.Relu).then_inc(S("relu_done"), 1)
            act.wait_ge(S("tensor_mark"), WBC_DONE)
            act.activation(wbc.rearrange("p b h -> p (b h)"), ps[:, 0, 0:P], ACT.Copy).then_inc(S("wbc_ready"), 1)
            act.activation(drelu[0:NB, :], ps[0:NB, 0, P:P + 16], ACT.Relu).then_inc(S("wbc_ready"), 1)
            def gathered_out(k):
                for o in range(2):
                    act.wait_ge(S("gat_turned"), 2 * k + o + 1)
                    act.wait_ge(S("dec_done"), OPEN + 2 * k)
                    act.activation(gatT[o], ps[:, 4 + o, :], ACT.Copy).then_inc(S("gatT_ready"), 1)

            for j in range(6):
                gathered_out(j)
                act.wait_ge(S("dense_done"), N_QKV + 7 + j)
                dst = uT[:, 6 + j, :] if j < 2 else kviq[:, j - 2, :]
                act.activation(two(dst), tile_out(j % 2), ACT.Copy).then_inc(S("dense_read"), 1)
            with act.Fori(6, NB) as k:
                gathered_out(k)
            act.wait_ge(S("dense_read"), N_SSM)
            act.activation(qkvs[:, 0:8, :], uT[:, :, SEQ:T], ACT.Copy).then_inc(S("qkvs_ready"), 1)
            act.activation(qkvs[:, 8:12, :], kviq[:, 0:4, SEQ:T], ACT.Copy).then_inc(S("qkvs_ready"), 1)
            act.wait_ge(S("tensor_mark"), IK_TURNED)
            act.activation(iktok[:, 0:4, :], ps[:, 4, 0:256].rearrange("p (b d) -> p b d", b=4), ACT.Copy).then_inc(S("iktok_copied"), 1)
            act.activation(iktok[0:NB, 4, :], ps[0:NB, 4, 256:320], ACT.Copy).then_inc(S("iktok_copied"), 1)
            for b in range(5):
                n, bank = (P, 5 + b % 2) if b < 4 else (NB, 5)
                act.wait_ge(S("kv_turned"), b + 1)
                act.activation(kvtok[0:n, b, :], ps[0:n, bank, :], ACT.Copy).then_inc(S("kvtok_copied"), 1)
            with act.Fori(0, NH // 2) as k:
                for i in (2 * k, 2 * k + 1):
                    for b in range(4):
                        act.wait_ge(S("neg_max"), 4 * i + b + 1)
                        l = lg[:, AT[b]:AT[b] + EXT[b]]
                        act.activation(l, l, ACT.Exp, scale=SCALE, bias=anm[:, b:b + 1],
                                       accum_out=asum[:, b:b + 1]).then_inc(S("exp_done"), 1)
                    for b, (t0, n) in enumerate(((0, 3), (3, 3), (6, 4))):
                        act.wait_ge(S("p_turned"), OPEN + 4 * i + b + 2)
                        if b == 0:
                            act.wait_ge(S("o_done"), OPEN + i)
                        act.activation(pT[:, t0:t0 + n, :], ps[:, 4 + b, 0:n * P].rearrange("p (a t) -> p a t", t=P),
                                       ACT.Copy).then_inc(S("pT_ready"), 1)
                    act.wait_ge(S("o_done"), OPEN + i + 1)
                    act.activation(uT[:, bass.ds(i, 1), 0:SEQ].rearrange("p o t -> p (o t)"), ps[:, 7, :],
                                   ACT.Copy).then_inc(S("o_read"), 1)

            def tile_in(g, i):
                act.wait_ge(S("dense_done"), 6 * g + N_SSM + i + 1)
                if i < 4:
                    if not isinstance(g, int) or g > 0:
                        act.wait_ge(S("conv_done"), 4 * g - 3 + i)
                        act.wait_ge(S("ctok_done"), g)
                        act.wait_ge(S("dconv_done"), g)
                    act.activation(two(raw[:, i, 3:T + 3]), tile_out(i % 2), ACT.Copy).then_inc(S("dense_read"), 1)
                else:
                    j = i - 4
                    z = ssm_o[:, bass.ds(2 * g + j, 1), :].rearrange("p o (h t) -> p (o h) t", h=2)
                    act.activation(two(thz[:, j, :]), tile_out(j), ACT.Tanh, scale=0.5).then_inc(S("thz_ready"), 1)
                    act.activation(z, tile_out(j), ACT.Copy, scale=0.5).then_inc(S("dense_read"), 1)

            def gate_ahead(i):
                if i < 2:
                    act.wait_ge(S("ctok_done"), NG)
                    act.wait_ge(S("dconv_done"), NG)
                else:
                    act.wait_ge(S("z_ready"), 2 * NG)
                act.wait_ge(S("dense_done"), N_SBR + i + 1)
                act.activation(two(gates_ahead[i]), tile_out(i % 2), ACT.Tanh, scale=0.5).then_inc(S("dense_read"), 1)

            def chunk(g, c):
                act.wait_ge(S("abc_done"), 4 * g + c + 1)
                if c > 1:
                    act.wait_ge(S("y_done"), 4 * g + c - 1)
                elif not isinstance(g, int) or g > 0:
                    act.wait_ge(S("y_done"), 4 * g)
                abc = ps[:, 4, :]
                for r in range(4):
                    act.activation(M2[:, c % 2, r * P:(r + 1) * P], abc[:, r * P:(r + 1) * P], ACT.Relu, scale=-1.0,
                                   bias=atg[:, c, r:r + 1]).then_inc(S("E_relu"), 1)
                act.activation(Cx2[:, c % 2, :], abc, ACT.Exp).then_inc(S("abc_read"), 1)
                act.wait_ge(S("E_relu"), 16 * g + 4 * c + 4)
                act.activation(M2[:, c % 2, :], M2[:, c % 2, :], ACT.Exp, scale=-1.0).then_inc(S("E_ready"), 1)

            def squares(g):
                for j in range(2):
                    act.wait_ge(S("Y_ready"), 2 * g + j + 1)
                    act.activation(sqg[:, j, :], Y[:, j, :], ACT.Square).then_inc(S("sqg_ready"), 1)

            def group(g, prev, more):
                for i in range(4):
                    act.wait_ge(S("cw_ready"), 3 * g + 3)
                    act.activation(xc[:, i, 0:SEQ], raw[:, i, 0:SEQ], ACT.Identity, scale=cw[:, 5 * i:5 * i + 1],
                                   bias=cw[:, 5 * i + 4:5 * i + 5]).then_inc(S("tap0"), 1)
                act.wait_ge(S("ctok_done"), g + 1)
                if prev:
                    act.wait_ge(S("ctok_out"), 96 * g)
                act.activation(ctok[0:11, :], ps[0:11, 5, :], ACT.Copy).then_inc(S("ctok_ready"), 1)
                act.wait_ge(S("aux_done"), g + 1)
                act.activation(sct, ps[:, 4, 0:96].rearrange("p (i c) -> p i c", c=24), ACT.Copy).then_inc(S("sct_ready"), 1)
                act.activation(alast.rearrange("p r c -> p (r c)"), ps[:, 4, 384:400], ACT.Copy).then_inc(S("alast"), 1)
                act.activation(ealast.rearrange("p r c -> p (r c)"), ps[:, 4, 384:400], ACT.Exp).then_inc(S("alast"), 1)
                act.activation(dts, ps[:, 4, 96:112].rearrange("p (i c) -> p i c", c=NB), ACT.Copy).then_inc(S("dts_ready"), 1)
                if prev:
                    act.wait_ge(S("sout_out"), 16 * g - 16 + OPEN)
                    act.activation(sout, ps[:, 4, P:3 * P].rearrange("p (j n) -> p j n", n=P), ACT.Copy).then_inc(S("sout_ready"), 1)
                act.activation(dAs, ps[:, 4, 112:128].rearrange("p (i c) -> p i c", c=NB), ACT.Exp).then_inc(S("aux_read"), 1)
                for i in range(4):
                    act.wait_ge(S("conv_done"), 4 * g + i + 1)
                    if i == 0:
                        act.wait_ge(S("dconv_done"), g + 1)
                    if i > 1:
                        act.wait_ge(S("silu_done"), 4 * g + i - 1)
                    act.activation(th[:, i % 2, :], xc[:, i, :], ACT.Tanh).then_inc(S("th_ready"), 1)
                act.wait_ge(S("wdiff"), g + 1)
                act.activation(wexp, wexp, ACT.Exp).then_inc(S("wexp_ready"), 1)
                if prev:
                    root_norm(act, g, 256)
                if more:
                    tile_in(g + 1, 0)
                    tile_in(g + 1, 1)
                else:
                    gate_ahead(0)
                    gate_ahead(1)
                if prev:
                    copy_norm(act, g, rbg)
                act.wait_ge(S("turned"), g + 1)
                act.activation(Bt, ps[:, 5, :].rearrange("p (c n) -> p c n", n=P), ACT.Copy).then_inc(S("Bt_ready"), 1)
                if more:
                    tile_in(g + 1, 2)
                    tile_in(g + 1, 3)
                else:
                    gate_ahead(2)
                    gate_ahead(3)
                chunk(g, 0)
                chunk(g, 1)
                if more:
                    tile_in(g + 1, 4)
                else:
                    gate_ahead(4)
                chunk(g, 2)
                chunk(g, 3)
                if more:
                    tile_in(g + 1, 5)
                squares(g)
                if not more:
                    gate_ahead(5)

            act.wait_ge(S("o_read"), OPEN + NH)
            for i in range(6):
                tile_in(0, i)
            group(0, False, True)
            with act.Fori(1, NG - 1) as g:
                group(g, True, True)
            group(NG - 1, True, False)
            root_norm(act, NG, 256)
            copy_norm(act, NG, rbg)
            act.wait_ge(S("aux_done"), NG + 1)
            act.wait_ge(S("sout_out"), 16 * NG - 16 + OPEN)
            act.activation(sout, ps[:, 4, P:3 * P].rearrange("p (j n) -> p j n", n=P), ACT.Copy).then_inc(S("sout_ready"), 1)

            def gate_tile(n, j, free):
                act.wait_ge(S("dense_done"), n + 1)
                if free:
                    act.wait_ge(S("mixed"), free)
                act.activation(two(gate[:, j, :]), tile_out(j), ACT.Tanh, scale=0.5).then_inc(S("dense_read"), 1)

            def sbr(it, j):
                act.wait_ge(S("dense_done"), SBR_TILES[it] + 1 + j)
                if it:
                    act.wait_ge(S("mixed"), 2 * it)
                act.activation(two(mix[:, 2 * it + j, :]), tile_out(j), ACT.Copy, scale=0.5).then_inc(S("dense_read"), 1)

            act.wait_ge(S("ssm_ready"), 2 * NG)
            act.wait_ge(S("dtop_kept"), 4 * NG + OPEN)
            sbr(0, 0)
            sbr(0, 1)
            act.wait_ge(S("tensor_mark"), POS_TURNED)
            act.activation(pos, ps[:, 4, 0:16], ACT.Copy).then_inc(S("decode_read"), 1)
            sbr(1, 0)
            sbr(1, 1)
            sbr(2, 0)
            for b in range(NB):
                act.wait_ge(S("keys_turned"), b + 1)
                if b >= 2:
                    act.wait_ge(S("dlogits_done"), b - 1)
                act.activation(KTd[:, b % 2, :], ps[:, 4 + b % 2, :], ACT.Copy).then_inc(S("KT_ready"), 1)
            sbr(2, 1)
            act.wait_ge(S("tensor_mark"), LK_TURNED)
            act.activation(lrow[0:64, :], ps[0:64, 7, 0:TOPK + 1], ACT.Copy).then_inc(S("decode_read"), 1)
            act.wait_ge(S("vector_mark"), DMAX_READY)
            act.activation(lrow[0:64, :], lrow[0:64, :], ACT.Exp, scale=SCALE, bias=dmax,
                           accum_out=dsum).then_inc(S("decode_read"), 1)
            for j in range(2):
                gate_tile(N_SBR + 12 + j, j, 5 + j)
            sbr(3, 0)
            sbr(3, 1)
            act.wait_ge(S("tensor_mark"), DP_TURNED)
            act.activation(pTd.rearrange("p o b h -> p (o b h)"), ps[:, 4, 0:128], ACT.Copy).then_inc(S("decode_read"), 1)
            for it in range(4):
                for j in range(2):
                    gate_tile(N_ATT + 4 * it + j, j, 8 + 2 * it + j - 1)
                for j in range(2):
                    act.wait_ge(S("dense_done"), N_ATT + 4 * it + 3 + j)
                    if it:
                        act.wait_ge(S("mixed"), 8 + 2 * it + j - 1)
                    act.activation(two(stage[:, j, :]), tile_out(j), ACT.Copy, scale=0.5).then_inc(S("dense_read"), 1)
            def residual(n0, before, i):
                for n in range(8):
                    act.wait_ge(S("dense_done"), n0 + n + 1)
                    if n >= 2:
                        act.wait_ge(S("res_added"), before + n - 1)
                    else:
                        act.wait_ge(S("mixed"), 16)
                        if before:
                            act.wait_ge(S("hid_ready"), 2 * OPEN + FT)
                    act.activation(two(stage[:, n % 2, :]), tile_out(n % 2), ACT.Copy).then_inc(S("dense_read"), 1)
                    if n:
                        square(act, i, n - 1, before)
                square(act, i, KT - 1, before)

            residual(N_OUT, 0, 1)
            root_norm(act, NORM2, D)
            copy_norm(act, NORM2, rbc)

            def ffn(k, o):
                for j in range(2):
                    act.wait_ge(S("dense_done"), 8 * k + N_FFN + 4 * o + j + 1)
                    act.wait_ge(S("hid_ready"), 2 * OPEN + 4 * k + 2 * o + j - 1)
                    act.activation(two(gate[:, j, :]), tile_out(j), ACT.Tanh, scale=0.5).then_inc(S("gate_read"), 1)
                    act.activation(hid[:, bass.ds(4 * k + 2 * o + j, 1), :].rearrange("p o (h t) -> p (o h) t", h=2),
                                   tile_out(j), ACT.Copy, scale=0.5).then_inc(S("dense_read"), 1)
                for j in range(2):
                    act.wait_ge(S("dense_done"), 8 * k + N_FFN + 4 * o + j + 3)
                    act.activation(two(stage[:, j, :]), tile_out(j), ACT.Copy).then_inc(S("dense_read"), 1)

            with act.Fori(0, 5) as k:
                ffn(k, 0)
                ffn(k, 1)
            ffn(5, 0)
            residual(N_DOWN, KT, 2)
            root_norm(act, NORMF, D)
            copy_norm(act, NORMF, rbc)
            for b in range(5):
                n = P if b < 4 else NB
                dst = ytok[:, b, :] if b < 4 else ystok[0:NB, :]
                act.wait_ge(S("y_turned"), b + 1)
                for h in range(2):
                    act.activation(dst[:, h * 512:(h + 1) * 512], ps[0:n, 2 * (b % 2) + h, :], ACT.Copy).then_inc(S("y_ready"), 1)

        @block.vector
        def _(v):
            v.sem_inc(S("idx_added"), HEAD)
            for name in ("drs_done", "dsc_ready", "top_cut", "logits_read", "dtop_cut", "dtop_kept"):
                v.sem_inc(S(name), OPEN)
            v.sem_inc(S("hid_ready"), 2 * OPEN)
            v.memset(eps[:], EPS).then_inc(S("vector_mark"), 1)
            v.memset(IQ, 0.0).then_inc(S("vector_mark"), 1)
            for b in range(5):
                v.wait_ge(S("norm_squared"), b + 1)
                dst, src = (sqsum[:, b * P:(b + 1) * P], sqx[b % 2]) if b < 4 else (sqsum[:, SEQ:T], sqxs)
                v.tensor_reduce(dst, src.rearrange("p k t -> p t k"), AX.X, ALU.add).then_inc(S("squares_added"), 1)
            v.wait_ge(S("vec_ready"), 1)
            rms_dve(v, 0, 0, 0)
            v.wait_ge(S("pages_in"), 16)
            v.tensor_copy(pgf[0:NB, 0:NPG], idxT[0:NB, 0:NPG]).then_inc(S("vector_mark"), 1)
            v.wait_ge(S("dense_read"), 2)
            chain = Chain(v, S("dt_steps"))
            chain(v.tensor_scalar(dtT, small[0:32, :], hvec[0:32, 0:1], None, ALU.add))
            v.scalar_tensor_tensor(spa[0:32, :], dtT, -1.0, dtT, ALU.mult, ALU.max).then_inc(S("vector_mark"), 1)
            v.wait_ge(S("dt_exp"), 1)
            chain(v.tensor_scalar(spz[0:32, :], spe[0:32, :], 2.0, None, ALU.add))
            chain(v.reciprocal(spz[0:32, :], spz[0:32, :]))
            chain(v.tensor_tensor(spz[0:32, :], spz[0:32, :], spe[0:32, :], ALU.mult))
            chain(v.tensor_tensor(spw[0:32, :], spz[0:32, :], spz[0:32, :], ALU.mult))
            chain(v.tensor_scalar(spe[0:32, :], spw[0:32, :], 1.0 / 17, None, ALU.mult))
            for i in (15, 13, 11, 9, 7, 5, 3):
                chain(v.scalar_tensor_tensor(spe[0:32, :], spe[0:32, :], 1.0 / i, spw[0:32, :], ALU.add, ALU.mult))
            chain(v.scalar_tensor_tensor(spe[0:32, :], spe[0:32, :], 1.0, spz[0:32, :], ALU.add, ALU.mult))
            chain(v.tensor_scalar(dtT, dtT, 0.0, None, ALU.max))
            chain(v.scalar_tensor_tensor(dtT, spe[0:32, :], 2.0, dtT, ALU.mult, ALU.add))
            v.wait_ge(S("tensor_mark"), IK_MEAN)
            v.tensor_tensor(two(ikt1), two(ik2), ps[:, 4:6, 0:TH], ALU.subtract).then_inc(S("vector_mark"), 1)
            v.wait_ge(S("tensor_mark"), PAGES_TURNED)
            v.tensor_copy(pgf[0:NPG, NPG:NPG + NB], ps[0:NPG, 6, 0:NB]).then_inc(S("vector_mark"), 1)
            v.wait_ge(S("a_exp"), 1)
            chain(v.tensor_scalar(acT[0:32, :], dtT, hvec[0:32, 2:3], -1.0, ALU.mult, ALU.mult))
            for c in range(4):
                v.tensor_tensor_scan(acT[0:32, c * P:(c + 1) * P], ones[0:32, :], acT[0:32, c * P:(c + 1) * P],
                                     0.0, ALU.mult, ALU.add).then_inc(S("a_summed"), 1)
            v.wait_ge(S("tensor_mark"), PAGES_SPREAD)
            v.scalar_tensor_tensor(gidx[:], ps[:, 6, 16:32], 16.0, cst[:, K_P16:K_P16 + 1].broadcast_to((P, 16)),
                                   ALU.mult, ALU.add).then_inc(S("vector_mark"), 1)
            v.wait_ge(S("ik_root"), 1)
            chain(v.reciprocal(ikt2, ikt2))
            chain(v.scalar_tensor_tensor(ikt1, ikt1, ilv[:, 0:1], ikt2, ALU.mult, ALU.mult))
            v.tensor_scalar(ik2, ikt1, ilv[:, 1:2], None, ALU.add).then_inc(S("vector_mark"), 1)
            v.wait_ge(S("iqs_swapped"), 32)
            v.wait_ge(S("vector_mark"), IQ_ZERO)
            for r, h, src in ((0, 0, iqs), (0, 1, iqsw), (1, 0, iqsw), (1, 1, iqs)):
                lo, hi = 64 * r, 64 * r + 64
                v.tensor_copy(IQ[lo:hi, :, 16 * r:16 * r + 16].rearrange("p b (j s) -> p b j s", s=2)[:, :, :, h],
                              src[lo:hi].rearrange("p j b -> p b j")).then_inc(S("IQ_ready"), 1)
            v.scalar_tensor_tensor(wdiag[32:48], small[32:48, SEQ:T].unsqueeze(2).broadcast_to((16, NB, IH)), 1.0 / 32,
                                   ident[32:48, 32:48].unsqueeze(1).broadcast_to((16, NB, IH)),
                                   ALU.mult, ALU.mult).then_inc(S("wdiag_ready"), 1)
            v.wait_ge(S("vector_mark"), IK_READY)
            v.tensor_tensor(iqp, iqs, ik2[:, SEQ:T].unsqueeze(1).broadcast_to((P, 8, NB)),
                            ALU.mult).then_inc(S("wdiag_ready"), 1)
            v.memset(sc, 0.0).then_inc(S("vector_mark"), 1)
            v.wait_ge(S("tok_copied"), 3)
            v.wait_ge(S("vector_mark"), IDX_ZERO)
            with v.Fori(0, 4) as k:
                for j in range(2):
                    for h in range(2):
                        for b in (1, 2, 3):
                            v.wait_ge(S("relu_done"), HEAD + 12 * k + 6 * j + 3 * h + b)
                            v.wait_ge(S("idx_added"), HEAD + 12 * k + 6 * j + 3 * h)
                            acc = sc[:, X0[b]:X0[b] + EXT[b]]
                            v.scalar_tensor_tensor(acc, rl[:, h, X0[b]:X0[b] + EXT[b]],
                                                   tok[:, b, bass.ds(4 * k + 32 + 2 * j + h, 1)], acc,
                                                   ALU.mult, ALU.add).then_inc(S("idx_added"), 1)
            v.wait_ge(S("idx_added"), HEAD + 48)
            for b in (1, 2, 3):
                d = sc[:, X0[b] + b * P:X0[b] + (b + 1) * P]
                v.scalar_tensor_tensor(d, cbias, -LOW / -MASK, d, ALU.mult, ALU.add).then_inc(S("sc_ready"), 1)
            v.wait_ge(S("sc_ready"), 3)
            v.tensor_copy(wk, sc).then_inc(S("vector_mark"), 1)
            v.wait_ge(S("wbc_ready"), 2)
            chain(v.tensor_tensor(drelu[0:NB, :], drelu[0:NB, :], tok[0:NB, 4, 32:48], ALU.mult))
            chain(v.tensor_reduce(smp[0:NB, PAST:PAST + 1], drelu[0:NB, :], AX.X, ALU.add))
            v.wait_ge(S("vector_mark"), WK_READY)
            def decode_sums(k):
                for o in range(2):
                    v.wait_ge(S("dec_done"), OPEN + 2 * k + o + 1)
                    v.wait_ge(S("dsc_ready"), OPEN + 2 * k + o)
                    v.scalar_tensor_tensor(drs.rearrange("p (a h) -> p a h", h=IH),
                                           ps[:, 6 + o, 0:P].rearrange("p (a h) -> p a h", h=IH), 0.0,
                                           wbc[:, bass.ds(k, 1), :].broadcast_to((P, 8, IH)),
                                           ALU.max, ALU.mult).then_inc(S("drs_done"), 1)
                    v.wait_ge(S("drs_done"), OPEN + 2 * k + o + 1)
                    v.tensor_reduce(dsc[:, bass.ds(16 * k + 8 * o, 8)], drs.rearrange("p (a h) -> p a h", h=IH),
                                    AX.X, ALU.add).then_inc(S("dsc_ready"), 1)

            def prompt_round(r):
                for b in (1, 2, 3):
                    v.wait_ge(S("top_cut"), OPEN + 3 * r)
                    v.sem_inc(S("pad"), 1)
                    v.max(m8[:, b - 1, :], wk[:, X0[b]:X0[b] + EXT[b]]).then_inc(S("top_max"), 1)
                for b in (1, 2, 3):
                    v.wait_ge(S("top_max"), 3 * r + b)
                    v.sem_inc(S("pad"), 1)
                    w_ = wk[:, X0[b]:X0[b] + EXT[b]]
                    v.match_replace(w_, m8[:, b - 1, :], w_, -3.3e38).then_inc(S("top_cut"), 1)

            with v.Fori(0, 4) as k:
                decode_sums(k)
                for r in range(3):
                    prompt_round(3 * k + r)
            with v.Fori(4, NB) as k:
                decode_sums(k)
                prompt_round(k + 8)
            v.wait_ge(S("top_cut"), OPEN + 3 * TOPK_P // 8)
            chain(v.tensor_tensor(sc, sc, wk, ALU.not_equal))
            v.tensor_scalar(sc, sc, -MASK, MASK, ALU.mult, ALU.add).then_inc(S("vector_mark"), 1)
            v.wait_ge(S("vector_mark"), MASK_READY)
            with v.Fori(0, NH) as i:
                for b in range(4):
                    if b == 0:
                        v.wait_ge(S("p_turned"), OPEN + 4 * i)
                    v.wait_ge(S("logits_done"), OPEN + 4 * i + b + 1)
                    v.sem_inc(S("pad"), 1)
                    mask = cbias if b == 0 else sc[:, X0[b]:X0[b] + EXT[b]]
                    v.tensor_tensor_reduce(lg[:, AT[b]:AT[b] + EXT[b]], ps[:, b, 0:EXT[b]], mask, 1.0, LOW,
                                           ALU.add, ALU.max, amx[:, b:b + 1]).then_inc(S("logits_read"), 1)
                    v.wait_ge(S("logits_read"), OPEN + 4 * i + b + 1)
                    v.tensor_scalar(anm[:, b:b + 1], amx[:, b:b + 1], -SCALE, None, ALU.mult).then_inc(S("neg_max"), 1)
                for b in range(4):
                    v.wait_ge(S("exp_done"), 4 * i + b + 1)
                    v.reciprocal(asum[:, b:b + 1], asum[:, b:b + 1]).then_inc(S("sum_recip"), 1)
                    v.wait_ge(S("sum_recip"), 4 * i + b + 1)
                    l = lg[:, AT[b]:AT[b] + EXT[b]]
                    v.tensor_scalar(l, l, asum[:, b:b + 1], None, ALU.mult).then_inc(S("p_ready"), 1)


            v.wait_ge(S("o_done"), OPEN + NH)
            v.memset(raw[:, :, 0:3], 0.0).then_inc(S("vector_mark"), 1)
            v.wait_ge(S("vector_mark"), RAW_ZERO)
            v.wait_ge(S("cwg_ready"), 12)

            def top(g, *pieces):
                best, row = dm8[0:NB, :], smp[0:NB, :]
                for piece in pieces:
                    r = piece // 3
                    if piece % 3 == 0:
                        v.wait_ge(S("dtop_cut"), 4 * g + r + OPEN)
                        v.sem_inc(S("pad"), 1)
                        v.max(best, row).then_inc(S("dtop_max"), 1)
                    elif piece % 3 == 1:
                        v.wait_ge(S("dtop_max"), 4 * g + r + 1)
                        v.wait_ge(S("dtop_kept"), 4 * g + r + OPEN)
                        v.sem_inc(S("pad"), 1)
                        v.max_index(dix[:], best, row).then_inc(S("dtop_index"), 1)
                    else:
                        v.match_replace(row, best, row, -3.3e38).then_inc(S("dtop_cut"), 1)
                        v.wait_ge(S("dtop_index"), 4 * g + r + 1)
                        v.tensor_copy(sel_idx[0:NB, bass.ds(32 * g + 8 * r, 8)], dix[:]).then_inc(S("dtop_kept"), 1)

            def z_gate(g):
                for j in range(2):
                    v.wait_ge(S("thz_ready"), 2 * g + j + 1)
                    v.wait_ge(S("dense_read"), 6 * g + N_SSM + 5 + j)
                    z = ssm_o[:, bass.ds(2 * g + j, 1), :].rearrange("p o t -> p (o t)")
                    v.scalar_tensor_tensor(z, thz[:, j, :], 1.0, z, ALU.add, ALU.mult).then_inc(S("z_ready"), 1)

            def norm(g):
                v.wait_ge(S("norm_copied"), 2 * g + 4)
                for j in range(2):
                    v.scalar_tensor_tensor(ssm_o[:, bass.ds(2 * g + j, 1), :].rearrange("p o t -> p (o t)"), Y[:, j, :],
                                           cwg[:, bass.ds(g, 1), 22 + j:23 + j].rearrange("p o t -> p (o t)"), rbg,
                                           ALU.mult, ALU.mult).then_inc(S("ssm_ready"), 1)

            def group(g, prev, more):
                if prev:
                    v.wait_ge(S("abc_read"), 4 * g)
                    v.wait_ge(S("Y_ready"), 2 * g)
                v.tensor_copy(cw, cwg[:, bass.ds(g, 1), :].rearrange("p o t -> p (o t)")).then_inc(S("cw_ready"), 1)
                v.tensor_copy(dtg, tok[:, 0:4, bass.ds(4 * g, 4)]).then_inc(S("cw_ready"), 1)
                v.tensor_copy(atg, actok[:, :, bass.ds(4 * g, 4)]).then_inc(S("cw_ready"), 1)
                v.wait_ge(S("cw_ready"), 3 * g + 3)
                for pair in range(2):
                    for t in range(1, 4):
                        for i in (2 * pair, 2 * pair + 1):
                            v.wait_ge(S("tap%d" % (t - 1)), 4 * g + i + 1)
                            v.scalar_tensor_tensor(xc[:, i, 0:SEQ], raw[:, i, t:t + SEQ], cw[:, 5 * i + t:5 * i + t + 1],
                                                   xc[:, i, 0:SEQ], ALU.mult,
                                                   ALU.add).then_inc(S("tap%d" % t if t < 3 else "conv_done"), 1)
                v.wait_ge(S("alast"), 2 * g + 2)
                v.tensor_tensor(wexp, alast.rearrange("p r c -> p c r"), atg, ALU.subtract).then_inc(S("wdiff"), 1)
                for i in range(4):
                    v.wait_ge(S("th_ready"), 4 * g + i + 1)
                    v.scalar_tensor_tensor(xc[:, i, :], th[:, i % 2, :], 1.0, xc[:, i, :], ALU.add,
                                           ALU.mult).then_inc(S("silu_done"), 1)
                if prev:
                    recip_norm(v, g)
                    top(g, 0)
                    norm(g - 1)
                else:
                    top(g, 0)
                v.wait_ge(S("turned"), g + 1)
                for c in range(2):
                    v.tensor_tensor(xdt[:, 2 * c:2 * c + 2, :].rearrange("p c (r q) -> p c r q", q=64),
                                    ps[:, 6 + c, :].rearrange("p (c r q) -> p c r q", r=4, q=64),
                                    dtg[:, 2 * c:2 * c + 2, :].unsqueeze(3).broadcast_to((P, 2, 4, 64)),
                                    ALU.mult).then_inc(S("xdt_ready"), 1)
                v.wait_ge(S("wexp_ready"), g + 1)
                v.wait_ge(S("xdt_ready"), 2 * g + 2)
                v.tensor_tensor(xw.rearrange("p c (r q) -> p (c r) q", q=64), xdt.rearrange("p c (r q) -> p (c r) q", q=64),
                                wexp.rearrange("p c r -> p (c r)").unsqueeze(2).broadcast_to((P, 16, 64)),
                                ALU.mult).then_inc(S("xw_ready"), 1)
                top(g, 1, 2)
                v.wait_ge(S("silu_done"), 4 * g + 4)
                v.wait_ge(S("dts_ready"), g + 1)
                v.tensor_tensor(xdts, xc[:, 0:2, SEQ:T], dts, ALU.mult).then_inc(S("xdts_ready"), 1)
                v.wait_ge(S("xdts_ready"), g + 1)
                v.wait_ge(S("bcast_done"), 2 * g + 1)
                for j in range(2):
                    if j:
                        v.wait_ge(S("state_new"), 2 * g + 1)
                    v.tensor_tensor(t2, ps[:, 6:8, :].rearrange("p k (b n) -> p (k b) n", n=NS),
                                    xdts[:, j, :].unsqueeze(2).broadcast_to((P, NB, NS)),
                                    ALU.mult).then_inc(S("B_used"), 1)
                    v.wait_ge(S("B_used"), 2 * g + j + 1)
                    v.wait_ge(S("st_decayed"), 2 * g + j + 1)
                    v.tensor_tensor(st[:, j], st[:, j], t2, ALU.add).then_inc(S("state_new"), 1)
                v.wait_ge(S("bcast_done"), 2 * g + 2)
                for j in range(2):
                    v.wait_ge(S("state_new"), 2 * g + 2)
                    if j:
                        v.wait_ge(S("ys_ready"), 2 * g + 1)
                    v.tensor_tensor(t2, ps[:, 4:6, :].rearrange("p k (b n) -> p (k b) n", n=NS), st[:, j],
                                    ALU.mult).then_inc(S("C_used"), 1)
                    v.wait_ge(S("C_used"), 2 * g + j + 1)
                    v.tensor_reduce(ys[:, j, :], t2, AX.X, ALU.add).then_inc(S("ys_ready"), 1)
                v.wait_ge(S("cb_done"), g + 1)
                v.tensor_tensor(CBm, ps[:, 5, :].rearrange("p (c l) -> p c l", l=P),
                                tri.unsqueeze(1).broadcast_to((P, 4, P)), ALU.mult).then_inc(S("CBm_ready"), 1)
                top(g, 3, 4, 5, 6, 7, 8)
                for c in range(4):
                    if c == 3 and more:
                        z_gate(g + 1)
                    v.wait_ge(S("y_done"), 4 * g + c + 1)
                    inc = ps[:, 5, 256 * (c % 2):256 * (c % 2) + 256]
                    if c == 0:
                        v.tensor_copy(hT, inc).then_inc(S("h_done"), 1)
                    else:
                        v.tensor_tensor(hT.rearrange("p (r q) -> p r q", q=64), hT.rearrange("p (r q) -> p r q", q=64),
                                        ealast[:, :, c:c + 1].broadcast_to((P, 4, 64)), ALU.mult).then_inc(S("h_decayed"), 1)
                        v.wait_ge(S("h_decayed"), 3 * g + c)
                        v.tensor_tensor(hT, hT, inc, ALU.add).then_inc(S("h_done"), 1)
                    if c == 0:
                        top(g, 9, 10)
                    if c == 1:
                        top(g, 11)
                for j in range(2):
                    v.scalar_tensor_tensor(Y[:, j, 0:SEQ], xc[:, j, 0:SEQ], cw[:, 20 + j:21 + j], ps[:, 6 + j, :],
                                           ALU.mult, ALU.add).then_inc(S("Y_sum"), 1)
                    v.wait_ge(S("ys_ready"), 2 * g + j + 1)
                    v.scalar_tensor_tensor(Y[:, j, SEQ:T], xc[:, j, SEQ:T], cw[:, 20 + j:21 + j], ys[:, j, :],
                                           ALU.mult, ALU.add).then_inc(S("Y_sum"), 1)
                for j in range(2):
                    v.wait_ge(S("Y_sum"), 4 * g + 2 * j + 2)
                    v.wait_ge(S("z_ready"), 2 * g + j + 1)
                    v.tensor_tensor(Y[:, j, :], Y[:, j, :], ssm_o[:, bass.ds(2 * g + j, 1), :].rearrange("p o t -> p (o t)"),
                                    ALU.mult).then_inc(S("Y_ready"), 1)

            z_gate(0)
            group(0, False, True)
            with v.Fori(1, NG - 1) as g:
                group(g, True, True)
            group(NG - 1, True, False)
            recip_norm(v, NG)
            norm(NG - 1)

            def gated(it, *js):
                for j in js or (0, 1):
                    v.wait_ge(S("dense_read"), SBR_TILES[it] + 1 + j)
                    m = mix[:, 2 * it + j, :]
                    gt = gates_ahead[2 * it + j] if it < 3 else gate[:, j, :]
                    v.scalar_tensor_tensor(m, gt, 1.0, m, ALU.add, ALU.mult).then_inc(S("mixed"), 1)

            
            v.wait_ge(S("pgb_in"), 16)
            v.wait_ge(S("dtop_kept"), 4 * NG + OPEN)
            chain(v.tensor_scalar(pgb.rearrange("p b j -> p (b j)"), pgb32[:], float(PAGE), None, ALU.mult))
            v.tensor_copy(dpg[:, :, 0:1], pgb[:, :, 0:1]).then_inc(S("dpg_ready"), 1)
            v.scalar_tensor_tensor(dpg[:, :, 1:NPG], pgb[:, :, 1:NPG], -float(PAGE), pgb[:, :, 0:NPG - 1], ALU.add,
                                   ALU.subtract).then_inc(S("dpg_ready"), 1)
            v.wait_ge(S("aux_done"), NG + 1)
            v.tensor_tensor(qk_new.rearrange("p b (g h) -> p g h b", g=2),
                            qkvs[:, 0:8, :].rearrange("p (g h) b -> p g h b", g=2),
                            qkvs[:, 8:10, :].unsqueeze(2).broadcast_to((P, 2, 4, NB)), ALU.mult).then_inc(S("vector_mark"), 1)
            gated(0)
            v.wait_ge(S("decode_read"), POS_READ)
            v.wait_ge(S("dpg_ready"), 2)
            chain(v.tensor_scalar(posc, pos, float(PAST - 1), None, ALU.min))
            v.tensor_scalar(gone, pos, PAST - 0.5, MASK, ALU.is_gt, ALU.mult).then_inc(S("gone_ready"), 1)
            chain(v.tensor_tensor(hit, posc.unsqueeze(2).broadcast_to((P, 16, 16)),
                                  cst[:, K_J:K_J + NPG].unsqueeze(1).broadcast_to((P, 16, 16)), ALU.is_ge))
            hit4 = hit.rearrange("p (o b) j -> p o b j", o=2)
            chain(v.tensor_tensor(hit4, hit4, dpg.unsqueeze(1).broadcast_to((P, 2, NB, NPG)), ALU.mult))
            chain(v.tensor_reduce(pos, hit, AX.X, ALU.add))
            v.tensor_tensor(gidx[:], pos, posc, ALU.add).then_inc(S("vector_mark"), 1)
            gated(1)
            gated(2, 0)
            v.wait_ge(S("dlogits_done"), NB)
            v.wait_ge(S("gone_ready"), 1)
            v.tensor_tensor(lk.rearrange("p o b h -> p (o b) h"), ps[:, 6, 0:128].rearrange("p (a h) -> p a h", h=NH),
                            gone.unsqueeze(2).broadcast_to((P, 16, NH)), ALU.add).then_inc(S("vector_mark"), 1)
            gated(2, 1)
            v.wait_ge(S("decode_read"), LROW_READY)
            chain(v.tensor_reduce(dmin, lrow[0:64, 0:TOPK], AX.X, ALU.min))
            chain(v.tensor_scalar(dmin, dmin, MASK / 2, MASK, ALU.is_gt, ALU.mult))
            chain(v.tensor_tensor(lrow[0:64, TOPK:TOPK + 1], lrow[0:64, TOPK:TOPK + 1], dmin, ALU.add))
            chain(v.tensor_reduce(dmax, lrow[0:64, :], AX.X, ALU.max))
            v.tensor_scalar(dmax, dmax, -SCALE, None, ALU.mult).then_inc(S("vector_mark"), 1)
            v.wait_ge(S("decode_read"), DEXP_DONE)
            chain(v.reciprocal(dsum, dsum))
            v.tensor_scalar(lrow[0:64, :], lrow[0:64, :], dsum, None, ALU.mult).then_inc(S("vector_mark"), 1)
            gated(3)
            v.wait_ge(S("tensor_mark"), DP_TURNED)
            v.wait_ge(S("decode_read"), PTD_READY)
            chain(v.tensor_tensor(pv_new.rearrange("p b (g h) -> p g h b", g=2),
                                  ps[:, 4, 128:192].rearrange("p (b g h) -> p g h b", g=2, h=4),
                                  qkvs[:, 10:12, :].unsqueeze(2).broadcast_to((P, 2, 4, NB)), ALU.mult))
            v.wait_ge(S("tensor_mark"), DVALUES_DONE)
            v.tensor_tensor(uT[:, :, SEQ:T].rearrange("p h b -> p b h"), ps[:, 5, 0:64].rearrange("p (b h) -> p b h", h=NH),
                            pv_new, ALU.add).then_inc(S("vector_mark"), 1)
            for it in range(4):
                for j in range(2):
                    v.wait_ge(S("dense_read"), N_ATT + 4 * it + 3 + j)
                    v.scalar_tensor_tensor(stage[:, j, :], gate[:, j, :], 1.0, stage[:, j, :], ALU.add,
                                           ALU.mult).then_inc(S("att_gated"), 1)
                    v.wait_ge(S("att_gated"), 2 * it + j + 1)
                    m = mix[:, 2 * it + j, :]
                    v.tensor_tensor(m, m, stage[:, j, :], ALU.add).then_inc(S("mixed"), 1)

            def residual(n0, i):
                for n in range(8):
                    v.wait_ge(S("dense_read"), n0 + n + 1)
                    v.tensor_tensor(xT[:, n, :], xT[:, n, :], stage[:, n % 2, :], ALU.add).then_inc(S("res_added"), 1)
                    if n > 1:
                        add_square(v, i, n - 1)
                add_square(v, i, KT - 1)

            residual(N_OUT, 1)
            rms_dve(v, 1, NORM2, 8)

            def ffn(k, o):
                hs = [hid[:, bass.ds(4 * k + 2 * o + j, 1), :].rearrange("p o t -> p (o t)") for j in range(2)]
                for j in range(2):
                    v.wait_ge(S("dense_read"), 8 * k + N_FFN + 4 * o + j + 1)
                    v.wait_ge(S("gate_read"), 4 * k + 2 * o + j + 1)
                    v.scalar_tensor_tensor(hs[j], gate[:, j, :], 1.0, hs[j], ALU.add, ALU.mult).then_inc(S("silu_h"), 1)
                for j in range(2):
                    v.wait_ge(S("silu_h"), 4 * k + 2 * o + j + 1)
                    v.wait_ge(S("dense_read"), 8 * k + N_FFN + 4 * o + j + 3)
                    v.tensor_tensor(hs[j], hs[j], stage[:, j, :], ALU.mult).then_inc(S("hid_ready"), 1)

            with v.Fori(0, 5) as k:
                ffn(k, 0)
                ffn(k, 1)
            ffn(5, 0)
            residual(N_DOWN, 2)
            rms_dve(v, 2, NORMF, 16)

        @block.gpsimd
        def _(g):
            g.wait_ge(S("vec_ready"), 1)
            g.wait_ge(S("taps_ready"), 1)
            g.wait_ge(S("dsk_ready"), 1)
            tp = taps.rearrange("p (t n) -> p n t", t=4)
            cb = vec[:, 40:72]
            for i, sl in enumerate((slice(0, 16, 2), slice(1, 16, 2), slice(16, 24), slice(24, 32))):
                g.tensor_copy(cwg[:, :, 5 * i:5 * i + 4], tp[:, sl, :]).then_inc(S("cwg_ready"), 1)
                g.tensor_scalar(cwg[:, :, 5 * i + 4], cb[:, sl], 0.5, None, ALU.mult).then_inc(S("cwg_ready"), 1)
            for j in range(2):
                g.tensor_copy(cwg[:, :, 20 + j], dsk[:, j:16:2]).then_inc(S("cwg_ready"), 1)
                g.tensor_copy(cwg[:, :, 22 + j], vec[:, 24 + j:40:2]).then_inc(S("cwg_ready"), 1)

            g.wait_ge(S("vector_mark"), GIDX_READY)
            rows = cache_idx_k[0].rearrange("n (s k) d -> (n s) (k d)", k=8)

            def gather(b, o):
                g.indirect_dma_start(gat[:, o, :], None, rows,
                                     bass.IndirectOffsetOnAxis(gidx[:, o * NB + b:o * NB + b + 1], 0)
                                     ).then_inc(S("gathered%d" % o), 16)

            gather(0, 0)
            gather(0, 1)
            g.wait_ge(S("dense_read"), N_QKV)
            g.wait_ge(S("vector_mark"), IK_READY)
            with g.Fori(0, 4) as k:
                for j in range(2):
                    g.wait_ge(S("idx_done"), TILE + 12 * k + 6 * j - 6)
                    g.tensor_copy(iqslot[j], kviq[:, bass.ds(2 * k + 4 + j, 1), :].rearrange("p o t -> p (o t)")).then_inc(S("iq_in_slot"), 1)
            for b in range(1, NB):
                for o in range(2):
                    g.wait_ge(S("gat_turned"), 2 * b - 1 + o)
                    gather(b, o)

            with g.Fori(0, NH) as i:
                g.wait_ge(S("logits_done"), OPEN + 4 * i)
                g.wait_ge(S("dense_read"), N_SSM)
                g.tensor_copy(qslot, uT[:, bass.ds(i, 1), :].rearrange("p o t -> p (o t)")).then_inc(S("q_in_slot"), 1)

            def add_squares(i):
                g.wait_ge(S("sqg_ready"), 2 * i + 2)
                g.tensor_tensor(sqg[:, 0, :], sqg[:, 0, :], sqg[:, 1, :], ALU.add).then_inc(S("sqg_added"), 1)

            def group(i, prev):
                if prev:
                    add_squares(i - 1)
                w4 = cw[:, 0:20].rearrange("p (i t) -> p i t", t=5)
                old = sct.rearrange("p i (b t) -> p i b t", t=3)
                g.wait_ge(S("sct_ready"), i + 1)
                g.wait_ge(S("cw_ready"), 3 * i + 3)
                g.wait_ge(S("dense_read"), 6 * i + N_SSM + 4)
                for t, o in enumerate((sc0, sc1, sc2)):
                    g.tensor_tensor(o, old[:, :, :, t], w4[:, :, t:t + 1].broadcast_to((P, 4, NB)),
                                    ALU.mult).then_inc(S("dconv_steps"), 1)
                g.tensor_tensor(sc3, raw[:, :, SEQ + 3:T + 3], w4[:, :, 3:4].broadcast_to((P, 4, NB)),
                                ALU.mult).then_inc(S("dconv_steps"), 1)
                g.wait_ge(S("dconv_steps"), 7 * i + 4)
                g.tensor_tensor(sc0, sc0, sc1, ALU.add).then_inc(S("dconv_steps"), 1)
                g.tensor_tensor(sc2, sc2, sc3, ALU.add).then_inc(S("dconv_steps"), 1)
                g.wait_ge(S("dconv_steps"), 7 * i + 6)
                g.tensor_tensor(sc0, sc0, sc2, ALU.add).then_inc(S("dconv_steps"), 1)
                g.wait_ge(S("dconv_steps"), 7 * i + 7)
                g.tensor_tensor(xc[:, :, SEQ:T], sc0, w4[:, :, 4:5].broadcast_to((P, 4, NB)), ALU.add).then_inc(S("dconv_done"), 1)
                g.wait_ge(S("aux_read"), i + 1)
                g.wait_ge(S("state_in"), 32 * i + 32)
                for j in range(2):
                    g.tensor_tensor(st[:, j], st[:, j], dAs[:, j, :].unsqueeze(2).broadcast_to((P, NB, NS)),
                                    ALU.mult).then_inc(S("st_decayed"), 1)
                for c in range(4):
                    g.wait_ge(S("CBm_ready"), i + 1)
                    g.wait_ge(S("E_ready"), 4 * i + c + 1)
                    m = M2[:, c % 2, :].rearrange("p (r l) -> p r l", l=P)
                    g.tensor_tensor(m, m, CBm[:, c:c + 1, :].broadcast_to((P, 4, P)), ALU.mult).then_inc(S("M_ready"), 1)
                    if c:
                        x = Cx2[:, c % 2, :].rearrange("p (r l) -> p r l", l=P)
                        g.tensor_tensor(x, x, xc[:, 3:4, c * P:(c + 1) * P].broadcast_to((P, 4, P)),
                                        ALU.mult).then_inc(S("M_ready"), 1)

            group(0, False)
            with g.Fori(1, NG) as i:
                group(i, True)
            add_squares(NG - 1)
            g.wait_ge(S("vector_mark"), ROWS_READY)
            g.wait_ge(S("ssm_ready"), 2 * NG)
            g.wait_ge(S("state_out"), 32 * NG)
            rows_k = cache_k[0].rearrange("n s g d -> (n s) (g d)")
            rows_v = cache_v[0].rearrange("n s g d -> (n s) (g d)")
            for kind, rows in enumerate((rows_k, rows_v)):
                if kind:
                    g.wait_ge(S("mixed"), 4)
                for b in range(NB):
                    for o in range(2):
                        c = NB * o + b
                        g.indirect_dma_start(KV[:, kind, c, :], None, rows,
                                             bass.IndirectOffsetOnAxis(gidx[:, c:c + 1], 0)
                                             ).then_inc(S("values_in" if kind else "keys_in"), 16)


_INS = ["x_prompt", "x_sample", "cache_k", "cache_v", "cache_idx_k", "state_ssm", "state_conv", "page_table",
        "norm1_w", "w_in", "idx_ln_w", "idx_ln_b", "conv_w", "conv_b", "dt_bias", "a_log", "d_skip",
        "ssm_norm_w", "w_attn_br", "w_ssm_br", "w_out", "norm2_w", "w_ffn_gate", "w_ffn_up", "w_ffn_down",
        "normf_w"]
_OUTS = [(1, 512, 1024), (8, 1, 1024), (1, 1, 512, 2, 128), (1, 1, 512, 2, 128), (1, 1, 512, 64),
         (1, 1, 32, 64, 128), (1, 1, 3, 4096), (1, 8, 1, 2, 128), (1, 8, 1, 2, 128), (1, 8, 1, 64),
         (1, 8, 32, 64, 128), (1, 8, 3, 4096)]


def _constants():
    import numpy as np

    p, q = np.arange(P)[:, None], np.arange(P)[None, :]
    c = np.zeros((P, NK), np.float32)
    c[:, K_ID:K_ID + P] = p == q
    c[:, K_ONE:K_ONE + P] = 1.0
    c[:, K_BLK:K_BLK + P] = (p // ID == q // ID) / float(ID)
    c[:, K_TRI:K_TRI + P] = p <= q
    c[:, K_CB:K_CB + P] = np.where(q <= p, 0.0, MASK)
    c[:, K_P16] = np.arange(P) % 16
    for o in range(2):
        c[0:NPG, K_PG + o * P:K_PG + (o + 1) * P] = np.arange(NPG)[:, None] == o * 8 + q // 16
    c[0:2, K_HALF:K_HALF + P] = p[0:2] == q // ID
    c[:, K_PAR] = np.arange(P) < ID
    c[:, K_PAR + 1] = np.arange(P) >= ID
    c[:, K_J:K_J + NPG] = np.arange(NPG) * PAGE
    g = np.zeros((NG, 32, GSEL), np.float32)
    h = np.arange(32)[:, None]
    for i in range(NG):
        for r in range(4):
            g[i, :, r * P:(r + 1) * P] = h == 4 * i + r
        for j in range(2):
            g[i, :, 512 + j * P:512 + (j + 1) * P] = h == 4 * i + 2 * j + q // ID
    return c, g


def kernel(**inputs):
    import concourse.bacc as _bacc
    import numpy as _np
    from concourse.bass_utils import run_bass_kernel_spmd as _run

    nc = _bacc.Bacc("TRN2", target_bir_lowering=False, num_devices=1)
    arrays, args = {}, []
    for name in _INS:
        a = _np.ascontiguousarray(inputs[name])
        arrays[f"in_{name}"] = a
        args.append(nc.dram_tensor(f"in_{name}", a.shape, mybir.dt.from_np(a.dtype), kind="ExternalInput").ap())
    for name, a in zip(("constants", "head_selectors"), _constants()):
        arrays[f"in_{name}"] = a
        args.append(nc.dram_tensor(f"in_{name}", a.shape, F32, kind="ExternalInput").ap())
    for i, shape in enumerate(_OUTS):
        args.append(nc.dram_tensor(f"out_{i}", shape, F32, kind="ExternalOutput").ap())
    build(nc, *args)
    r = _run(nc, [arrays], core_ids=[0])
    return tuple(r.results[0][f"out_{i}"] for i in range(len(_OUTS)))
```
